# Optimizing a Trainium2 kernel written in Bass

```python
import jax, jax.numpy as jnp
from jax import lax
import numpy as np

D_MODEL = 1024
BATCH = 1
SEQ = 512
DEPTH = 2
DEC_BATCH = 8
DEC_SEQ = 1
PAST_LEN = 2048
PAGE_SIZE = 128

MIX_WIDTH = D_MODEL
HEAD_DIM = 64
NSA_WIDTH = MIX_WIDTH // 2
NSA_HEADS = NSA_WIDTH // HEAD_DIM
NSA_KV_HEADS = 2
HEADS_PER_KV = NSA_HEADS // NSA_KV_HEADS
KV_WIDTH = NSA_KV_HEADS * HEAD_DIM
N_BRANCH = 3
CMP_STRIDE = 16
CMP_BLOCK = 2 * CMP_STRIDE
CMP_HIDDEN = HEAD_DIM
SEL_BLOCK = 64
SEL_TOPN = 16
WINDOW = 512
ROPE_THETA = 500000.0
ROPE_DIM = HEAD_DIM // 4
Q_BLOCK = 64
RWKV_WIDTH = MIX_WIDTH - NSA_WIDTH
RWKV_HEAD = 64
RWKV_HEADS = RWKV_WIDTH // RWKV_HEAD
DECAY_LORA = 64
AAA_LORA = 64
GATE_LORA = 128
NSA_PROJ = NSA_WIDTH + 6 * KV_WIDTH + N_BRANCH * NSA_HEADS
RWKV_PROJ = 3 * RWKV_WIDTH + DECAY_LORA + AAA_LORA + GATE_LORA
IN_PROJ = NSA_PROJ + RWKV_PROJ
D_FF = 2816
CONV_WIDTH = 3
NORM_EPS = 1e-6
LNX_EPS = 64e-5
NEG = -1e30
FORCED_SCORE = 1e9

kernel_name = "hybrid_nsa_rwkv7_convffn_step"

def rms_norm(x, g):
    xf = x.astype(jnp.float32)
    y = xf * lax.rsqrt(jnp.mean(xf * xf, axis=-1, keepdims=True) + NORM_EPS)
    return (y * g.astype(jnp.float32)).astype(x.dtype)

def rope(x, pos):
    half = ROPE_DIM // 2
    inv_freq = ROPE_THETA ** (-jnp.arange(half, dtype=jnp.float32) / half)
    ang = pos.astype(jnp.float32)[:, None] * inv_freq[None, :]
    cos = jnp.cos(ang)[None, :, None, :]
    sin = jnp.sin(ang)[None, :, None, :]
    xf = x.astype(jnp.float32)
    x1, x2 = xf[..., :half], xf[..., half:ROPE_DIM]
    out = jnp.concatenate([x1 * cos - x2 * sin, x2 * cos + x1 * sin, xf[..., ROPE_DIM:]], axis=-1)
    return out.astype(x.dtype)

def masked_softmax(s, mask):
    s = jnp.where(mask, s.astype(jnp.float32), NEG)
    m = jnp.max(s, axis=-1, keepdims=True)
    e = jnp.where(mask, jnp.exp(s - m), 0.0)
    return e / jnp.maximum(jnp.sum(e, axis=-1, keepdims=True), 1e-30)

def nsa_project(proj, pos):
    B, T, _ = proj.shape
    q = rope(proj[..., :NSA_WIDTH].reshape(B, T, NSA_HEADS, HEAD_DIM), pos)
    kv = proj[..., NSA_WIDTH:NSA_WIDTH + 6 * KV_WIDTH].reshape(B, T, N_BRANCH, 2, NSA_KV_HEADS, HEAD_DIM)
    k = rope(kv[:, :, :, 0].reshape(B, T, N_BRANCH * NSA_KV_HEADS, HEAD_DIM), pos)
    k = k.reshape(B, T, N_BRANCH, NSA_KV_HEADS, HEAD_DIM)
    kv = jnp.stack([k, kv[:, :, :, 1]], axis=3)
    kv_rows = kv[:, :, :2].reshape(B, T, 4, NSA_KV_HEADS, HEAD_DIM)
    win_rows = kv[:, :, 2]
    gates = jax.nn.sigmoid(proj[..., NSA_WIDTH + 6 * KV_WIDTH:].astype(jnp.float32))
    return q, kv_rows, win_rows, gates.reshape(B, T, NSA_HEADS, N_BRANCH)

def compress(rows, pe, w1, w2):
    B, L = rows.shape[:2]
    n_chunk = L // CMP_STRIDE
    ch = rows[:, :n_chunk * CMP_STRIDE].reshape(B, n_chunk, CMP_STRIDE, NSA_KV_HEADS, HEAD_DIM)
    blocks = jnp.concatenate([ch[:, :-1], ch[:, 1:]], axis=2) + pe[None, None, :, None, :]
    h = jax.nn.gelu(jnp.einsum('bnlgd,lde->bnge', blocks, w1))
    return jnp.einsum('bnge,ef->bgnf', h, w2)

def cmp_to_sel(n_cmp, n_sel):
    c0 = jnp.arange(n_cmp) * CMP_STRIDE
    s0 = jnp.arange(n_sel) * SEL_BLOCK
    hit = (c0[:, None] < s0[None, :] + SEL_BLOCK) & (c0[:, None] + CMP_BLOCK > s0[None, :])
    return hit.astype(jnp.float32)

def cmp_sel_attend(q, qpos, kc, vc, ksb, vsb):
    B, Tq = q.shape[:2]
    scale = HEAD_DIM ** -0.5
    qg = q.reshape(B, Tq, NSA_KV_HEADS, HEADS_PER_KV, HEAD_DIM).transpose(0, 2, 1, 3, 4)
    n_cmp, n_sel = kc.shape[2], ksb.shape[2]
    cmp_end = jnp.arange(n_cmp, dtype=jnp.int32) * CMP_STRIDE + CMP_BLOCK - 1
    cmask = (cmp_end[None, :] <= qpos[:, None])[None, None, :, None, :]
    pc = masked_softmax(jnp.einsum('bgqhd,bgnd->bgqhn', qg, kc) * scale, cmask)
    o_cmp = jnp.einsum('bgqhn,bgnd->bgqhd', pc.astype(vc.dtype), vc)
    imp = jnp.einsum('bgqhn,ns->bgqs', pc, cmp_to_sel(n_cmp, n_sel))
    blk = jnp.arange(n_sel, dtype=jnp.int32)[None, :]
    cur = (qpos // SEL_BLOCK)[:, None]
    forced = (blk == 0) | (blk == cur) | (blk == cur - 1)
    valid = blk * SEL_BLOCK <= qpos[:, None]
    score = jnp.where(valid, jnp.where(forced, FORCED_SCORE, imp), NEG)
    top_val, top_idx = lax.top_k(score, min(SEL_TOPN, n_sel))
    chosen = top_val > 0.5 * NEG
    gather = jax.vmap(jax.vmap(lambda blocks, idx: blocks[idx]))
    ks = gather(ksb, top_idx)
    vs = gather(vsb, top_idx)
    tok = top_idx[..., None] * SEL_BLOCK + jnp.arange(SEL_BLOCK, dtype=jnp.int32)
    smask = chosen[..., None] & (tok <= qpos[None, None, :, None, None])
    n_top = top_idx.shape[-1]
    ss = (jnp.einsum('bgqhd,bgqnld->bgqhnl', qg, ks) * scale).reshape(B, NSA_KV_HEADS, Tq, HEADS_PER_KV, n_top * SEL_BLOCK)
    ps = masked_softmax(ss, smask.reshape(B, NSA_KV_HEADS, Tq, 1, n_top * SEL_BLOCK))
    ps = ps.reshape(B, NSA_KV_HEADS, Tq, HEADS_PER_KV, n_top, SEL_BLOCK)
    o_sel = jnp.einsum('bgqhnl,bgqnld->bgqhd', ps.astype(vs.dtype), vs)
    to_heads = lambda o: o.transpose(0, 2, 1, 3, 4).reshape(B, Tq, NSA_HEADS, HEAD_DIM)
    return to_heads(o_cmp), to_heads(o_sel)

def window_attend(q, qpos, kw, vw, kpos):
    B, Tq = q.shape[:2]
    qg = q.reshape(B, Tq, NSA_KV_HEADS, HEADS_PER_KV, HEAD_DIM)
    s = jnp.einsum('bqghd,bkgd->bgqhk', qg, kw) * (HEAD_DIM ** -0.5)
    rel = qpos[:, None] - kpos[None, :]
    mask = ((rel >= 0) & (rel < WINDOW) & (kpos[None, :] >= 0))[None, None, :, None, :]
    p = masked_softmax(s, mask)
    o = jnp.einsum('bgqhk,bkgd->bqghd', p.astype(vw.dtype), vw)
    return o.reshape(B, Tq, NSA_HEADS, HEAD_DIM)

def combine_branches(o_cmp, o_sel, o_win, g):
    return g[..., 0:1] * o_cmp + g[..., 1:2] * o_sel + g[..., 2:3] * o_win

def nsa_prompt(q, kv_rows, win_rows, gates, lp):
    B, T = q.shape[:2]
    kc = compress(kv_rows[:, :, 0], lp["cmp_pe"][0], lp["cmp_w1"][0], lp["cmp_w2"][0])
    vc = compress(kv_rows[:, :, 1], lp["cmp_pe"][1], lp["cmp_w1"][1], lp["cmp_w2"][1])
    n_sel = T // SEL_BLOCK
    to_blocks = lambda r: r.reshape(B, n_sel, SEL_BLOCK, NSA_KV_HEADS, HEAD_DIM).transpose(0, 3, 1, 2, 4)
    ksb, vsb = to_blocks(kv_rows[:, :, 2]), to_blocks(kv_rows[:, :, 3])
    pad = ((0, 0), (WINDOW, 0), (0, 0), (0, 0))
    kw_pad = jnp.pad(win_rows[:, :, 0], pad)
    vw_pad = jnp.pad(win_rows[:, :, 1], pad)

    def one_block(i):
        qs = i * Q_BLOCK
        qb = lax.dynamic_slice_in_dim(q, qs, Q_BLOCK, axis=1)
        gb = lax.dynamic_slice_in_dim(gates, qs, Q_BLOCK, axis=1)
        qpos = qs + jnp.arange(Q_BLOCK, dtype=jnp.int32)
        o_cmp, o_sel = cmp_sel_attend(qb, qpos, kc, vc, ksb, vsb)
        kw = lax.dynamic_slice_in_dim(kw_pad, qs, Q_BLOCK + WINDOW, axis=1)
        vw = lax.dynamic_slice_in_dim(vw_pad, qs, Q_BLOCK + WINDOW, axis=1)
        kpos = qs - WINDOW + jnp.arange(Q_BLOCK + WINDOW, dtype=jnp.int32)
        o_win = window_attend(qb, qpos, kw, vw, kpos)
        return combine_branches(o_cmp, o_sel, o_win, gb).astype(q.dtype)

    o = lax.map(one_block, jnp.arange(T // Q_BLOCK, dtype=jnp.int32))
    o = jnp.moveaxis(o, 0, 1).reshape(B, T, NSA_WIDTH)
    return o, win_rows[:, T - min(WINDOW, T):]

def nsa_sample(q, kv_rows, win_rows, gates, lp, past_kv, win_buf):
    B, Tn = q.shape[:2]
    past_len = past_kv.shape[1]
    full = lambda c: jnp.concatenate([past_kv[:, :, c].astype(kv_rows.dtype), kv_rows[:, :, c]], axis=1)
    kc = compress(full(0), lp["cmp_pe"][0], lp["cmp_w1"][0], lp["cmp_w2"][0])
    vc = compress(full(1), lp["cmp_pe"][1], lp["cmp_w1"][1], lp["cmp_w2"][1])
    L = past_len + Tn
    n_sel = -(-L // SEL_BLOCK)
    pad = ((0, 0), (0, n_sel * SEL_BLOCK - L), (0, 0), (0, 0))
    to_blocks = lambda r: jnp.pad(r, pad).reshape(B, n_sel, SEL_BLOCK, NSA_KV_HEADS, HEAD_DIM).transpose(0, 3, 1, 2, 4)
    ksb, vsb = to_blocks(full(2)), to_blocks(full(3))
    qpos = past_len + jnp.arange(Tn, dtype=jnp.int32)
    o_cmp, o_sel = cmp_sel_attend(q, qpos, kc, vc, ksb, vsb)
    wb = win_buf.shape[1]
    win_all = jnp.concatenate([win_buf.astype(win_rows.dtype), win_rows], axis=1)
    kpos = past_len - wb + jnp.arange(wb + Tn, dtype=jnp.int32)
    o_win = window_attend(q, qpos, win_all[:, :, 0], win_all[:, :, 1], kpos)
    o = combine_branches(o_cmp, o_sel, o_win, gates).astype(q.dtype)
    return o.reshape(B, Tn, NSA_WIDTH), win_all[:, Tn:]

def wkv_scan(r, decay, k, v, a, b, s0):
    def step(s, inp):
        r_t, w_t, k_t, v_t, a_t, b_t = inp
        sa = jnp.einsum('bhvk,bhk->bhv', s, a_t)
        s = s * w_t[:, :, None, :] + sa[..., None] * b_t[:, :, None, :] + v_t[..., None] * k_t[:, :, None, :]
        return s, jnp.einsum('bhvk,bhk->bhv', s, r_t)
    xs = tuple(jnp.moveaxis(t, 1, 0) for t in (r, decay, k, v, a, b))
    s, y = lax.scan(step, s0, xs)
    return jnp.moveaxis(y, 0, 1), s

def rwkv_time_mix(proj, prev, s0, lp):
    B, T, _ = proj.shape
    f32 = jnp.float32
    p = proj.astype(f32)
    shifted = jnp.concatenate([prev.astype(f32)[:, None], p[:, :-1]], axis=1)
    xs = p + (shifted - p) * lp["rwkv_mu"].astype(f32)
    o1, o2, o3 = RWKV_WIDTH, 2 * RWKV_WIDTH, 3 * RWKV_WIDTH
    o4, o5 = o3 + DECAY_LORA, o3 + DECAY_LORA + AAA_LORA
    r, k, v = xs[..., :o1], xs[..., o1:o2], xs[..., o2:o3]
    wl, al, gl = xs[..., o3:o4], xs[..., o4:o5], xs[..., o5:]
    w = -jax.nn.softplus(-(lp["rwkv_w0"].astype(f32) + jnp.tanh(wl) @ lp["rwkv_w_up"].astype(f32))) - 0.5
    decay = jnp.exp(-jnp.exp(w))
    a = jax.nn.sigmoid(lp["rwkv_a0"].astype(f32) + al @ lp["rwkv_a_up"].astype(f32))
    g = jax.nn.sigmoid(gl) @ lp["rwkv_g_up"].astype(f32)
    heads = lambda t: t.reshape(B, T, RWKV_HEADS, RWKV_HEAD)
    kk = heads(k * lp["rwkv_k_k"].astype(f32))
    kk = kk / jnp.maximum(jnp.sqrt(jnp.sum(kk * kk, axis=-1, keepdims=True)), 1e-12)
    k = k * (1.0 + (a - 1.0) * lp["rwkv_k_a"].astype(f32))
    rh, kh, vh, ah = heads(r), heads(k), heads(v), heads(a)
    y, s = wkv_scan(rh, heads(decay), kh, vh, -kk, kk * ah, s0.astype(f32))
    mu = jnp.mean(y, axis=-1, keepdims=True)
    var = jnp.mean(jnp.square(y - mu), axis=-1, keepdims=True)
    lnx_w = lp["rwkv_lnx_w"].astype(f32).reshape(RWKV_HEADS, RWKV_HEAD)
    lnx_b = lp["rwkv_lnx_b"].astype(f32).reshape(RWKV_HEADS, RWKV_HEAD)
    y = (y - mu) * lax.rsqrt(var + LNX_EPS) * lnx_w + lnx_b
    y = y + jnp.sum(rh * kh * lp["rwkv_r_k"].astype(f32), axis=-1, keepdims=True) * vh
    out = y.reshape(B, T, RWKV_WIDTH) * g
    return out.astype(proj.dtype), proj[:, -1], s

def conv_ffn(x, prev, lp):
    T = x.shape[1]
    u = x @ lp["ffn_w_up"]
    gate, val = u[..., :D_FF], u[..., D_FF:]
    ext = jnp.concatenate([prev.astype(gate.dtype), gate], axis=1)
    conv = lp["ffn_conv_b"] + sum(ext[:, j:j + T] * lp["ffn_conv_w"][j] for j in range(CONV_WIDTH))
    h = jax.nn.gelu(conv) * val
    return h @ lp["ffn_w_down"], ext[:, -(CONV_WIDTH - 1):]

def layer_step(x, pos, nsa_fn, shift_prev, wkv_prev, conv_prev, lp):
    h = rms_norm(x, lp["norm_mix_pre"])
    proj = h @ lp["w_in"]
    q, kv_rows, win_rows, gates = nsa_project(proj[..., :NSA_PROJ], pos)
    o_nsa, win_state = nsa_fn(q, kv_rows, win_rows, gates)
    o_rwkv, shift_new, wkv_new = rwkv_time_mix(proj[..., NSA_PROJ:], shift_prev, wkv_prev, lp)
    mixed = jnp.concatenate([o_nsa.astype(x.dtype), o_rwkv.astype(x.dtype)], axis=-1) @ lp["w_out"]
    x = x + rms_norm(mixed, lp["norm_mix_post"])
    f, conv_new = conv_ffn(rms_norm(x, lp["norm_ffn_pre"]), conv_prev, lp)
    x = x + rms_norm(f, lp["norm_ffn_post"])
    return x, kv_rows, win_state, wkv_new, shift_new, conv_new

def setup_inputs(seed: int = 0) -> dict:
    key = jax.random.key(seed)
    ks = iter(jax.random.split(key, 40))
    f32 = jnp.float32
    nrm = lambda shape, scale: scale * jax.random.normal(next(ks), shape, f32)
    n_pages = PAST_LEN // PAGE_SIZE
    n_used = DEC_BATCH * n_pages
    n_pool = n_used + max(1, n_used // 4)
    wb = min(WINDOW, PAST_LEN)
    return {
        "x_prompt": nrm((BATCH, SEQ, D_MODEL), 1.0),
        "x_sample": nrm((DEC_BATCH, DEC_SEQ, D_MODEL), 1.0),
        "cache_kv": nrm((DEPTH, n_pool, PAGE_SIZE, 4, NSA_KV_HEADS, HEAD_DIM), 1.0),
        "page_table": jax.random.permutation(next(ks), n_pool)[:n_used].reshape(DEC_BATCH, n_pages).astype(jnp.int32),
        "state_win": nrm((DEPTH, DEC_BATCH, wb, 2, NSA_KV_HEADS, HEAD_DIM), 1.0),
        "state_wkv": nrm((DEPTH, DEC_BATCH, RWKV_HEADS, RWKV_HEAD, RWKV_HEAD), 0.5),
        "state_shift": nrm((DEPTH, DEC_BATCH, RWKV_PROJ), 1.0),
        "state_conv": nrm((DEPTH, DEC_BATCH, CONV_WIDTH - 1, D_FF), 1.0),
        "norm_mix_pre": 1.0 + nrm((DEPTH, D_MODEL), 0.05),
        "norm_mix_post": 1.0 + nrm((DEPTH, D_MODEL), 0.05),
        "norm_ffn_pre": 1.0 + nrm((DEPTH, D_MODEL), 0.05),
        "norm_ffn_post": 1.0 + nrm((DEPTH, D_MODEL), 0.05),
        "w_in": nrm((DEPTH, D_MODEL, IN_PROJ), D_MODEL ** -0.5),
        "w_out": nrm((DEPTH, MIX_WIDTH, D_MODEL), MIX_WIDTH ** -0.5),
        "cmp_pe": nrm((DEPTH, 2, CMP_BLOCK, HEAD_DIM), 0.1),
        "cmp_w1": nrm((DEPTH, 2, CMP_BLOCK, HEAD_DIM, CMP_HIDDEN), (CMP_BLOCK * HEAD_DIM) ** -0.5),
        "cmp_w2": nrm((DEPTH, 2, CMP_HIDDEN, HEAD_DIM), 1.5 * CMP_HIDDEN ** -0.5),
        "rwkv_mu": jax.random.uniform(next(ks), (DEPTH, RWKV_PROJ), f32, 0.05, 0.95),
        "rwkv_w0": jnp.linspace(-6.5, -1.5, RWKV_WIDTH, dtype=f32)[None, :] + nrm((DEPTH, RWKV_WIDTH), 0.1),
        "rwkv_w_up": nrm((DEPTH, DECAY_LORA, RWKV_WIDTH), 0.1),
        "rwkv_a0": nrm((DEPTH, RWKV_WIDTH), 0.5),
        "rwkv_a_up": nrm((DEPTH, AAA_LORA, RWKV_WIDTH), 0.1),
        "rwkv_g_up": nrm((DEPTH, GATE_LORA, RWKV_WIDTH), GATE_LORA ** -0.5),
        "rwkv_k_k": 0.85 + nrm((DEPTH, RWKV_WIDTH), 0.05),
        "rwkv_k_a": 1.0 + nrm((DEPTH, RWKV_WIDTH), 0.05),
        "rwkv_r_k": nrm((DEPTH, RWKV_HEADS, RWKV_HEAD), 0.1),
        "rwkv_lnx_w": 1.0 + nrm((DEPTH, RWKV_WIDTH), 0.05),
        "rwkv_lnx_b": nrm((DEPTH, RWKV_WIDTH), 0.02),
        "ffn_w_up": nrm((DEPTH, D_MODEL, 2 * D_FF), D_MODEL ** -0.5),
        "ffn_conv_w": nrm((DEPTH, CONV_WIDTH, D_FF), 0.5),
        "ffn_conv_b": nrm((DEPTH, D_FF), 0.02),
        "ffn_w_down": nrm((DEPTH, D_FF, D_MODEL), D_FF ** -0.5),
    }

def reference(x_prompt, x_sample, cache_kv, page_table, state_win, state_wkv, state_shift, state_conv,
              norm_mix_pre, norm_mix_post, norm_ffn_pre, norm_ffn_post, w_in, w_out,
              cmp_pe, cmp_w1, cmp_w2, rwkv_mu, rwkv_w0, rwkv_w_up, rwkv_a0, rwkv_a_up, rwkv_g_up,
              rwkv_k_k, rwkv_k_a, rwkv_r_k, rwkv_lnx_w, rwkv_lnx_b,
              ffn_w_up, ffn_conv_w, ffn_conv_b, ffn_w_down):
    B, T, _ = x_prompt.shape
    DB, TN, _ = x_sample.shape
    pos_p = jnp.arange(T, dtype=jnp.int32)
    pos_s = PAST_LEN + jnp.arange(TN, dtype=jnp.int32)
    xp, xs = x_prompt, x_sample
    outs_p, outs_s = [], []
    for l in range(DEPTH):
        lp = {
            "norm_mix_pre": norm_mix_pre[l], "norm_mix_post": norm_mix_post[l],
            "norm_ffn_pre": norm_ffn_pre[l], "norm_ffn_post": norm_ffn_post[l],
            "w_in": w_in[l], "w_out": w_out[l],
            "cmp_pe": cmp_pe[l], "cmp_w1": cmp_w1[l], "cmp_w2": cmp_w2[l],
            "rwkv_mu": rwkv_mu[l], "rwkv_w0": rwkv_w0[l], "rwkv_w_up": rwkv_w_up[l],
            "rwkv_a0": rwkv_a0[l], "rwkv_a_up": rwkv_a_up[l], "rwkv_g_up": rwkv_g_up[l],
            "rwkv_k_k": rwkv_k_k[l], "rwkv_k_a": rwkv_k_a[l], "rwkv_r_k": rwkv_r_k[l],
            "rwkv_lnx_w": rwkv_lnx_w[l], "rwkv_lnx_b": rwkv_lnx_b[l],
            "ffn_w_up": ffn_w_up[l], "ffn_conv_w": ffn_conv_w[l], "ffn_conv_b": ffn_conv_b[l],
            "ffn_w_down": ffn_w_down[l],
        }
        xp, *st_p = layer_step(
            xp, pos_p, lambda q, kv, w, g: nsa_prompt(q, kv, w, g, lp),
            jnp.zeros((B, RWKV_PROJ), xp.dtype),
            jnp.zeros((B, RWKV_HEADS, RWKV_HEAD, RWKV_HEAD), jnp.float32),
            jnp.zeros((B, CONV_WIDTH - 1, D_FF), xp.dtype), lp)
        past = cache_kv[l, page_table].reshape(DB, -1, 4, NSA_KV_HEADS, HEAD_DIM)
        buf = state_win[l]
        xs, *st_s = layer_step(
            xs, pos_s, lambda q, kv, w, g: nsa_sample(q, kv, w, g, lp, past, buf),
            state_shift[l], state_wkv[l], state_conv[l], lp)
        outs_p.append(st_p)
        outs_s.append(st_s)
    stack = lambda outs, i: jnp.stack([o[i] for o in outs])
    return (xp, xs, stack(outs_p, 0), stack(outs_s, 0), stack(outs_p, 1), stack(outs_s, 1),
            stack(outs_p, 2), stack(outs_s, 2), stack(outs_p, 3), stack(outs_s, 3),
            stack(outs_p, 4), stack(outs_s, 4))


_drawn_inputs = setup_inputs


def setup_inputs(seed=0):
    import zlib

    import numpy as np

    out = dict(_drawn_inputs(seed))
    spreads = {}
    factors = {'rwkv_lnx_b': 2.915, 'ffn_conv_b': 2.801}
    for name, (base, spread) in spreads.items():
        noise = np.random.default_rng([zlib.crc32(name.encode()), seed]).standard_normal(out[name].shape)
        drawn = base * np.exp(spread * noise) if base else spread * noise
        out[name] = __import__('jax').numpy.asarray(drawn.astype(out[name].dtype))
    for name, factor in factors.items():
        out[name] = (out[name] * factor).astype(out[name].dtype)
    return out
```

```python
from contextlib import ExitStack
import math

import numpy as np
import concourse.bass as bass
from concourse import mybir

F32 = mybir.dt.float32
F32R = mybir.dt.float32r
I32 = mybir.dt.int32
ALU = mybir.AluOpType
ACT = mybir.ActivationFunctionType
AX = mybir.AxisListType.X

P = 128
D_MODEL, SEQ, DEPTH, DEC, PAST, PAGE = 1024, 512, 2, 8, 2048, 128
HD, HEADS, GROUPS = 64, 8, 2
PER = HEADS // GROUPS
TOK = SEQ + DEC
HALF = TOK // 2
KB = D_MODEL // P
PAGES = PAST // PAGE
N_POOL = (DEC * PAGES) + (DEC * PAGES) // 4
STRIDE, BLOCK = 16, 32
NCP = SEQ // STRIDE - 1
NCS = (PAST + 1) // STRIDE - 1
SELB = 64
NSEL = -(-(PAST + 1) // SELB)
WIN = 512
ROPE, THETA = HD // 4, 500000.0
RW = 512
RJ = RW // P
RP = 3 * RJ + 2
FF = 2816
FT = FF // P
NT = 10
CH = 64
SC = 128
NQ = SEQ // P
NEG = -1e30
ROWS = DEC * HEADS
EPS, LNX_EPS = 1e-6, 64e-5

C_IN, C_GATE = 0, NT + RP
C_OUT = C_GATE + 1
C_UP = C_OUT + KB
C_DOWN = C_UP + 2 * FT
DCH = [(0, 8), (8, 16), (16, FT)]
N_CHUNK = C_DOWN + 3 * KB
RING = 3
RING_HI = 2

COLS = {}
_n = 0
for _name, _w in [("mix_pre", KB), ("mix_post", KB), ("ffn_pre", KB), ("ffn_post", KB), ("mu", RP),
                  ("w0", RJ), ("a0", RJ), ("k_k", RJ), ("k_a", RJ), ("r_k", RJ), ("lnw", RJ),
                  ("lnb", RJ), ("cw0", FT), ("cw1", FT), ("cw2", FT), ("cb", FT)]:
    COLS[_name] = (_n, _n + _w)
    _n += _w
NCOL = _n

LEVELS = 6
CONST = {}
_n = 0
for _name, _w in [("ident", P), ("blk", P), ("causal", P), ("rot", P), ("gmask", P), ("scan", RJ * SC), ("eye", CH), ("lev", LEVELS * CH), ("lev0t", CH),
                  ("cmask", NQ * NCP), ("hit", NSEL), ("same", ROWS), ("selb", DEC),
                  ("keep", NSEL), ("force", NSEL)]:
    CONST[_name] = (_n, _n + _w)
    _n += _w
NCONST = _n


def constants():
    c = np.zeros((P, NCONST), np.float32)

    def put(name, a):
        lo, hi = CONST[name]
        c[:a.shape[0], lo:hi] = a

    p = np.arange(P)
    s64, t64 = np.arange(CH)[:, None], np.arange(CH)[None, :]
    two = lambda a: np.concatenate([a, a], 0)
    put("ident", np.eye(P))
    put("blk", (p[:, None] // HD == p[None, :] // HD).astype(np.float32))
    put("causal", np.where(p[None, :] <= p[:, None], 0.0, NEG))
    rot = np.zeros((P, P))
    half = ROPE // 2
    for g in range(GROUPS):
        for i in range(half):
            rot[g * HD + half + i, g * HD + i] = -1.0
            rot[g * HD + i, g * HD + half + i] = 1.0
    put("rot", rot)
    put("gmask", two(np.concatenate([s64 < t64, s64 <= t64], 1).astype(np.float32)))
    inv = np.float32(THETA) ** (-np.arange(half, dtype=np.float32) / np.float32(half))
    pos = np.concatenate([np.arange(SEQ), np.full(DEC, PAST)]).astype(np.float32)
    ang = (pos[None, :] * inv.astype(np.float32)[:, None]).astype(np.float32)
    cos, sin = np.ones((P, TOK), np.float32), np.zeros((P, TOK), np.float32)
    for g in range(GROUPS):
        for k in range(2):
            r = slice(g * HD + k * half, g * HD + (k + 1) * half)
            cos[r], sin[r] = np.cos(ang), np.sin(ang)
    put("scan", np.tile((np.arange(RJ * SC) % CH != 0).astype(np.float32), (P, 1)))
    put("eye", two(np.eye(CH)))
    lev = [(s64 // (2 << i) == t64 // (2 << i)) & (s64 // (1 << i) % 2 == 0) & (t64 // (1 << i) % 2 == 1)
           for i in range(LEVELS)]
    put("lev", two(np.concatenate(lev, 1).astype(np.float32)))
    put("lev0t", two(lev[0].T.astype(np.float32)))
    q = np.arange(SEQ).reshape(NQ, P).T
    end = np.arange(NCP) * STRIDE + BLOCK - 1
    put("cmask", np.where(end[None, None, :] <= q[:, :, None], 0.0, NEG).reshape(P, -1))
    c0, s0 = np.arange(NCS) * STRIDE, np.arange(NSEL) * SELB
    put("hit", ((c0[:, None] < s0 + SELB) & (c0[:, None] + BLOCK > s0)).astype(np.float32))
    r = np.arange(ROWS)
    put("same", (r[:, None] // PER == r[None, :] // PER).astype(np.float32))
    put("selb", (r[:, None] // HEADS == np.arange(DEC)[None, :]).astype(np.float32))
    cur = PAST // SELB
    forced = np.isin(np.arange(NSEL), [0, cur, cur - 1]).astype(np.float32)
    put("keep", np.tile(1.0 - forced, (ROWS, 1)))
    put("force", np.tile(forced * 1e9, (ROWS, 1)))
    return c, np.concatenate([cos, sin], 1)


class Order:

    def __init__(self, eng, sem):
        self.eng, self.sem, self.n = eng, sem, 0

    def go(self, ins):
        self.n += 1
        ins.then_inc(self.sem, 1)

    def settle(self):
        self.eng.wait_ge(self.sem, self.n)

    def do(self, ins):
        self.go(ins)
        self.settle()

    def tell(self, sem):
        self.settle()
        self.eng.sem_inc(sem, 1)


def build(nc, I, O):
    with ExitStack() as ctx:
        def sb(name, shape, dt=F32):
            return ctx.enter_context(nc.sbuf_tensor(name, shape, dt))

        def at_bytes(name, base, floats, shape):
            return nc.alloc_sbuf_tensor_at(name, shape, F32R, offset=base + 4 * floats)

        x = sb("x", [P, KB, TOK])
        hm = sb("hm", [P, KB, TOK])
        nsa = sb("nsa", [P, NT, TOK])
        ring_base = nc.sbuf_base
        ring = sb("ring", [P, RING, KB * P])
        ring_lo = at_bytes("ring_lo", ring_base, 0, [P, RING, KB * P])
        ring_hi = sb("ring_hi", [P, RING_HI, KB * P], F32R)
        cst = sb("cst", [P, NCONST])
        par = sb("par", [P, NCOL])
        gates = sb("gates", [P, NQ + 1, 24])
        gate_s = sb("gate_s", [ROWS, 3])
        state = sb("state", [P, RJ, CH])
        rstd = sb("rstd", [P, 2, HALF])
        pages = sb("pages", [1, DEC * PAGES], I32)
        ones = sb("ones", [P, P])
        onesblk = sb("onesblk", [P, P])

        ARENA = 30900
        arena_base = nc.sbuf_base
        arena = sb("arena", [P, ARENA])
        where = [0]

        def at(*shape, reset=None):
            if reset is not None:
                where[0] = reset
            n = int(np.prod(shape))
            a = arena[:, where[0]:where[0] + n]
            where[0] += n
            assert where[0] <= ARENA, where[0]
            if len(shape) > 1:
                names = "abcde"[:len(shape)]
                a = a.rearrange(f"p ({' '.join(names)}) -> p {' '.join(names)}",
                                **{k: s for k, s in zip(names[1:], shape[1:])})
            return a

        sq = at(KB, TOK, reset=0)
        pr = at(RP, 1 + TOK, reset=0)
        prev_s = at(RP, DEC)
        lora = at(2 * RW)
        rw0 = where[0]
        dif = at(RP, SC)
        xs = at(RP, SC)
        tanw = at(SC)
        siggl = at(SC)
        sw = at(RJ, SC)
        aa = at(RJ, SC)
        gg = at(RJ, SC)
        kk = at(RJ, SC)
        t0 = at(RJ, SC)
        t1 = at(RJ, SC)
        km = at(RJ, SC)
        cum = at(RJ, SC)
        pin = at(RJ, SC)
        pex = at(RJ, SC)
        piv = at(RJ, SC)
        ar = at(RJ, 2, 2, CH)
        bt = at(RJ, SC)
        kt = at(RJ, SC)
        rk = at(RJ, SC)
        gb = at(2, RJ, 2, CH)
        gk = at(2, RJ, 2, CH)
        zz = at(2, RJ, CH)
        ww = at(2, RJ, CH)
        mm = at(LEVELS - 1, 2 * RJ, CH)
        qq = at(2, RJ, CH)
        btm = at(2, RJ, CH)
        ktm = at(2, RJ, CH)
        vtm = at(2, RJ, CH)
        rh = at(RJ, CH)
        uu = at(RJ, CH)
        ss = at(RJ, DEC, CH, reset=rw0 + 2 * RP * SC + 2 * SC + 11 * RJ * SC)
        s1 = at(RJ, DEC, CH)
        s2 = at(RJ, DEC, CH)
        cache = at(2, 8192, reset=0)
        w1 = at(2, BLOCK, P)
        w2 = at(2, P)
        pe_c = at(2, BLOCK)
        cb = at(2)
        n0 = where[0]
        kcs = at(DEC, NCS)
        vcs = at(DEC, P)
        hid = at(2, 2, NCS + 1)
        ssel = at(NSEL, SELB, reset=n0)
        at(72 + 512, reset=n0 + NSEL * SELB)
        qpad = at(DEC, ROWS)
        pt_s = at(PAGES, ROWS)
        swin = at(WIN)
        ptw = at(4, ROWS)
        pcs = at(NCS + 1)
        pct = at(ROWS)
        imp = at(NSEL)
        work = at(NSEL)
        top = at(8)
        diag = at(2, ROWS)
        pnew = at(2, ROWS)
        vnew = at(2, P)
        impt = at(ROWS)
        sm = at(16)
        vt = at(2, NQ, P, reset=n0)
        kcp = at(NCP)
        vcp = at(P)
        hip = at(2, NCP)
        ppt = at(2, 2, WIN)
        pc = at(HEADS, NCP)
        nm = at(2, 2)
        sums = at(2, 2)
        rr = at(2, 2)
        cm = at(3, HEADS)
        pp = at(2, 2, WIN, reset=8192)
        pcp = at(HEADS, P)
        tr = at(TOK, reset=0)
        tr2 = at(TOK)
        trig = at(2, TOK)
        hf = at(FT, TOK, reset=0)
        gx = at(2, 2 + TOK)
        cv = at(2, TOK)
        cprev = at(FT, 2, DEC)
        cout = at(FT, 2)
        couts = at(FT, 2, DEC)
        sq2 = at(KB, TOK)

        HS = 20480
        hm_hi = at_bytes("hm_hi", arena_base, HS, [P, KB, TOK])
        hm_lo = at_bytes("hm_lo", arena_base, HS + KB * TOK, [P, KB, TOK])
        hf_lo = at_bytes("hf_lo", arena_base, 0, [P, FT, TOK])
        hf_hi = at_bytes("hf_hi", arena_base, 14272, [P, FT, TOK])

        ps = ctx.enter_context(nc.psum_tensor("ps", [P, 8, 512], F32))

        names = ("arrive v_own a_own p_own params w_used evac_a evac_v gate_mm gate_ev norm_sq norm_mm "
                 "norm_v norm_a norm_h rs_x rs_act rs_lora rs_prep rs_mm rs_var rs_out gs_ready loads_s stores "
                 "rope_mm rope_ok nsa_ready w1_zero w1_ready vt_mm vt_ev cmpp_mm gelu_p kcp_ok at_mm pc_sub pc_exp "
                 "pc_ok pcp_ok sc_mm mx ex sc_v pt_mm pt_ev_a pt_ev_v pv o_ev qpad_ok ss_mm ss_v ss_a c_free "
                 "cmp_h cmp_act cmp_o cmp_k mixed ffn_c ffn_act ffn_h ffn_t w_hi w_lo s_hi s_lo trig_ok").split()
        loop_names = ("l_arrive lv la lp x1 act1 lora1 sig1 ld_ok kk1 root1 exp1 prep gmm gmask nmm mm_ok inv_q inv_qc "
                      "inv_d inv_z tm_mm tm_ev rh_mm rh_ev u_mm u_ev ds_mm s_ok y_ev mean_mm yc var_mm var_v "
                      "var_a").split()
        S = {n: ctx.enter_context(nc.semaphore(n)) for n in names}
        T = {n: ctx.enter_context(nc.semaphore("loop_" + n)) for n in loop_names}
        w_ready = [ctx.enter_context(nc.semaphore(f"w_ready{i}")) for i in range(RING)]
        c_ready = [ctx.enter_context(nc.semaphore(f"c_ready{i}")) for i in range(2)]
        go = {e: ctx.enter_context(nc.semaphore(f"go_{e}")) for e in ("pe", "v", "a", "p")}
        const_ok = ctx.enter_context(nc.semaphore("const_ok"))
        ones_ok = ctx.enter_context(nc.semaphore("ones_ok"))
        p_const = ctx.enter_context(nc.semaphore("p_const"))
        block = ctx.enter_context(nc.Block())

        def K(name, rows=P):
            lo, hi = CONST[name]
            return cst[0:rows, lo:hi]

        def C(name, i=None):
            lo, hi = COLS[name]
            return par[:, lo:hi] if i is None else par[:, lo + i:lo + i + 1]

        ident, blk = K("ident"), K("blk")
        eye = K("eye")

        def wide(col, n):
            return col.unsqueeze(2).to_broadcast((P, col.shape[1], n))

        def bank2(b):
            return ps[:, b:b + 2, 0:HALF]

        def halves(a):
            return a.rearrange("p (h n) -> p h n", h=2)

        def b4(i, n=SC):
            return ps[:, i, 0:RJ * n].rearrange("p (j n) -> p j n", j=RJ)

        HALVES = [(h, slice(h * HALF, (h + 1) * HALF)) for h in range(2)]
        UNITS = [(t, i, g) for t in range(NQ) for i in range(PER) for g in range(GROUPS)]
        CMP_U = DEC // 2
        N_UNIT = 1 + CMP_U + 4

        def tile_done(n):
            if n < NT + RP:
                return n + 1
            down = n - (NT + RP + KB + 2 * FT)
            return n + 2 if down < 0 else C_DOWN + 3 * (down + 1)

        def meet(eng, who, arrive):
            eng.sem_inc(arrive, 1)
            eng.wait_ge(go[who], 1)
            eng.sem_clear(go[who])

        @block.sync
        def _(sp):
            sp.dma_start(cst[:], I["consts"]).then_inc(const_ok, 16)
            sp.dma_start(pages[:], I["pages"]).then_inc(const_ok, 16)
            sp.dma_start(x[:], I["x"].rearrange("k p t -> p k t")).then_inc(const_ok, 16)

            def host_meet(arrive, sems):
                sp.wait_ge(arrive, 4)
                for s in sems:
                    sp.sem_clear(s)
                for e in go:
                    sp.sem_inc(go[e], 1)

            with sp.Fori(0, DEPTH) as l:
                sp.dma_start(par[:], I["cols"][l]).then_inc(S["params"], 16)
                sp.dma_start(prev_s, I["shift"][l].rearrange("p (a b) -> p a b", a=RP)).then_inc(S["params"], 16)
                sp.dma_start(lora, I["lora"][l]).then_inc(S["params"], 16)

                def chunk(n):
                    if n >= RING:
                        sp.wait_ge(S["w_used"], n - RING + 1)
                    sp.dma_start(ring[:, n % RING, :], I["w"][l, n]).then_inc(w_ready[n % RING], 16)

                for n in range(C_OUT):
                    chunk(n)
                sp.dma_start(ss, I["wkv"][l].rearrange("p (a b c) -> p a b c", a=RJ, b=DEC)).then_inc(S["loads_s"], 16)
                for n in range(C_OUT, C_OUT + RING):
                    chunk(n)
                sp.wait_ge(S["rs_out"], 1)
                sp.dma_start(O["wkv_s"][l].rearrange("p (a b c) -> p a b c", a=RJ, b=DEC), ss).then_inc(S["stores"], 16)
                sp.dma_start(O["shift"][l].rearrange("p (a b) -> p a b", a=RP), pr[:, :, SEQ:SEQ + 1 + DEC]).then_inc(S["stores"], 16)
                sp.wait_ge(S["stores"], 32)
                sp.wait_ge(S["gate_ev"], NQ + 1)
                sp.dma_start(gate_s[:], gates[0:DEC, NQ, :].rearrange("b (h n) -> b h n", n=3)).then_inc(S["gs_ready"], 16)
                with sp.Fori(0, SEQ // SC) as _sc:
                    host_meet(T["l_arrive"], list(T.values()))
                sp.dma_start(O["wkv_p"][l].rearrange("p (a b) -> p a b", a=RJ), state[:]).then_inc(S["stores"], 16)
                sp.dma_start(trig, I["trig"].rearrange("p (a t) -> p a t", a=2)).then_inc(S["trig_ok"], 16)
                sp.wait_ge(S["w1_zero"], 1)
                for c in range(2):
                    for g in range(GROUPS):
                        r = slice(g * HD, (g + 1) * HD)
                        sp.dma_start(w1[r, c, :, r], I["w1"][l, c].rearrange("d (k e) -> d k e", k=BLOCK)).then_inc(S["w1_ready"], 16)
                        sp.dma_start(w2[r, c, r], I["w2"][l, c]).then_inc(S["w1_ready"], 16)
                        sp.dma_start(pe_c[r, c, :], I["pe"][l, c]).then_inc(S["w1_ready"], 16)
                sp.wait_ge(S["nsa_ready"], 1)
                sp.dma_start(O["kv"][l].rearrange("p (a b) -> p a b", a=6), nsa[:, 4:NT, :]).then_inc(S["stores"], 16)
                for b in range(DEC):
                    sp.dma_start(O["win_old"][l, b], I["win"][l, b]).then_inc(S["stores"], 16)

                def page_regs(b):
                    _, pages_b = nc.values_load_multi_w_load_instructions(
                        pages[0:1, b * PAGES:(b + 1) * PAGES], engines=[mybir.EngineType.SP], min_val=0, max_val=N_POOL - 1)
                    return pages_b

                for u in range(N_UNIT):
                    if u == 1:
                        sp.wait_ge(S["o_ev"], NQ)
                    if u >= 2:
                        sp.wait_ge(S["c_free"], u - 1)
                    slot, done = cache[:, u % 2, :], c_ready[u % 2]
                    if u == 0:
                        sp.dma_start(slot[:, 0:DEC * WIN].rearrange("p (b n) -> p b n", b=DEC),
                                     I["kwin"][l].rearrange("b p n -> p b n")).then_inc(done, 16)
                        sp.dma_start(slot[:, DEC * WIN:].rearrange("p (b n) -> p b n", b=DEC),
                                     I["vwin"][l].rearrange("b p n -> p b n")).then_inc(done, 16)
                    elif u <= CMP_U:
                        dst = slot.rearrange("p (c b n t) -> p c b n t", c=2, b=2, t=PAGE)
                        for b in range(2):
                            regs = page_regs(2 * (u - 1) + b)
                            for i, r in enumerate(regs):
                                sp.dma_start(dst[:, :, b, i, :], I["kv_cmp"][l * N_POOL + r].rearrange("p (c t) -> p c t", c=2)).then_inc(done, 16)
                    else:
                        src = I["k_sel"] if u < CMP_U + 3 else I["v_sel"]
                        dst = slot.rearrange("p (b n t) -> p b n t", b=4, t=PAGE)
                        for b in range(4):
                            regs = page_regs(4 * ((u - CMP_U - 1) % 2) + b)
                            for i, r in enumerate(regs):
                                sp.dma_start(dst[:, b, i, :], src[l * N_POOL + r]).then_inc(done, 16)
                for n in range(C_OUT + RING, C_UP):
                    chunk(n)
                sp.wait_ge(S["mixed"], 1)
                sp.dma_start(cprev, I["conv"][l].rearrange("p (a b c) -> p a b c", a=FT, b=2)).then_inc(S["loads_s"], 16)
                for n in range(C_UP, N_CHUNK):
                    chunk(n)
                sp.wait_ge(S["ffn_t"], FT)
                sp.dma_start(O["conv_p"][l].rearrange("p (a b) -> p a b", a=FT), cout).then_inc(S["stores"], 16)
                sp.dma_start(O["conv_s"][l].rearrange("p (a b c) -> p a b c", a=FT, b=2), couts).then_inc(S["stores"], 16)
                sp.wait_ge(S["stores"], 16 * (6 + DEC))
                host_meet(S["arrive"], list(S.values()) + w_ready + c_ready)
            sp.dma_start(O["y"].rearrange("k p t -> p k t"), x[:]).then_inc(const_ok, 16)
            sp.wait_ge(const_ok, 64)

        @block.tensor
        def _(pe):
            mmul = nc.tensor.matmul

            def w_wait(n):
                if n == C_GATE:
                    pe.wait_ge(w_ready[n % RING], 16 * (n // RING + 1))
                else:
                    pe.wait_ge(S["w_lo"], n + 1 - (n > C_GATE))

            dense_n = [0]

            def dense_tile(chunks, hi, lo, first=None):
                b = 2 * (dense_n[0] % 3)
                if dense_n[0] >= 3:
                    pe.wait_ge(S["evac_a"], dense_n[0] - 2)
                    pe.wait_ge(S["evac_v"], dense_n[0] - 2)
                for ci, (n, k0, k1) in enumerate(chunks):
                    w_wait(n)
                    for k in range(k0, k1):
                        if first is not None:
                            pe.wait_ge(S["s_lo"], first + k + 1)
                        w = slice((k - k0) * P, (k - k0 + 1) * P)
                        wh, wl = ring_hi[:, n % RING_HI, w], ring_lo[:, n % RING, w]
                        for h, cols in HALVES:
                            out = ps[:, b + h, 0:HALF]
                            mmul(out, wh, hi[:, k, cols], start=(k == 0), stop=False)
                            mmul(out, wh, lo[:, k, cols], start=False, stop=False)
                            last = mmul(out, wl, hi[:, k, cols], start=False, stop=(ci == len(chunks) - 1 and k == k1 - 1))
                    last.then_inc(S["w_used"], 1)
                dense_n[0] += 1

            norm_n = [0]

            def norm(src):
                pe.wait_ge(S["norm_sq"], norm_n[0] + 1)
                for h, cols in HALVES:
                    for k in range(KB):
                        last = mmul(ps[:, 6 + h, 0:HALF], ones[:], src[:, k, cols], start=(k == 0), stop=(k == KB - 1))
                last.then_inc(S["norm_mm"], 1)
                norm_n[0] += 1

            pe.wait_ge(ones_ok, 1)
            pe.wait_ge(const_ok, 48)
            with pe.Fori(0, DEPTH) as _l:
                dense_n[0] = norm_n[0] = 0
                norm(sq)
                for m in range(NT + RP):
                    dense_tile([(m, 0, KB)], hm_hi, hm_lo, 0 if m == 0 else None)
                w_wait(C_GATE)
                wg = ring[:, C_GATE % RING, 0:KB * 24].rearrange("p (k n) -> p k n", k=KB)
                for t in range(NQ + 1):
                    n = P if t < NQ else DEC
                    if t >= 1:
                        pe.wait_ge(S["gate_ev"], t)
                    for k in range(KB):
                        last = mmul(ps[0:n, 6, 0:24], hm[:, k, t * P:t * P + n], wg[:, k, :], start=(k == 0), stop=(k == KB - 1))
                    last.then_inc(S["gate_mm"], 1)
                pe.wait_ge(S["gate_mm"], NQ + 1)
                pe.sem_inc(S["w_used"], 1)

                def lora_products(n, ready, done):
                    pe.wait_ge(*ready)
                    for j in range(RJ):
                        c = slice(j * P, (j + 1) * P)
                        mmul(ps[:, 0, j * n:(j + 1) * n], lora[0:HD, c], tanw[0:HD, 0:n], start=True, stop=True)
                        mmul(ps[:, 1, j * n:(j + 1) * n], lora[HD:P, c], xs[HD:P, 3 * RJ, 0:n], start=True, stop=True)
                        last = mmul(ps[:, 2, j * n:(j + 1) * n], lora[:, RW + j * P:RW + (j + 1) * P], siggl[:, 0:n], start=True, stop=True)
                    last.then_inc(done, 1)

                pe.wait_ge(S["evac_a"], NT + RP)
                pe.wait_ge(S["evac_v"], NT + RP)
                pe.wait_ge(S["params"], 48)
                pe.wait_ge(S["loads_s"], 16)
                lora_products(DEC, (S["rs_act"], 1), S["rs_lora"])
                pe.wait_ge(S["rs_x"], 1)
                mmul(ps[:, 3, 0:RJ * DEC], blk, t0[:, :, 0:DEC], start=True, stop=True).then_inc(S["rs_mm"], 1)
                pe.wait_ge(S["rs_prep"], 1)
                mmul(ps[:, 3, 0:RJ * DEC], blk, t1[:, :, 0:DEC], start=True, stop=True)
                for part in range(2):
                    for j in range(RJ):
                        for b in range(DEC):
                            for h in range(2):
                                r = slice(h * HD, (h + 1) * HD)
                                if part == 0:
                                    last = mmul(ps[r, 4 + j, b * CH:(b + 1) * CH],
                                                pex[r, j, b:b + 1].to_broadcast((HD, HD)), ss[r, j, b, :], start=True, stop=True)
                                else:
                                    last = mmul(ps[r, 4 + j, b * CH:(b + 1) * CH],
                                                xs[r, 2 * RJ + j, b:b + 1].to_broadcast((HD, HD)), eye[r, :], start=True, stop=True)
                    last.then_inc(S["rs_mm"], 1)
                    pe.wait_ge(S["rs_prep"], 2 + part)
                pe.wait_ge(S["rs_prep"], 4)
                for j in range(RJ):
                    for b in range(DEC):
                        for h in range(2):
                            r = slice(h * HD, (h + 1) * HD)
                            last = mmul(ps[r, 0, j * DEC + b:j * DEC + b + 1], ss[r, j, b, :], xs[r, j, b:b + 1], start=True, stop=True)
                last.then_inc(S["rs_mm"], 1)
                for i, src in ((5, kk), (6, t0)):
                    pe.wait_ge(S["rs_prep"], i)
                    mmul(ps[:, 1, 0:RJ * DEC], onesblk[:], src[:, :, 0:DEC], start=True, stop=True).then_inc(S["rs_mm"], 1)
                pe.wait_ge(S["rs_out"], 1)

                with pe.Fori(0, SEQ // SC) as _sc:
                    lora_products(SC, (T["act1"], 1), T["lora1"])
                    pe.wait_ge(T["x1"], 2)
                    mmul(ps[:, 3, :], blk, t0, start=True, stop=True).then_inc(T["kk1"], 1)
                    pe.wait_ge(T["prep"], 1)
                    mmul(ps[:, 3, :], blk, t1, start=True, stop=True).then_inc(T["kk1"], 1)
                    pe.wait_ge(T["prep"], 2)
                    HP = [(h, slice(h * HD, (h + 1) * HD)) for h in range(2)]
                    for c in range(2):
                        cs = slice(c * CH, (c + 1) * CH)
                        for j in range(RJ):
                            for h, r in HP:
                                mmul(ps[r, 4 + 2 * c, j * P:(j + 1) * P], bt[r, j, cs], ar[r, j, c, :, :], start=True, stop=True)
                                last = mmul(ps[r, 5 + 2 * c, j * P:(j + 1) * P], kt[r, j, cs], ar[r, j, c, :, :], start=True, stop=True)
                        last.then_inc(T["gmm"], 1)
                    for c in range(2):
                        cs = slice(c * CH, (c + 1) * CH)
                        for j in range(RJ):
                            for h, r in HP:
                                last = mmul(ps[r, 0, (c * RJ + j) * CH:(c * RJ + j + 1) * CH], ar[r, j, c, 0, :], bt[r, j, cs], start=True, stop=True)
                    last.then_inc(T["nmm"], 1)
                    for n, src in ((1, bt), (2, kt), (4, None)):
                        if n == 4:
                            pe.wait_ge(T["gmask"], 1)
                        for c in range(2):
                            cs = slice(c * CH, (c + 1) * CH)
                            for j in range(RJ):
                                for h, r in HP:
                                    s = src[r, j, cs] if src is not None else xs[r, 2 * RJ + j, cs]
                                    last = mmul(ps[r, n, (c * RJ + j) * CH:(c * RJ + j + 1) * CH], s, eye[r, :], start=True, stop=True)
                        last.then_inc(T["tm_mm"], 1)
                    for lv in range(1, LEVELS):
                        pe.wait_ge(T["inv_z"], lv)
                        pe.wait_ge(T["mm_ok"], lv)
                        for cj in range(2 * RJ):
                            c, j = divmod(cj, RJ)
                            for h, r in HP:
                                last = mmul(ps[r, 5, cj * CH:(cj + 1) * CH], mm[r, lv - 1, cj, :], ww[r, c, j, :], start=True, stop=True)
                        last.then_inc(T["inv_q"], 1)
                        pe.wait_ge(T["inv_qc"], lv)
                        for cj in range(2 * RJ):
                            c, j = divmod(cj, RJ)
                            for h, r in HP:
                                last = mmul(ps[r, 6, cj * CH:(cj + 1) * CH], qq[r, c, j, :], zz[r, c, j, :], start=True, stop=True)
                                if lv < LEVELS - 1:
                                    last = mmul(ps[r, 7, cj * CH:(cj + 1) * CH], zz[r, c, j, :], qq[r, c, j, :], start=True, stop=True)
                        last.then_inc(T["inv_d"], 1)
                    pe.wait_ge(T["inv_z"], LEVELS)
                    pe.wait_ge(T["tm_ev"], 3)
                    for c in range(2):
                        if c:
                            pe.wait_ge(T["s_ok"], c)
                        for j in range(RJ):
                            for h, r in HP:
                                o = ps[r, 5, j * CH:(j + 1) * CH]
                                mmul(o, ar[r, j, c, 0, :], state[r, j, :], start=True, stop=False)
                                last = mmul(o, gk[r, c, j, 0, :], vtm[r, c, j, :], start=False, stop=True)
                        last.then_inc(T["rh_mm"], 1)
                        pe.wait_ge(T["rh_ev"], c + 1)
                        for j in range(RJ):
                            for h, r in HP:
                                last = mmul(ps[r, 6, j * CH:(j + 1) * CH], zz[r, c, j, :], rh[r, j, :], start=True, stop=True)
                        last.then_inc(T["u_mm"], 1)
                        pe.wait_ge(T["u_ev"], c + 1)
                        for j in range(RJ):
                            for h, r in HP:
                                o = ps[r, 0, j * SC + c * CH:j * SC + (c + 1) * CH]
                                mmul(o, state[r, j, :], ar[r, j, c, 1, :], start=True, stop=False)
                                mmul(o, uu[r, j, :], gb[r, c, j, 1, :], start=False, stop=False)
                                mmul(o, vtm[r, c, j, :], gk[r, c, j, 1, :], start=False, stop=True)
                                o = ps[r, 7, j * CH:(j + 1) * CH]
                                mmul(o, btm[r, c, j, :], uu[r, j, :], start=True, stop=False)
                                last = mmul(o, ktm[r, c, j, :], vtm[r, c, j, :], start=False, stop=True)
                        last.then_inc(T["ds_mm"], 1)
                    pe.wait_ge(T["y_ev"], 1)
                    mmul(ps[:, 1, :], onesblk[:], kk, start=True, stop=True).then_inc(T["mean_mm"], 1)
                    pe.wait_ge(T["yc"], 1)
                    mmul(ps[:, 2, :], onesblk[:], t0, start=True, stop=True).then_inc(T["var_mm"], 1)
                    pe.wait_ge(T["var_mm"], 1)
                    meet(pe, "pe", T["l_arrive"])

                for n, tile in enumerate((0, 1, 2, 3, 4, 6, 8)):
                    if n >= 1:
                        pe.wait_ge(S["rope_ok"], n)
                    for h, cols in HALVES:
                        last = mmul(ps[:, h, 0:HALF], K("rot"), nsa[:, tile, cols], start=True, stop=True)
                    last.then_inc(S["rope_mm"], 1)
                pe.wait_ge(S["rope_ok"], 7)
                for br in range(2):
                    for t in range(NQ):
                        last = nc.tensor.transpose(ps[:, br, t * P:(t + 1) * P], nsa[:, 7 + 2 * br, t * P:(t + 1) * P], ident)
                last.then_inc(S["vt_mm"], 1)
                pe.wait_ge(S["w1_ready"], 16 * 12)
                for c in range(2):
                    for k in range(BLOCK):
                        mmul(ps[:, 2, c:c + 1], w1[:, c, k, :], pe_c[:, c, k:k + 1], start=(k == 0), stop=(k == BLOCK - 1))
                    for k in range(BLOCK):
                        last = mmul(ps[:, 3, c * P:c * P + NCP], w1[:, c, k, :], nsa[:, 4 + c, k:k + STRIDE * (NCP - 1) + 1:STRIDE],
                                    start=(k == 0), stop=(k == BLOCK - 1))
                last.then_inc(S["cmpp_mm"], 1)
                pe.wait_ge(S["gelu_p"], 1)
                mmul(ps[:, 4, 0:NCP], w2[:, 0, :], hip[:, 0, :], start=True, stop=True)
                mmul(ps[0:NCP, 5, 0:P], hip[:, 1, :], w2[:, 1, :], start=True, stop=True).then_inc(S["cmpp_mm"], 1)
                pe.wait_ge(S["kcp_ok"], 1)
                pe.wait_ge(S["vt_ev"], 1)

                def scores(u):
                    t, i, g = UNITS[u]
                    r = slice(g * HD, (g + 1) * HD)
                    b = 2 * (u % 2)
                    if u >= 2:
                        pe.wait_ge(S["ex"], u - 1)
                    for br in range(2):
                        last = mmul(ps[:, b + br, 0:(t + 1) * P], nsa[r, i, t * P:(t + 1) * P],
                                    nsa[r, 6 + 2 * br, 0:(t + 1) * P], start=True, stop=True)
                    last.then_inc(S["sc_mm"], 1)

                def cmp_scores(t):
                    for g in range(GROUPS):
                        if g:
                            pe.wait_ge(S["at_mm"], 4 * t + 1)
                        for i in range(PER):
                            r = slice(g * HD, (g + 1) * HD)
                            h = g * PER + i
                            last = mmul(ps[:, 7, h * NCP:(h + 1) * NCP], nsa[r, i, t * P:(t + 1) * P], kcp[r, :], start=True, stop=True)
                        last.then_inc(S["at_mm"], 1)
                    pe.wait_ge(S["pc_ok"], t + 1)
                    for half in range(2):
                        if half:
                            pe.wait_ge(S["pcp_ok"], 2 * t + 1)
                        for h in range(4):
                            last = nc.tensor.transpose(ps[0:NCP, 7, h * P:(h + 1) * P], pc[:, 4 * half + h, :], ident)
                        last.then_inc(S["at_mm"], 1)
                    pe.wait_ge(S["pcp_ok"], 2 * t + 2)

                def attend(u):
                    t, i, g = UNITS[u]
                    r = slice(g * HD, (g + 1) * HD)
                    h = g * PER + i
                    pe.wait_ge(S["sc_v"], u + 1)
                    for br in range(2):
                        for k in range(t + 1):
                            last = nc.tensor.transpose(ps[:, 4 + br, k * P:(k + 1) * P], pp[:, u % 2, br, k * P:(k + 1) * P], ident)
                    last.then_inc(S["pt_mm"], 1)
                    pe.wait_ge(S["pt_ev_a"], u + 1)
                    pe.wait_ge(S["pt_ev_v"], u + 1)
                    if u % HEADS == 0 and t:
                        pe.wait_ge(S["o_ev"], t)
                    o = ps[r, 6, i * P:(i + 1) * P]
                    mmul(o, vcp[0:NCP, r], pcp[0:NCP, h, :], start=True, stop=False)
                    for br in range(2):
                        for k in range(t + 1):
                            last = mmul(o, vt[:, br, k, r], ppt[:, u % 2, br, k * P:(k + 1) * P], start=False,
                                        stop=(br == 1 and k == t))
                    last.then_inc(S["pv"], 1)

                for u in range(len(UNITS) + 1):
                    if u < len(UNITS):
                        scores(u)
                    if u >= 1:
                        attend(u - 1)
                    if u < len(UNITS) and u % HEADS == 0:
                        cmp_scores(u // HEADS)

                unit_dmas = [2] + [2 * PAGES] * CMP_U + [4 * PAGES] * 4

                def unit(u):
                    pe.wait_ge(c_ready[u % 2], 16 * sum(unit_dmas[u % 2:u + 1:2]))
                    return cache[:, u % 2, :]

                sink = dict(start=False, skip_group_check=True)
                pe.wait_ge(S["qpad_ok"], 1)
                slot = unit(0)
                for b in range(DEC):
                    mmul(ps[0:ROWS, 0, 1:WIN], qpad[:, b, :], slot[:, b * WIN + 1:(b + 1) * WIN], start=(b == 0), stop=(b == DEC - 1))
                for b in range(DEC):
                    mmul(ps[0:ROWS, 1, 0:1], qpad[:, b, :], nsa[:, 8, SEQ + b:SEQ + b + 1], start=(b == 0), stop=(b == DEC - 1))
                for n in range(2):
                    last = nc.tensor.transpose(ps[0:DEC, 2, n * P:(n + 1) * P], nsa[:, 7 + 2 * n, SEQ:TOK], ident)
                last.then_inc(S["ss_mm"], 1)
                pe.wait_ge(S["ss_v"], 2)
                for k in range(4):
                    nc.tensor.transpose(ps[:, 3, k * ROWS:(k + 1) * ROWS], swin[0:ROWS, k * P:(k + 1) * P], ident[0:ROWS, 0:ROWS])
                mmul(ps[0:DEC, 4, 0:ROWS], K("selb", ROWS), diag[0:ROWS, 1, :], start=True, stop=True).then_inc(S["ss_mm"], 1)
                pe.wait_ge(S["ss_v"], 3)
                mmul(ps[:, 7, 0:ROWS], vnew[0:DEC, 1, :], pnew[0:DEC, 1, :], start=True, stop=False, skip_group_check=True)
                for b in range(DEC):
                    for k in range(4):
                        v0 = DEC * WIN + b * WIN + k * P
                        last = mmul(ps[:, 7, b * HEADS:(b + 1) * HEADS], slot[:, v0:v0 + P], ptw[:, k, b * HEADS:(b + 1) * HEADS], stop=False, **sink)
                last.then_inc(S["c_free"], 1)
                for u in range(1, CMP_U + 1):
                    slot = unit(u).rearrange("p (c b n) -> p c b n", c=2, b=2)
                    for c in range(2):
                        for k in range(BLOCK):
                            last = mmul(ps[:, c, 0:2 * NCS], w1[:, c, k, :], slot[:, c, :, k:k + STRIDE * (NCS - 1) + 1:STRIDE],
                                        start=(k == 0), stop=(k == BLOCK - 1))
                    last.then_inc(S["cmp_h"], 1)
                    pe.wait_ge(S["cmp_h"], u)
                    pe.sem_inc(S["c_free"], 1)
                    pe.wait_ge(S["cmp_act"], u)
                    if u >= 2:
                        pe.wait_ge(S["cmp_k"], u - 1)
                    mmul(ps[:, 2, 0:2 * NCS], w2[:, 0, :], hid[:, 0, :, 0:NCS], start=True, stop=True)
                    for b in range(2):
                        last = mmul(ps[0:NCS, 3, b * P:(b + 1) * P], hid[:, 1, b, 0:NCS], w2[:, 1, :], start=True, stop=True)
                    last.then_inc(S["cmp_o"], 1)
                pe.wait_ge(S["cmp_k"], CMP_U)
                for b in range(DEC):
                    last = mmul(ps[0:ROWS, 0, 0:NCS], qpad[:, b, :], kcs[:, b, :], start=(b == 0), stop=(b == DEC - 1))
                last.then_inc(S["ss_mm"], 1)
                pe.wait_ge(S["ss_v"], 5)
                mmul(ps[0:NCS, 1, 0:ROWS], pcs[0:ROWS, 0:NCS], K("same", ROWS), start=True, stop=True).then_inc(S["ss_mm"], 1)
                pe.wait_ge(S["ss_v"], 6)
                mmul(ps[0:ROWS, 2, 0:NSEL], impt[0:NCS, :], K("hit", NCS), start=True, stop=True)
                nc.tensor.transpose(ps[0:NCS, 3, 0:ROWS], pcs[0:ROWS, 0:NCS], ident[0:ROWS, 0:ROWS]).then_inc(S["ss_mm"], 1)
                pe.wait_ge(S["ss_v"], 7)
                for b in range(DEC):
                    mmul(ps[:, 7, b * HEADS:(b + 1) * HEADS], vcs[0:NCS, b, :], pct[0:NCS, b * HEADS:(b + 1) * HEADS], stop=False, **sink)
                for half in range(2):
                    slot = unit(CMP_U + 1 + half).rearrange("p (b n) -> p b n", b=4)
                    for b in range(4):
                        for k in range(4):
                            last = mmul(ps[0:ROWS, k, :], qpad[:, 4 * half + b, :], slot[:, b, k * 512:(k + 1) * 512],
                                        start=(half == 0 and b == 0), stop=(half == 1 and b == 3))
                    last.then_inc(S["c_free"], 1)
                for b in range(DEC):
                    last = mmul(ps[0:ROWS, 4, 0:1], qpad[:, b, :], nsa[:, 6, SEQ + b:SEQ + b + 1], start=(b == 0), stop=(b == DEC - 1))
                last.then_inc(S["ss_mm"], 1)
                pe.wait_ge(S["ss_v"], 9)
                flat = ssel.rearrange("p a b -> p (a b)")
                for k in range(PAGES):
                    nc.tensor.transpose(ps[:, k // 8, (k % 8) * ROWS:(k % 8 + 1) * ROWS], flat[0:ROWS, k * P:(k + 1) * P], ident[0:ROWS, 0:ROWS])
                mmul(ps[0:DEC, 2, 0:ROWS], K("selb", ROWS), diag[0:ROWS, 0, :], start=True, stop=True).then_inc(S["ss_mm"], 1)
                pe.wait_ge(S["ss_v"], 10)
                mmul(ps[:, 7, 0:ROWS], vnew[0:DEC, 0, :], pnew[0:DEC, 0, :], stop=False, **sink)
                for half in range(2):
                    slot = unit(CMP_U + 3 + half).rearrange("p (b n t) -> p b n t", b=4, t=PAGE)
                    for b in range(4):
                        s = 4 * half + b
                        for k in range(PAGES):
                            last = mmul(ps[:, 7, s * HEADS:(s + 1) * HEADS], slot[:, b, k, :], pt_s[:, k, s * HEADS:(s + 1) * HEADS],
                                        stop=(s == DEC - 1 and k == PAGES - 1), **sink)
                last.then_inc(S["ss_mm"], 1)
                pe.wait_ge(S["mixed"], 1)

                for m in range(KB):
                    dense_tile([(C_OUT + m, 0, KB)], hm_hi, hm_lo, KB if m == 0 else None)
                norm(sq2)
                norm(sq2)
                for m in range(2 * FT):
                    dense_tile([(C_UP + m, 0, KB)], hm_hi, hm_lo, 2 * KB if m == 0 else None)
                for m in range(KB):
                    dense_tile([(C_DOWN + 3 * m + i, a, b) for i, (a, b) in enumerate(DCH)], hf_hi, hf_lo, 3 * KB if m == 0 else None)
                norm(sq2)
                pe.wait_ge(S["norm_mm"], 4)
                meet(pe, "pe", S["arrive"])

        @block.scalar
        def _(act):
            o = Order(act, S["a_own"])
            A = nc.scalar.activation
            act.wait_ge(const_ok, 48)
            with act.Fori(0, DEPTH) as _l:
                o.n = 0
                n_dense = [0]

                def norm_root(n):
                    act.wait_ge(S["norm_v"], n)
                    o.do(A(rstd[:], rstd[:], ACT.Sqrt))
                    o.tell(S["norm_a"])

                def evac(dst):
                    n = n_dense[0]
                    act.wait_ge(S["w_used"], tile_done(n))
                    A(dst, ps[:, 2 * (n % 3), 0:HALF], ACT.Copy).then_inc(S["evac_a"], 1)
                    n_dense[0] += 1

                def split_w(*chunks):
                    for n in chunks:
                        if n != C_GATE and n < N_CHUNK:
                            act.wait_ge(w_ready[n % RING], 16 * (n // RING + 1))
                            if n >= RING_HI:
                                act.wait_ge(S["w_used"], n - RING_HI + 1)
                            A(ring_hi[:, n % RING_HI, :], ring[:, n % RING, :], ACT.Copy).then_inc(S["w_hi"], 1)

                def split_s(dst, src, k):
                    A(dst[:, k, :], src[:, k, :], ACT.Copy).then_inc(S["s_hi"], 1)

                def squares(dst, src):
                    for k in range(KB):
                        o.go(A(dst[:, k, :], src[:, k, :], ACT.Square))
                    o.tell(S["norm_sq"])

                squares(sq, x)
                split_w(0, 1)
                norm_root(1)
                for k in range(KB):
                    act.wait_ge(S["norm_h"], k + 1)
                    split_s(hm_hi, hm, k)
                for m in range(NT + RP):
                    if m + 2 < C_GATE:
                        split_w(m + 2)
                    evac(nsa[:, m, 0:HALF] if m < NT else pr[:, m - NT, 1:1 + HALF])
                for t in range(NQ + 1):
                    n = P if t < NQ else DEC
                    act.wait_ge(S["gate_mm"], t + 1)
                    o.do(A(gates[0:n, t, :], ps[0:n, 6, 0:24], ACT.Sigmoid))
                    o.tell(S["gate_ev"])

                act.wait_ge(S["params"], 48)
                act.wait_ge(S["rs_x"], 1)
                o.go(A(tanw[0:HD, 0:DEC], xs[0:HD, 3 * RJ, 0:DEC], ACT.Tanh))
                o.go(A(siggl[:, 0:DEC], xs[:, 3 * RJ + 1, 0:DEC], ACT.Sigmoid))
                o.tell(S["rs_act"])
                act.wait_ge(S["rs_lora"], 1)
                for j in range(RJ):
                    o.go(A(sw[:, j, 0:DEC], ps[:, 0, j * DEC:(j + 1) * DEC], ACT.Sigmoid, bias=C("w0", j)))
                    o.go(A(aa[:, j, 0:DEC], ps[:, 1, j * DEC:(j + 1) * DEC], ACT.Sigmoid, bias=C("a0", j)))
                    o.go(A(gg[:, j, 0:DEC], ps[:, 2, j * DEC:(j + 1) * DEC], ACT.Copy))
                act.wait_ge(S["rs_mm"], 1)
                o.go(A(t1[:, :, 0:DEC], b4(3, DEC), ACT.Sqrt))
                o.settle()
                o.go(A(pin[:, :, 0:DEC], sw[:, :, 0:DEC], ACT.Exp, scale=-math.exp(-0.5)))
                o.tell(S["rs_act"])
                act.wait_ge(S["rs_var"], 1)
                o.go(A(t1[:, :, 0:DEC], t1[:, :, 0:DEC], ACT.Sqrt))
                o.tell(S["rs_act"])
                act.wait_ge(S["rs_out"], 1)

                with act.Fori(0, SEQ // SC) as _sc:
                    q = Order(act, T["la"])
                    act.wait_ge(T["x1"], 1)
                    q.go(A(tanw[0:HD, :], xs[0:HD, 3 * RJ, :], ACT.Tanh))
                    q.go(A(siggl, xs[:, 3 * RJ + 1, :], ACT.Sigmoid))
                    q.tell(T["act1"])
                    act.wait_ge(T["lora1"], 1)
                    for j in range(RJ):
                        q.go(A(sw[:, j, :], ps[:, 0, j * SC:(j + 1) * SC], ACT.Sigmoid, bias=C("w0", j)))
                        q.go(A(aa[:, j, :], ps[:, 1, j * SC:(j + 1) * SC], ACT.Sigmoid, bias=C("a0", j)))
                    q.tell(T["sig1"])
                    q.go(A(gg, b4(2), ACT.Copy))
                    act.wait_ge(T["kk1"], 1)
                    q.go(A(t1, b4(3), ACT.Sqrt))
                    q.tell(T["root1"])
                    act.wait_ge(T["ld_ok"], 1)
                    q.go(A(pin, cum, ACT.Exp))
                    q.go(A(pex, pex, ACT.Exp))
                    q.go(A(piv, cum, ACT.Exp, scale=-1.0))
                    q.tell(T["exp1"])
                    for n, (b, dst) in enumerate(((1, btm), (2, ktm), (4, vtm))):
                        act.wait_ge(T["tm_mm"], n + 1)
                        q.go(A(dst.rearrange("p c j t -> p (c j t)"), ps[:, b, :], ACT.Copy))
                        q.tell(T["tm_ev"])
                    for lv in range(1, LEVELS):
                        act.wait_ge(T["inv_q"], lv)
                        q.go(A(qq.rearrange("p c j t -> p (c j t)"), ps[:, 5, :], ACT.Copy))
                        q.tell(T["inv_qc"])
                    for c in range(2):
                        act.wait_ge(T["rh_mm"], c + 1)
                        q.go(A(rh.rearrange("p j t -> p (j t)"), ps[:, 5, 0:RJ * CH], ACT.Copy))
                        q.tell(T["rh_ev"])
                        act.wait_ge(T["u_mm"], c + 1)
                        q.go(A(uu.rearrange("p j t -> p (j t)"), ps[:, 6, 0:RJ * CH], ACT.Copy))
                        q.tell(T["u_ev"])
                    act.wait_ge(T["ds_mm"], 2)
                    q.go(A(kk, b4(0), ACT.Copy))
                    q.tell(T["y_ev"])
                    act.wait_ge(T["var_v"], 1)
                    q.go(A(t1, t1, ACT.Sqrt))
                    q.tell(T["var_a"])
                    meet(act, "a", T["l_arrive"])

                act.wait_ge(S["vt_mm"], 1)
                for br in range(2):
                    o.go(A(vt[:, br, :, :].rearrange("p t n -> p (t n)"), ps[:, br, :], ACT.Copy))
                o.tell(S["vt_ev"])
                act.wait_ge(S["cmpp_mm"], 1)
                o.do(A(cb, ps[:, 2, 0:2], ACT.Copy))
                for c in range(2):
                    o.go(A(hip[:, c, :], ps[:, 3, c * P:c * P + NCP], ACT.Gelu_apprx_tanh, bias=cb[:, c:c + 1]))
                o.tell(S["gelu_p"])
                act.wait_ge(S["cmpp_mm"], 2)
                o.go(A(kcp, ps[:, 4, 0:NCP], ACT.Copy))
                o.go(A(vcp[0:NCP, :], ps[0:NCP, 5, 0:P], ACT.Copy))
                o.tell(S["kcp_ok"])

                def exps(u):
                    t, i, g = UNITS[u]
                    n, b, s = (t + 1) * P, 2 * (u % 2), u % 2
                    act.wait_ge(S["mx"], u + 1)
                    if u >= 2:
                        act.wait_ge(S["pt_mm"], u - 1)
                    for br in range(2):
                        o.go(A(pp[:, s, br, 0:n], ps[:, b + br, 0:n], ACT.Exp, bias=nm[:, s, br:br + 1], accum_out=sums[:, s, br:br + 1]))
                    o.tell(S["ex"])

                def pt_evac(u):
                    t = UNITS[u][0]
                    act.wait_ge(S["pt_mm"], u + 1)
                    if u >= 2:
                        act.wait_ge(S["pv"], u - 1)
                    o.go(A(ppt[:, u % 2, 0, 0:(t + 1) * P], ps[:, 4, 0:(t + 1) * P], ACT.Copy))
                    o.tell(S["pt_ev_a"])

                for u in range(len(UNITS) + 1):
                    if u < len(UNITS):
                        exps(u)
                    if u >= 1:
                        pt_evac(u - 1)
                    if u < len(UNITS) and u % HEADS == 0:
                        act.wait_ge(S["pc_sub"], u // HEADS + 1)
                        o.go(A(pc, pc, ACT.Exp))
                        o.tell(S["pc_exp"])

                act.wait_ge(S["ss_v"], 1)
                o.go(A(swin[0:ROWS, :], swin[0:ROWS, :], ACT.Exp, bias=sm[0:ROWS, 0:1], accum_out=sm[0:ROWS, 1:2]))
                o.tell(S["ss_a"])
                for u in range(1, CMP_U + 1):
                    act.wait_ge(S["cmp_h"], u)
                    if u >= 2:
                        act.wait_ge(S["cmp_o"], u - 1)
                    for c in range(2):
                        o.go(A(hid[:, c, :, 0:NCS], ps[:, c, 0:2 * NCS].rearrange("p (b n) -> p b n", b=2), ACT.Gelu_apprx_tanh, bias=cb[:, c:c + 1]))
                    o.tell(S["cmp_act"])
                act.wait_ge(S["ss_v"], 4)
                o.go(A(pcs[0:ROWS, 0:NCS], ps[0:ROWS, 0, 0:NCS], ACT.Exp, bias=sm[0:ROWS, 4:5], accum_out=sm[0:ROWS, 5:6]))
                o.tell(S["ss_a"])
                act.wait_ge(S["ss_v"], 8)
                flat = ssel.rearrange("p a b -> p (a b)")
                o.go(A(flat[0:ROWS, 0:PAST + 1], flat[0:ROWS, 0:PAST + 1], ACT.Exp, bias=sm[0:ROWS, 8:9], accum_out=sm[0:ROWS, 9:10]))
                o.tell(S["ss_a"])

                split_w(C_OUT, C_OUT + 1)
                act.wait_ge(S["mixed"], 1)
                for k in range(KB):
                    split_s(hm_hi, hm, k)
                for m in range(KB):
                    split_w(C_OUT + m + 2)
                    evac(hf[:, m, 0:HALF])
                act.wait_ge(S["evac_a"], NT + RP + KB)
                act.wait_ge(S["evac_v"], NT + RP + KB)
                squares(sq2, hf)
                norm_root(2)
                act.wait_ge(S["norm_h"], KB + 1)
                squares(sq2, x)
                norm_root(3)
                for k in range(KB):
                    act.wait_ge(S["norm_h"], KB + 1 + k + 1)
                    split_s(hm_hi, hm, k)
                for m in range(2 * FT):
                    split_w(C_UP + m + 2)
                    i, n = m // 2, n_dense[0]
                    n_dense[0] += 1
                    if m % 2:
                        act.sem_inc(S["evac_a"], 1)
                        continue
                    if i >= 2:
                        act.wait_ge(S["ffn_c"], i - 1)
                        act.wait_ge(S["ffn_t"], i - 1)
                    act.wait_ge(S["w_used"], tile_done(n))
                    for h in range(2):
                        o.go(A(gx[:, i % 2, 2 + h * HALF:2 + (h + 1) * HALF], ps[:, 2 * (n % 3) + h, 0:HALF], ACT.Copy))
                    o.tell(S["evac_a"])
                    act.wait_ge(S["ffn_c"], i + 1)
                    o.go(A(cv[:, i % 2, :], cv[:, i % 2, :], ACT.Gelu_apprx_tanh))
                    o.tell(S["ffn_act"])
                act.wait_ge(S["w_used"], C_DOWN)
                for k in range(FT):
                    act.wait_ge(S["ffn_h"], k + 1)
                    split_s(hf_hi, hf, k)
                for m in range(KB):
                    split_w(*(C_DOWN + 3 * m + i for i in (2, 3, 4)))
                    evac(hm[:, m, 0:HALF])
                act.wait_ge(S["evac_a"], NT + RP + 2 * KB + 2 * FT)
                act.wait_ge(S["evac_v"], NT + RP + 2 * KB + 2 * FT)
                squares(sq2, hm)
                norm_root(4)
                meet(act, "a", S["arrive"])

        @block.gpsimd
        def _(pool):
            o = Order(pool, S["p_own"])
            g = nc.gpsimd
            g.memset(ones[:], 1.0 / D_MODEL).then_inc(p_const, 1)
            pool.wait_ge(p_const, 1)
            pool.sem_inc(ones_ok, 1)
            pool.wait_ge(const_ok, 48)
            with pool.Fori(0, DEPTH) as _l:
                o.n = 0
                with pool.Fori(0, SEQ // SC) as _sc:
                    q = Order(pool, T["lp"])
                    pool.wait_ge(T["gmask"], 2)
                    for lv in range(1, LEVELS):
                        lo = CONST["lev"][0] + lv * CH
                        m = cst[:, lo:lo + CH].unsqueeze(1).to_broadcast((P, RJ, CH))
                        for c in range(2):
                            q.go(g.tensor_tensor(mm[:, lv - 1, c * RJ:(c + 1) * RJ, :], gb[:, c, :, 0, :], m, ALU.mult))
                        q.tell(T["mm_ok"])
                    meet(pool, "p", T["l_arrive"])
                o.go(g.memset(w1, 0.0))
                o.go(g.memset(w2, 0.0))
                o.tell(S["w1_zero"])
                for i in range(FT):
                    pool.wait_ge(S["evac_a"], NT + RP + KB + 2 * i + 1)
                    if i == 0:
                        pool.wait_ge(S["loads_s"], 32)
                    o.go(g.tensor_copy(cout[:, i, :], gx[:, i % 2, SEQ:SEQ + 2]))
                    o.go(g.tensor_copy(couts[:, i, 0, :], cprev[:, i, 1, :]))
                    o.go(g.tensor_copy(couts[:, i, 1, :], gx[:, i % 2, 2 + SEQ:2 + TOK]))
                    o.tell(S["ffn_t"])
                meet(pool, "p", S["arrive"])

        @block.vector
        def _(dve):
            o = Order(dve, S["v_own"])
            v = nc.vector
            MUL, ADD, SUB, MAX = ALU.mult, ALU.add, ALU.subtract, ALU.max
            LD = -math.exp(-0.5)
            dve.wait_ge(const_ok, 48)
            o.do(v.tensor_scalar(onesblk[:], blk, 1.0 / HD, None, MUL))
            with dve.Fori(0, DEPTH) as _l:
                dve.sem_clear(S["v_own"])
                o.n = 0
                n_dense = [0]

                def norm_inv(n):
                    dve.wait_ge(S["norm_mm"], n)
                    o.do(v.tensor_scalar(rstd[:], bank2(6), EPS, None, ADD))
                    o.do(v.reciprocal(rstd[:], rstd[:]))
                    o.tell(S["norm_v"])
                    dve.wait_ge(S["norm_a"], n)

                rs = rstd[:].rearrange("p h n -> p (h n)")

                def evac(dst):
                    n = n_dense[0]
                    dve.wait_ge(S["w_used"], tile_done(n))
                    v.tensor_copy(dst, ps[:, 2 * (n % 3) + 1, 0:HALF]).then_inc(S["evac_v"], 1)
                    n_dense[0] += 1

                n_split = [0, 0]

                def split_w(*chunks):
                    for n in chunks:
                        if n != C_GATE and n < N_CHUNK:
                            n_split[0] += 1
                            dve.wait_ge(S["w_hi"], n_split[0])
                            r = ring[:, n % RING, :]
                            v.tensor_tensor(ring_lo[:, n % RING, :], r, ring_hi[:, n % RING_HI, :], SUB).then_inc(S["w_lo"], 1)

                def split_s(dst, src, hi, blocks):
                    for k in range(blocks):
                        n_split[1] += 1
                        dve.wait_ge(S["s_hi"], n_split[1])
                        v.tensor_tensor(dst[:, k, :], src[:, k, :], hi[:, k, :], SUB).then_inc(S["s_lo"], 1)

                dve.wait_ge(S["params"], 48)
                split_w(0, 1)
                norm_inv(1)
                for k in range(KB):
                    v.scalar_tensor_tensor(hm[:, k, :], x[:, k, :], C("mix_pre", k), rs, MUL, MUL).then_inc(S["norm_h"], 1)
                split_s(hm_lo, hm, hm_hi, KB)
                o.go(v.memset(pr[:, :, 0:1], 0.0))
                o.go(v.memset(state[:], 0.0))
                for m in range(NT + RP):
                    if m + 2 < C_GATE:
                        split_w(m + 2)
                    evac(nsa[:, m, HALF:TOK] if m < NT else pr[:, m - NT, 1 + HALF:1 + TOK])

                def mix(q, n, cur, prev):
                    q.do(v.tensor_tensor(dif[:, :, 0:n], prev, cur, SUB))
                    q.do(v.tensor_tensor(dif[:, :, 0:n], dif[:, :, 0:n], wide(C("mu"), n), MUL))
                    q.do(v.tensor_tensor(xs[:, :, 0:n], dif[:, :, 0:n], cur, ADD))

                def key_squares(q, n):
                    q.do(v.tensor_tensor(kk[:, :, 0:n], xs[:, RJ:2 * RJ, 0:n], wide(C("k_k"), n), MUL))
                    q.do(v.tensor_tensor(t0[:, :, 0:n], kk[:, :, 0:n], kk[:, :, 0:n], MUL))

                def keys(q, n, b_out):
                    q.do(v.tensor_scalar(t1[:, :, 0:n], t1[:, :, 0:n], 1e-12, None, MAX))
                    q.do(v.reciprocal(t1[:, :, 0:n], t1[:, :, 0:n]))
                    q.do(v.tensor_tensor(kk[:, :, 0:n], kk[:, :, 0:n], t1[:, :, 0:n], MUL))
                    q.do(v.scalar_tensor_tensor(t0[:, :, 0:n], aa[:, :, 0:n], -1.0, wide(C("k_a"), n), ADD, MUL))
                    q.do(v.scalar_tensor_tensor(km[:, :, 0:n], t0[:, :, 0:n], 1.0, xs[:, RJ:2 * RJ, 0:n], ADD, MUL))
                    q.go(v.tensor_tensor(b_out, kk[:, :, 0:n], aa[:, :, 0:n], MUL))
                    q.do(v.tensor_tensor(t1[:, :, 0:n], xs[:, 0:RJ, 0:n], km[:, :, 0:n], MUL))
                    q.do(v.tensor_tensor(t1[:, :, 0:n], t1[:, :, 0:n], wide(C("r_k"), n), MUL))

                def finish(q, n, rkv, dst):
                    q.do(v.tensor_tensor(kk[:, :, 0:n], kk[:, :, 0:n], t1[:, :, 0:n], MUL))
                    q.do(v.tensor_tensor(kk[:, :, 0:n], kk[:, :, 0:n], wide(C("lnw"), n), MUL))
                    q.do(v.tensor_tensor(kk[:, :, 0:n], kk[:, :, 0:n], wide(C("lnb"), n), ADD))
                    q.do(v.tensor_tensor(t0[:, :, 0:n], rkv, xs[:, 2 * RJ:3 * RJ, 0:n], MUL))
                    q.do(v.tensor_tensor(kk[:, :, 0:n], kk[:, :, 0:n], t0[:, :, 0:n], ADD))
                    q.do(v.tensor_tensor(dst, kk[:, :, 0:n], gg[:, :, 0:n], MUL))

                dve.wait_ge(S["evac_a"], NT + RP)
                dve.wait_ge(S["evac_v"], NT + RP)
                mix(o, DEC, pr[:, :, 1 + SEQ:1 + TOK], prev_s)
                key_squares(o, DEC)
                o.tell(S["rs_x"])
                dve.wait_ge(S["rs_act"], 2)
                bs = cum[:, :, 0:DEC]
                keys(o, DEC, bs)
                o.do(v.tensor_scalar(pex[:, :, 0:DEC], kk[:, :, 0:DEC], -1.0, None, MUL))
                o.tell(S["rs_prep"])
                rks = dif[:, 0:RJ, 0:DEC]
                over = lambda a: a.unsqueeze(3).to_broadcast((P, RJ, DEC, CH))
                b47 = ps[:, 4:8, :].rearrange("p j (b n) -> p j b n", b=DEC)
                dve.wait_ge(S["rs_mm"], 2)
                dve.wait_ge(S["loads_s"], 16)
                o.go(v.tensor_copy(rks, b4(3, DEC)))
                o.go(v.tensor_tensor(s1, b47, over(bs), MUL))
                o.tell(S["rs_prep"])
                dve.wait_ge(S["rs_mm"], 3)
                o.go(v.tensor_tensor(s2, b47, over(km[:, :, 0:DEC]), MUL))
                o.tell(S["rs_prep"])
                o.do(v.tensor_tensor(ss, ss, over(pin[:, :, 0:DEC]), MUL))
                o.do(v.tensor_tensor(ss, ss, s1, ADD))
                o.do(v.tensor_tensor(ss, ss, s2, ADD))
                o.tell(S["rs_prep"])
                dve.wait_ge(S["rs_mm"], 4)
                o.go(v.tensor_copy(kk[:, :, 0:DEC], b4(0, DEC)))
                o.tell(S["rs_prep"])
                dve.wait_ge(S["rs_mm"], 5)
                o.do(v.tensor_tensor(kk[:, :, 0:DEC], kk[:, :, 0:DEC], b4(1, DEC), SUB))
                o.do(v.tensor_tensor(t0[:, :, 0:DEC], kk[:, :, 0:DEC], kk[:, :, 0:DEC], MUL))
                o.tell(S["rs_prep"])
                dve.wait_ge(S["rs_mm"], 6)
                o.do(v.tensor_scalar(t1[:, :, 0:DEC], b4(1, DEC), LNX_EPS, None, ADD))
                o.do(v.reciprocal(t1[:, :, 0:DEC], t1[:, :, 0:DEC]))
                o.tell(S["rs_var"])
                dve.wait_ge(S["rs_act"], 3)
                finish(o, DEC, rks, hm[:, RJ:2 * RJ, SEQ:TOK])
                o.tell(S["rs_out"])
                dve.wait_ge(S["stores"], 32)

                with dve.Fori(0, SEQ // SC) as sc:
                    q = Order(dve, T["lv"])
                    mix(q, SC, pr[:, :, bass.ds(sc * SC + 1, SC)], pr[:, :, bass.ds(sc * SC, SC)])
                    q.tell(T["x1"])
                    key_squares(q, SC)
                    q.tell(T["x1"])
                    dve.wait_ge(T["sig1"], 1)
                    flat = lambda a: a.rearrange("p j t -> p (j t)")
                    q.do(v.tensor_scalar(sw, sw, LD, None, MUL))
                    q.do(v.tensor_tensor_scan(flat(cum), K("scan"), flat(sw), 0.0, MUL, ADD))
                    q.do(v.tensor_tensor(pex, cum, sw, SUB))
                    q.tell(T["ld_ok"])
                    dve.wait_ge(T["root1"], 1)
                    bb = sw
                    keys(q, SC, bb)
                    q.tell(T["prep"])
                    dve.wait_ge(T["exp1"], 1)
                    in2 = lambda a: a.rearrange("p j (c t) -> p j c t", c=2)
                    q.go(v.scalar_tensor_tensor(ar[:, :, :, 0, :], in2(kk), -1.0, in2(pex), MUL, MUL))
                    q.go(v.tensor_tensor(ar[:, :, :, 1, :], in2(xs[:, 0:RJ, :]), in2(pin), MUL))
                    q.go(v.tensor_tensor(bt, bb, piv, MUL))
                    q.go(v.tensor_tensor(kt, km, piv, MUL))
                    q.tell(T["prep"])
                    dve.wait_ge(T["kk1"], 2)
                    q.go(v.tensor_copy(rk, b4(3)))
                    gm = K("gmask").unsqueeze(1).to_broadcast((P, RJ, P))
                    for c in range(2):
                        dve.wait_ge(T["gmm"], c + 1)
                        for n, dst in ((4, gb), (5, gk)):
                            q.go(v.tensor_tensor(dst[:, c, :, :, :].rearrange("p j a t -> p j (a t)"), b4(n + 2 * c), gm, MUL))
                        q.tell(T["gmask"])
                    lo = CONST["lev"][0]
                    lev0 = cst[:, lo:lo + CH].unsqueeze(1).to_broadcast((P, RJ, CH))
                    eye8 = eye.unsqueeze(1).to_broadcast((P, 2 * RJ, CH))
                    z8, w8 = (a.rearrange("p c j t -> p (c j) t") for a in (zz, ww))
                    bank8 = lambda b: ps[:, b, :].rearrange("p (a t) -> p a t", t=CH)
                    for c in range(2):
                        q.go(v.tensor_tensor(zz[:, c, :, :], gb[:, c, :, 0, :], lev0, MUL))
                    dve.wait_ge(T["nmm"], 1)
                    q.do(v.tensor_tensor(w8, bank8(0), K("lev0t").unsqueeze(1).to_broadcast((P, 2 * RJ, CH)), MUL))
                    q.go(v.tensor_tensor(z8, z8, eye8, ADD))
                    q.go(v.tensor_tensor(w8, w8, eye8, ADD))
                    q.tell(T["inv_z"])
                    for lv in range(1, LEVELS):
                        dve.wait_ge(T["inv_d"], lv)
                        q.go(v.tensor_tensor(z8, z8, bank8(6), ADD))
                        if lv < LEVELS - 1:
                            q.go(v.tensor_tensor(w8, w8, bank8(7), ADD))
                        q.tell(T["inv_z"])
                    for c in range(2):
                        dve.wait_ge(T["ds_mm"], c + 1)
                        q.do(v.tensor_tensor(state[:], state[:], b4(7, CH), ADD))
                        e = c * CH + CH - 1
                        q.do(v.tensor_tensor(state[:], state[:], pin[:, :, e:e + 1].to_broadcast((P, RJ, CH)), MUL))
                        q.tell(T["s_ok"])
                    dve.wait_ge(T["mean_mm"], 1)
                    q.do(v.tensor_tensor(kk, kk, b4(1), SUB))
                    q.do(v.tensor_tensor(t0, kk, kk, MUL))
                    q.tell(T["yc"])
                    dve.wait_ge(T["var_mm"], 1)
                    q.do(v.tensor_scalar(t1, b4(2), LNX_EPS, None, ADD))
                    q.do(v.reciprocal(t1, t1))
                    q.tell(T["var_v"])
                    dve.wait_ge(T["var_a"], 1)
                    finish(q, SC, rk, hm[:, RJ:2 * RJ, bass.ds(sc * SC, SC)])
                    meet(dve, "v", T["l_arrive"])

                dve.wait_ge(S["trig_ok"], 16)
                for n, tile in enumerate((0, 1, 2, 3, 4, 6, 8)):
                    scale = HD ** -0.5 if tile < 4 else 1.0
                    o.go(v.scalar_tensor_tensor(tr, nsa[:, tile, :], scale, trig[:, 0, :], MUL, MUL))
                    dve.wait_ge(S["rope_mm"], n + 1)
                    o.do(v.scalar_tensor_tensor(halves(tr2), bank2(0), scale, halves(trig[:, 1, :]), MUL, MUL))
                    o.do(v.tensor_tensor(nsa[:, tile, :], tr, tr2, ADD))
                    o.tell(S["rope_ok"])
                o.tell(S["nsa_ready"])

                def maxima(u):
                    t, n, b, s = UNITS[u][0], (UNITS[u][0] + 1) * P, 2 * (u % 2), u % 2
                    dve.wait_ge(S["sc_mm"], u + 1)
                    d = ps[:, b:b + 2, t * P:(t + 1) * P]
                    o.do(v.tensor_tensor(d, d, K("causal").unsqueeze(1).to_broadcast((P, 2, P)), ADD))
                    o.go(v.tensor_reduce(nm[:, s, :], ps[:, b:b + 2, 0:n], AX, MAX, negate=True))
                    o.tell(S["mx"])

                def normalise(u):
                    t, i, g = UNITS[u]
                    h, s, n = g * PER + i, u % 2, (t + 1) * P
                    dve.wait_ge(S["ex"], u + 1)
                    o.do(v.tensor_scalar(sums[:, s, :], sums[:, s, :], 1e-30, None, MAX))
                    o.do(v.reciprocal(rr[:, s, :], sums[:, s, :]))
                    o.do(v.tensor_tensor(rr[:, s, :], rr[:, s, :], gates[:, t, 3 * h + 1:3 * h + 3], MUL))
                    o.go(v.tensor_tensor(pp[:, s, :, 0:n], pp[:, s, :, 0:n], wide(rr[:, s, :], n), MUL))
                    o.tell(S["sc_v"])

                def pt_evac(u):
                    t = UNITS[u][0]
                    dve.wait_ge(S["pt_mm"], u + 1)
                    if u >= 2:
                        dve.wait_ge(S["pv"], u - 1)
                    o.go(v.tensor_copy(ppt[:, u % 2, 1, 0:(t + 1) * P], ps[:, 5, 0:(t + 1) * P]))
                    o.tell(S["pt_ev_v"])
                    if u % HEADS == HEADS - 1:
                        dve.wait_ge(S["pv"], u + 1)
                        o.go(v.tensor_copy(hm[:, 0:PER, t * P:(t + 1) * P], b4(6)))
                        o.tell(S["o_ev"])

                def compressed(t):
                    dve.wait_ge(S["at_mm"], 4 * t + 2)
                    lo = CONST["cmask"][0] + t * NCP
                    mask = cst[:, lo:lo + NCP].unsqueeze(1).to_broadcast((P, HEADS, NCP))
                    o.do(v.tensor_tensor(pc, ps[:, 7, 0:HEADS * NCP].rearrange("p (h n) -> p h n", h=HEADS), mask, ADD))
                    o.do(v.tensor_reduce(cm[:, 0, :], pc, AX, MAX))
                    o.do(v.tensor_scalar(cm[:, 0, :], cm[:, 0, :], NEG / 10, None, MAX))
                    o.do(v.tensor_tensor(pc, pc, wide(cm[:, 0, :], NCP), SUB))
                    o.tell(S["pc_sub"])
                    dve.wait_ge(S["pc_exp"], t + 1)
                    o.do(v.tensor_reduce(cm[:, 1, :], pc, AX, ADD))
                    o.do(v.tensor_scalar(cm[:, 1, :], cm[:, 1, :], 1e-30, None, MAX))
                    o.do(v.reciprocal(cm[:, 2, :], cm[:, 1, :]))
                    o.do(v.tensor_tensor(cm[:, 2, :], cm[:, 2, :], gates[:, t, 0:24:3], MUL))
                    o.do(v.tensor_tensor(pc, pc, wide(cm[:, 2, :], NCP), MUL))
                    o.tell(S["pc_ok"])
                    for half in range(2):
                        dve.wait_ge(S["at_mm"], 4 * t + 3 + half)
                        o.go(v.tensor_copy(pcp[0:NCP, 4 * half:4 * half + 4, :], ps[0:NCP, 7, :].rearrange("p (h n) -> p h n", h=4)))
                        o.tell(S["pcp_ok"])

                dve.wait_ge(S["gate_ev"], NQ + 1)
                for u in range(len(UNITS) + 1):
                    if u < len(UNITS):
                        maxima(u)
                    if u >= 1:
                        pt_evac(u - 1)
                    if u < len(UNITS):
                        if u % HEADS == 0:
                            compressed(u // HEADS)
                        normalise(u)

                o.do(v.memset(qpad, 0.0))
                qflat = qpad.rearrange("p b n -> p (b n)")
                for i in range(PER):
                    for g in range(GROUPS):
                        r = slice(g * HD, (g + 1) * HD)
                        h = g * PER + i
                        step = ROWS + HEADS
                        o.go(v.tensor_copy(qflat[r, h:h + step * (DEC - 1) + 1:step], nsa[r, i, SEQ:TOK]))
                o.tell(S["qpad_ok"])
                R = slice(0, ROWS)
                dve.wait_ge(S["gs_ready"], 16)

                def weigh(p, den, col, gate):
                    o.do(v.tensor_scalar(sm[R, den:den + 1], sm[R, den:den + 1], 1e-30, None, MAX))
                    o.do(v.reciprocal(sm[R, col:col + 1], sm[R, den:den + 1]))
                    if gate is not None:
                        o.do(v.tensor_tensor(sm[R, col:col + 1], sm[R, col:col + 1], gate_s[:, gate:gate + 1], MUL))
                    o.do(v.tensor_scalar(p, p, sm[R, col:col + 1], None, MUL))

                dve.wait_ge(S["ss_mm"], 1)
                o.go(v.tensor_copy(swin[R, 1:WIN], ps[R, 0, 1:WIN]))
                o.go(v.tensor_copy(swin[R, 0:1], ps[R, 1, 0:1]))
                o.go(v.tensor_copy(vnew[0:DEC, :, :], ps[0:DEC, 2, 0:2 * P].rearrange("p (a n) -> p a n", a=2)))
                o.settle()
                o.go(v.tensor_reduce(sm[R, 0:1], swin[R, :], AX, MAX, negate=True))
                o.tell(S["ss_v"])
                dve.wait_ge(S["ss_a"], 1)
                weigh(swin[R, :], 1, 2, 2)
                o.do(v.tensor_scalar(diag[R, 1, :], ident[R, 0:ROWS], swin[R, 0:1], None, MUL))
                o.go(v.memset(swin[R, 0:1], 0.0))
                o.tell(S["ss_v"])
                dve.wait_ge(S["ss_mm"], 2)
                o.go(v.tensor_copy(ptw.rearrange("p k n -> p (k n)"), ps[:, 3, 0:4 * ROWS]))
                o.go(v.tensor_copy(pnew[0:DEC, 1, :], ps[0:DEC, 4, 0:ROWS]))
                o.tell(S["ss_v"])
                for u in range(1, CMP_U + 1):
                    dve.wait_ge(S["cmp_o"], u)
                    b = 2 * (u - 1)
                    o.go(v.tensor_copy(kcs[:, b:b + 2, :], ps[:, 2, 0:2 * NCS].rearrange("p (b n) -> p b n", b=2)))
                    o.go(v.tensor_copy(vcs[0:NCS, b:b + 2, :], ps[0:NCS, 3, 0:2 * P].rearrange("p (b n) -> p b n", b=2)))
                    o.tell(S["cmp_k"])
                dve.wait_ge(S["ss_mm"], 3)
                o.go(v.tensor_reduce(sm[R, 4:5], ps[R, 0, 0:NCS], AX, MAX, negate=True))
                o.tell(S["ss_v"])
                dve.wait_ge(S["ss_a"], 2)
                weigh(pcs[R, 0:NCS], 5, 6, None)
                o.tell(S["ss_v"])
                dve.wait_ge(S["ss_mm"], 4)
                o.go(v.tensor_copy(impt[0:NCS, :], ps[0:NCS, 1, 0:ROWS]))
                o.go(v.tensor_scalar(pcs[R, 0:NCS], pcs[R, 0:NCS], gate_s[:, 0:1], None, MUL))
                o.tell(S["ss_v"])
                dve.wait_ge(S["ss_mm"], 5)
                o.go(v.tensor_copy(pct[0:NCS, :], ps[0:NCS, 3, 0:ROWS]))
                o.do(v.tensor_tensor(work[R, :], ps[R, 2, 0:NSEL], K("keep", ROWS), MUL))
                o.tell(S["ss_v"])
                o.do(v.tensor_tensor(work[R, :], work[R, :], K("force", ROWS), ADD))
                for _ in range(2):
                    o.do(v.max(top[R, :], work[R, :]))
                    o.do(v.match_replace(work[R, :], top[R, :], work[R, :], 2 * NEG))
                o.do(v.tensor_scalar(imp[R, :], work[R, :], 1.5 * NEG, NEG, ALU.is_ge, MUL))
                dve.wait_ge(S["ss_mm"], 6)
                for k in range(4):
                    bias = imp[R, 8 * k:8 * k + 8].unsqueeze(2).to_broadcast((ROWS, 8, SELB))
                    o.go(v.tensor_tensor(ssel[R, 8 * k:8 * k + 8, :], ps[R, k, :].rearrange("p (a b) -> p a b", b=SELB), bias, ADD))
                fs = ssel.rearrange("p a b -> p (a b)")
                o.do(v.tensor_tensor(fs[R, PAST:PAST + 1], ps[R, 4, 0:1], imp[R, NSEL - 1:NSEL], ADD))
                o.do(v.tensor_reduce(sm[R, 8:9], fs[R, 0:PAST + 1], AX, MAX, negate=True))
                o.tell(S["ss_v"])
                dve.wait_ge(S["ss_a"], 3)
                weigh(fs[R, 0:PAST + 1], 9, 10, 1)
                o.do(v.tensor_scalar(diag[R, 0, :], ident[R, 0:ROWS], fs[R, PAST:PAST + 1], None, MUL))
                o.tell(S["ss_v"])
                dve.wait_ge(S["ss_mm"], 7)
                o.go(v.tensor_copy(pt_s.rearrange("p (a k) n -> p a (k n)", a=2), ps[:, 0:2, :]))
                o.go(v.tensor_copy(pnew[0:DEC, 0, :], ps[0:DEC, 2, 0:ROWS]))
                o.tell(S["ss_v"])
                dve.wait_ge(S["ss_mm"], 8)
                for g in range(GROUPS):
                    r = slice(g * HD, (g + 1) * HD)
                    src = ps[r, 7, 0:ROWS].rearrange("p (b h) -> p h b", h=HEADS)[:, g * PER:(g + 1) * PER, :]
                    o.go(v.tensor_copy(hm[r, 0:PER, SEQ:TOK], src))
                o.tell(S["mixed"])

                split_w(C_OUT, C_OUT + 1)
                split_s(hm_lo, hm, hm_hi, KB)
                for m in range(KB):
                    split_w(C_OUT + m + 2)
                    evac(hf[:, m, HALF:TOK])

                def add_normed(src, g):
                    for k in range(KB):
                        o.go(v.scalar_tensor_tensor(src[:, k, :], src[:, k, :], C(g, k), rs, MUL, MUL))
                    o.settle()
                    for k in range(KB):
                        o.go(v.tensor_tensor(x[:, k, :], x[:, k, :], src[:, k, :], ADD))
                    o.settle()

                norm_inv(2)
                add_normed(hf, "mix_post")
                o.tell(S["norm_h"])
                norm_inv(3)
                for k in range(KB):
                    v.scalar_tensor_tensor(hm[:, k, :], x[:, k, :], C("ffn_pre", k), rs, MUL, MUL).then_inc(S["norm_h"], 1)
                split_s(hm_lo, hm, hm_hi, KB)
                o.do(v.memset(gx[:, :, 0:2], 0.0))
                dve.wait_ge(S["loads_s"], 32)

                def conv(i):
                    s = i % 2
                    n = NT + RP + KB + 2 * i + 1
                    dve.wait_ge(S["evac_a"], n)
                    if i >= 2:
                        dve.wait_ge(S["ffn_h"], i - 1)
                    p_, s_ = cv[:, s, 0:SEQ], cv[:, s, SEQ:TOK]
                    o.go(v.tensor_scalar(p_, gx[:, s, 0:SEQ], C("cw0", i), C("cb", i), MUL, ADD))
                    o.do(v.tensor_scalar(s_, cprev[:, i, 0, :], C("cw0", i), C("cb", i), MUL, ADD))
                    o.go(v.scalar_tensor_tensor(p_, gx[:, s, 1:1 + SEQ], C("cw1", i), p_, MUL, ADD))
                    o.do(v.scalar_tensor_tensor(s_, cprev[:, i, 1, :], C("cw1", i), s_, MUL, ADD))
                    o.go(v.scalar_tensor_tensor(cv[:, s, :], gx[:, s, 2:2 + TOK], C("cw2", i), cv[:, s, :], MUL, ADD))
                    o.tell(S["ffn_c"])

                for i in range(FT):
                    split_w(C_UP + 2 * i + 2)
                    dve.sem_inc(S["evac_v"], 1)
                    conv(i)
                    n_dense[0] += 1
                    n = n_dense[0]
                    split_w(C_UP + 2 * i + 3)
                    dve.wait_ge(S["w_used"], tile_done(n))
                    dve.wait_ge(S["ffn_act"], i + 1)
                    o.do(v.tensor_tensor(halves(hf[:, i, :]), halves(cv[:, i % 2, :]), bank2(2 * (n % 3)), MUL))
                    dve.sem_inc(S["evac_v"], 1)
                    dve.sem_inc(S["ffn_h"], 1)
                    n_dense[0] += 1
                split_s(hf_lo, hf, hf_hi, FT)
                for m in range(KB):
                    split_w(*(C_DOWN + 3 * m + i for i in (2, 3, 4)))
                    evac(hm[:, m, HALF:TOK])
                norm_inv(4)
                add_normed(hm, "ffn_post")
                meet(dve, "v", S["arrive"])


HEAD_ORDER = [g * PER + i for i in range(PER) for g in range(GROUPS)]


def tiles(a):
    return np.swapaxes(a.reshape(a.shape[:-1] + (-1, P)), -1, -2)


def weight_chunks(w_in, w_out, w_up, w_down):
    q_cols = np.concatenate([np.arange(h * HD, (h + 1) * HD) for h in HEAD_ORDER])
    nsa_w = HEADS * HD
    kv_w = 6 * P
    out = np.zeros((DEPTH, N_CHUNK, P, KB, P), w_in.dtype)

    def put(at, w):
        k, m = w.shape[1] // P, w.shape[2] // P
        t = w.reshape(DEPTH, k, P, m, P).transpose(0, 3, 2, 1, 4)
        for i in range(m):
            for c in range(-(-k // KB)):
                part = t[:, i, :, c * KB:(c + 1) * KB]
                out[:, at, :, 0:part.shape[2]] = part
                at += 1
        return at

    wq = w_in[:, :, q_cols]
    rest = w_in[:, :, nsa_w:nsa_w + kv_w]
    gate = w_in[:, :, nsa_w + kv_w:nsa_w + kv_w + 24]
    n = put(0, np.concatenate([wq, rest, w_in[:, :, nsa_w + kv_w + 24:]], 2))
    flat = out.reshape(DEPTH, N_CHUNK, P, KB * P)
    flat[:, n, :, 0:KB * 24] = gate.reshape(DEPTH, KB, P, 24).transpose(0, 2, 1, 3).reshape(DEPTH, P, KB * 24)
    n = put(n + 1, np.concatenate([w_out[:, q_cols], w_out[:, nsa_w:]], 1))
    up = np.stack([w_up[:, :, 0:FF].reshape(DEPTH, D_MODEL, FT, P), w_up[:, :, FF:].reshape(DEPTH, D_MODEL, FT, P)], 3)
    n = put(n, up.reshape(DEPTH, D_MODEL, 2 * FF))
    n = put(n, w_down)
    assert n == N_CHUNK
    return flat


OUTS = {
    "y": (KB, P, TOK), "kv": (DEPTH, P, 6 * TOK), "win_old": (DEPTH, DEC, (WIN - 1) * 2 * P),
    "wkv_p": (DEPTH, P, RJ * CH), "wkv_s": (DEPTH, P, RJ * DEC * CH), "shift": (DEPTH, P, RP * (1 + DEC)),
    "conv_p": (DEPTH, P, FT * 2), "conv_s": (DEPTH, P, FT * 2 * DEC),
}


def kernel(x_prompt, x_sample, cache_kv, page_table, state_win, state_wkv, state_shift, state_conv,
           norm_mix_pre, norm_mix_post, norm_ffn_pre, norm_ffn_post, w_in, w_out,
           cmp_pe, cmp_w1, cmp_w2, rwkv_mu, rwkv_w0, rwkv_w_up, rwkv_a0, rwkv_a_up, rwkv_g_up,
           rwkv_k_k, rwkv_k_a, rwkv_r_k, rwkv_lnx_w, rwkv_lnx_b,
           ffn_w_up, ffn_conv_w, ffn_conv_b, ffn_w_down):
    import concourse.bacc as bacc
    from concourse.bass_utils import run_bass_kernel_spmd

    arr = lambda a: np.asarray(a)
    xp, xs = arr(x_prompt)[0], arr(x_sample)[:, 0]
    cache = arr(cache_kv).reshape(DEPTH * N_POOL, PAGE, 4, P)
    win = arr(state_win)
    fm = cache.transpose(0, 3, 2, 1)
    conv_w = arr(ffn_conv_w)
    lora = np.concatenate([np.concatenate([arr(rwkv_w_up), arr(rwkv_a_up)], 1), arr(rwkv_g_up)], 2)
    wkv = arr(state_wkv).reshape(DEPTH, DEC, RJ, 2, HD, HD)
    cols = {"mix_pre": norm_mix_pre, "mix_post": norm_mix_post, "ffn_pre": norm_ffn_pre, "ffn_post": norm_ffn_post,
            "mu": rwkv_mu, "w0": rwkv_w0, "a0": rwkv_a0, "k_k": rwkv_k_k, "k_a": rwkv_k_a,
            "r_k": arr(rwkv_r_k).reshape(DEPTH, RW), "lnw": rwkv_lnx_w, "lnb": rwkv_lnx_b,
            "cw0": conv_w[:, 0], "cw1": conv_w[:, 1], "cw2": conv_w[:, 2], "cb": ffn_conv_b}
    inputs = {
        "consts": constants()[0],
        "trig": constants()[1],
        "pages": arr(page_table).reshape(1, -1),
        "x": np.concatenate([xp, xs], 0).T.reshape(KB, P, TOK),
        "cols": np.concatenate([tiles(arr(cols[n])) for n in COLS], 2),
        "shift": arr(state_shift).reshape(DEPTH, DEC, RP, P).transpose(0, 3, 2, 1).reshape(DEPTH, P, -1),
        "lora": lora,
        "w": weight_chunks(arr(w_in), arr(w_out), arr(ffn_w_up), arr(ffn_w_down)),
        "wkv": wkv.transpose(0, 3, 5, 2, 1, 4).reshape(DEPTH, P, -1),
        "w1": arr(cmp_w1).transpose(0, 1, 3, 2, 4).reshape(DEPTH, 2, HD, -1),
        "w2": arr(cmp_w2),
        "pe": arr(cmp_pe).transpose(0, 1, 3, 2),
        "win": win[:, :, 1:].reshape(DEPTH, DEC, -1),
        "kwin": win[:, :, :, 0].reshape(DEPTH, DEC, WIN, P).transpose(0, 1, 3, 2),
        "vwin": win[:, :, :, 1].reshape(DEPTH, DEC, 4, P, P).transpose(0, 1, 3, 2, 4).reshape(DEPTH, DEC, P, WIN),
        "kv_cmp": fm[:, :, 0:2].reshape(DEPTH * N_POOL, P, 2 * PAGE),
        "k_sel": fm[:, :, 2],
        "v_sel": cache[:, :, 3],
        "conv": arr(state_conv).reshape(DEPTH, DEC, 2, FT, P).transpose(0, 4, 3, 2, 1).reshape(DEPTH, P, -1),
    }
    nc = bacc.Bacc("TRN2", target_bir_lowering=False, num_devices=1)
    arrays, I, O = {}, {}, {}
    for name, a in inputs.items():
        a = np.ascontiguousarray(a)
        arrays["in_" + name] = a
        I[name] = nc.dram_tensor("in_" + name, a.shape, mybir.dt.from_np(a.dtype), kind="ExternalInput").ap()
    for name, shape in OUTS.items():
        O[name] = nc.dram_tensor("out_" + name, shape, F32, kind="ExternalOutput").ap()
    build(nc, I, O)
    res = run_bass_kernel_spmd(nc, [arrays], core_ids=[0]).results[0]
    r = {n: np.asarray(res["out_" + n]) for n in OUTS}

    y = r["y"].reshape(D_MODEL, TOK).T
    kv = r["kv"].reshape(DEPTH, GROUPS, HD, 6, TOK).transpose(0, 4, 3, 1, 2)
    win_new = np.concatenate([r["win_old"].reshape(DEPTH, DEC, WIN - 1, 2, GROUPS, HD), kv[:, SEQ:, None, 4:6]], 2)
    back = lambda a: a.reshape(DEPTH, 2, HD, RJ, -1, HD).transpose(0, 4, 3, 1, 5, 2).reshape(DEPTH, -1, HEADS, HD, HD)
    shift = r["shift"].reshape(DEPTH, P, RP, 1 + DEC).transpose(0, 3, 2, 1).reshape(DEPTH, 1 + DEC, RP * P)
    conv_p = r["conv_p"].reshape(DEPTH, P, FT, 2).transpose(0, 3, 2, 1).reshape(DEPTH, 1, 2, FF)
    conv_s = r["conv_s"].reshape(DEPTH, P, FT, 2, DEC).transpose(0, 4, 3, 2, 1).reshape(DEPTH, DEC, 2, FF)
    outs = (y[None, 0:SEQ], y[SEQ:, None], kv[:, None, 0:SEQ, 0:4], kv[:, SEQ:, None, 0:4],
            kv[:, None, 0:SEQ, 4:6], win_new, back(r["wkv_p"]), back(r["wkv_s"]),
            shift[:, 0:1], shift[:, 1:], conv_p, conv_s)
    return tuple(np.ascontiguousarray(a) for a in outs)
```

```python
from contextlib import ExitStack
import math

import numpy as np
import concourse.bass as bass
from concourse import mybir

F32 = mybir.dt.float32
F32R = mybir.dt.float32r
I32 = mybir.dt.int32
ALU = mybir.AluOpType
ACT = mybir.ActivationFunctionType
AX = mybir.AxisListType.X

P = 128
D_MODEL, SEQ, DEPTH, DEC, PAST, PAGE = 1024, 512, 2, 8, 2048, 128
HD, HEADS, GROUPS = 64, 8, 2
PER = HEADS // GROUPS
TOK = SEQ + DEC
HALF = TOK // 2
KB = D_MODEL // P
PAGES = PAST // PAGE
N_POOL = (DEC * PAGES) + (DEC * PAGES) // 4
STRIDE, BLOCK = 16, 32
NCP = SEQ // STRIDE - 1
NCS = (PAST + 1) // STRIDE - 1
SELB = 64
NSEL = -(-(PAST + 1) // SELB)
WIN = 512
ROPE, THETA = HD // 4, 500000.0
RW = 512
RJ = RW // P
RP = 3 * RJ + 2
FF = 2816
FT = FF // P
NT = 10
CH = 64
SC = 128
NQ = SEQ // P
NEG = -1e30
ROWS = DEC * HEADS
EPS, LNX_EPS = 1e-6, 64e-5

C_IN, C_GATE = 0, NT + RP
C_OUT = C_GATE + 1
C_UP = C_OUT + KB
C_DOWN = C_UP + 2 * FT
DCH = [(0, 8), (8, 16), (16, FT)]
N_CHUNK = C_DOWN + 3 * KB
RING = 3
RING_HI = 2

COLS = {}
_n = 0
for _name, _w in [("mix_pre", KB), ("mix_post", KB), ("ffn_pre", KB), ("ffn_post", KB), ("mu", RP),
                  ("w0", RJ), ("a0", RJ), ("k_k", RJ), ("k_a", RJ), ("r_k", RJ), ("lnw", RJ),
                  ("lnb", RJ), ("cw0", FT), ("cw1", FT), ("cw2", FT), ("cb", FT)]:
    COLS[_name] = (_n, _n + _w)
    _n += _w
NCOL = _n

LEVELS = 6
CONST = {}
_n = 0
for _name, _w in [("ident", P), ("blk", P), ("causal", P), ("rot", P), ("gmask", P), ("scan", RJ * SC), ("eye", CH), ("lev", LEVELS * CH), ("lev0t", CH),
                  ("cmask", NQ * NCP), ("hit", NSEL), ("same", ROWS), ("selb", DEC),
                  ("keep", NSEL), ("force", NSEL)]:
    CONST[_name] = (_n, _n + _w)
    _n += _w
NCONST = _n


def constants():
    c = np.zeros((P, NCONST), np.float32)

    def put(name, a):
        lo, hi = CONST[name]
        c[:a.shape[0], lo:hi] = a

    p = np.arange(P)
    s64, t64 = np.arange(CH)[:, None], np.arange(CH)[None, :]
    two = lambda a: np.concatenate([a, a], 0)
    put("ident", np.eye(P))
    put("blk", (p[:, None] // HD == p[None, :] // HD).astype(np.float32))
    put("causal", np.where(p[None, :] <= p[:, None], 0.0, NEG))
    rot = np.zeros((P, P))
    half = ROPE // 2
    for g in range(GROUPS):
        for i in range(half):
            rot[g * HD + half + i, g * HD + i] = -1.0
            rot[g * HD + i, g * HD + half + i] = 1.0
    put("rot", rot)
    put("gmask", two(np.concatenate([s64 < t64, s64 <= t64], 1).astype(np.float32)))
    inv = np.float32(THETA) ** (-np.arange(half, dtype=np.float32) / np.float32(half))
    pos = np.concatenate([np.arange(SEQ), np.full(DEC, PAST)]).astype(np.float32)
    ang = (pos[None, :] * inv.astype(np.float32)[:, None]).astype(np.float32)
    cos, sin = np.ones((P, TOK), np.float32), np.zeros((P, TOK), np.float32)
    for g in range(GROUPS):
        for k in range(2):
            r = slice(g * HD + k * half, g * HD + (k + 1) * half)
            cos[r], sin[r] = np.cos(ang), np.sin(ang)
    put("scan", np.tile((np.arange(RJ * SC) % CH != 0).astype(np.float32), (P, 1)))
    put("eye", two(np.eye(CH)))
    lev = [(s64 // (2 << i) == t64 // (2 << i)) & (s64 // (1 << i) % 2 == 0) & (t64 // (1 << i) % 2 == 1)
           for i in range(LEVELS)]
    put("lev", two(np.concatenate(lev, 1).astype(np.float32)))
    put("lev0t", two(lev[0].T.astype(np.float32)))
    q = np.arange(SEQ).reshape(NQ, P).T
    end = np.arange(NCP) * STRIDE + BLOCK - 1
    put("cmask", np.where(end[None, None, :] <= q[:, :, None], 0.0, NEG).reshape(P, -1))
    c0, s0 = np.arange(NCS) * STRIDE, np.arange(NSEL) * SELB
    put("hit", ((c0[:, None] < s0 + SELB) & (c0[:, None] + BLOCK > s0)).astype(np.float32))
    r = np.arange(ROWS)
    put("same", (r[:, None] // PER == r[None, :] // PER).astype(np.float32))
    put("selb", (r[:, None] // HEADS == np.arange(DEC)[None, :]).astype(np.float32))
    cur = PAST // SELB
    forced = np.isin(np.arange(NSEL), [0, cur, cur - 1]).astype(np.float32)
    put("keep", np.tile(1.0 - forced, (ROWS, 1)))
    put("force", np.tile(forced * 1e9, (ROWS, 1)))
    return c, np.concatenate([cos, sin], 1)


PER_SC = {"x1": 2, "act1": 1, "lora1": 1, "sig1": 1, "ld_ok": 1, "kk1": 2, "root1": 1, "exp1": 1, "prep": 2,
          "gmm": 2, "gmask": 2, "nmm": 1, "mm_ok": LEVELS - 1, "inv_q": LEVELS - 1, "inv_qc": LEVELS - 1,
          "inv_d": LEVELS - 1, "inv_z": LEVELS, "tm_mm": 3, "tm_ev": 3, "rh_mm": 2, "rh_ev": 2, "u_mm": 2,
          "u_ev": 2, "ds_mm": 2, "s_ok": 2, "y_ev": 1, "mean_mm": 1, "yc": 1, "var_mm": 1, "var_v": 1, "var_a": 1}
UNITS = [(t, i, g) for t in range(NQ) for i in range(PER) for g in range(GROUPS)]


def paired():
    stages = ["mix", "squares", "lora", "decay", "keys", "scaled", "pairs", "turn"]
    for lv in range(1, LEVELS):
        stages += [("invert", lv), ("double", lv)]
    for c in range(2):
        stages += [("rhs", c), ("solve", c), ("advance", c)]
    stages += ["mean", "var", "out"]
    rwkv = [("rwkv", sc, st) for sc in range(SEQ // SC) for st in stages]
    att = []
    for t in range(NQ):
        att += [("att", t, "cmp_scores"), ("att", t, "cmp_turn"), ("att", t, "cmp_done")]
        for u in range(HEADS * t, HEADS * (t + 1)):
            att += [("att", u, "scores"), ("att", u, "turn"), ("att", u, "values")]
        att += [("att", t, "heads_out")]
    n = max(len(rwkv), len(att))
    out = []
    for k in range(n):
        for steps in (rwkv, att):
            out += steps[k * len(steps) // n:(k + 1) * len(steps) // n]
    return out


PAIRED = paired()


class Order:

    def __init__(self, eng, sem):
        self.eng, self.sem, self.n = eng, sem, 0

    def go(self, ins):
        self.n += 1
        ins.then_inc(self.sem, 1)

    def settle(self):
        self.eng.wait_ge(self.sem, self.n)

    def do(self, ins):
        self.go(ins)
        self.settle()

    def tell(self, sem):
        self.settle()
        self.eng.sem_inc(sem, 1)


def build(nc, I, O):
    with ExitStack() as ctx:
        def sb(name, shape, dt=F32):
            return ctx.enter_context(nc.sbuf_tensor(name, shape, dt))

        def at_bytes(name, base, floats, shape):
            return nc.alloc_sbuf_tensor_at(name, shape, F32R, offset=base + 4 * floats)

        x = sb("x", [P, KB, TOK])
        hm = sb("hm", [P, KB, TOK])
        nsa = sb("nsa", [P, NT, TOK])
        ring_base = nc.sbuf_base
        ring = sb("ring", [P, RING, KB * P])
        ring_lo = at_bytes("ring_lo", ring_base, 0, [P, RING, KB * P])
        ring_hi = sb("ring_hi", [P, RING_HI, KB * P], F32R)
        cst = sb("cst", [P, NCONST])
        par = sb("par", [P, NCOL])
        cb = sb("cb", [P, 2])
        gates = sb("gates", [P, NQ + 1, 24])
        gate_s = sb("gate_s", [ROWS, 3])
        state = sb("state", [P, RJ, CH])
        rstd = sb("rstd", [P, 2, HALF])
        pages = sb("pages", [1, DEC * PAGES], I32)
        ones = sb("ones", [P, P])
        onesblk = sb("onesblk", [P, P])

        ARENA = 30900
        arena_base = nc.sbuf_base
        arena = sb("arena", [P, ARENA])
        where = [0]

        def at(*shape, reset=None):
            if reset is not None:
                where[0] = reset
            n = int(np.prod(shape))
            a = arena[:, where[0]:where[0] + n]
            where[0] += n
            assert where[0] <= ARENA, where[0]
            if len(shape) > 1:
                names = "abcde"[:len(shape)]
                a = a.rearrange(f"p ({' '.join(names)}) -> p {' '.join(names)}",
                                **{k: s for k, s in zip(names[1:], shape[1:])})
            return a

        sq = at(KB, TOK, reset=0)
        pr = at(RP, 1 + TOK, reset=0)
        prev_s = at(RP, DEC)
        lora = at(2 * RW)
        work0 = where[0]
        xs = at(RP, SC)
        dif = at(RP, SC)
        zz = at(2, RJ, CH, reset=where[0] - RP * SC)
        ww = at(2, RJ, CH)
        qq = at(2, RJ, CH)
        tanw = at(SC, reset=work0 + 2 * RP * SC)
        siggl = at(SC)
        gg = at(RJ, SC)
        kk = at(RJ, SC)
        t0 = at(RJ, SC)
        t1 = at(RJ, SC)
        rk = at(RJ, SC)
        pin = at(RJ, SC)
        dead = where[0]
        sw = at(RJ, SC)
        aa = at(RJ, SC)
        cum = at(RJ, SC)
        pex = at(RJ, SC)
        km = at(RJ, SC)
        piv = at(RJ, SC)
        gb = at(2, RJ, 2, CH, reset=dead)
        gk = at(2, RJ, 2, CH)
        btm = at(2, RJ, CH)
        ktm = at(2, RJ, CH)
        vtm = at(2, RJ, CH)
        ar = at(RJ, 2, 2, CH)
        bt = at(RJ, SC)
        kt = at(RJ, SC)
        mm = at(2, 2 * RJ, CH)
        rh = at(RJ, CH)
        uu = at(RJ, CH)
        side = where[0] + 50
        ss = at(RJ, DEC, CH, reset=dead + 6 * RJ * SC)
        s1 = at(RJ, DEC, CH)
        assert where[0] <= side
        w1 = at(2, BLOCK, P, reset=work0)
        w2 = at(2, P)
        pe_c = at(2, BLOCK)
        assert where[0] <= dead + 6 * RJ * SC
        trig = at(2, TOK, reset=20480)
        tr = at(TOK)
        tr2 = at(TOK)
        assert where[0] <= side
        vt = at(2, NQ, P, reset=side)
        kcp = at(NCP)
        vcp = at(P)
        hip = at(2, NCP)
        pp = at(2, WIN)
        ppt = at(2, WIN)
        pc = at(HEADS, NCP)
        pcp = at(HEADS, P)
        nm = at(2)
        sums = at(2)
        rr = at(2)
        cm = at(3, HEADS)
        cache = at(2, 8192, reset=0)
        w1s = at(2, BLOCK, P)
        w2s = at(2, P)
        n0 = where[0]
        kcs = at(DEC, NCS)
        vcs = at(DEC, P)
        hid = at(2, 2, NCS + 1)
        ssel = at(NSEL, SELB, reset=n0)
        at(72 + 512, reset=n0 + NSEL * SELB)
        qpad = at(DEC, ROWS)
        pt_s = at(PAGES, ROWS)
        swin = at(WIN)
        ptw = at(4, ROWS)
        pcs = at(NCS + 1)
        pct = at(ROWS)
        imp = at(NSEL)
        work = at(NSEL)
        top = at(8)
        diag = at(2, ROWS)
        pnew = at(2, ROWS)
        vnew = at(2, P)
        impt = at(ROWS)
        sm = at(16)
        hf = at(FT, TOK, reset=0)
        gx = at(2, 2 + TOK)
        cv = at(2, TOK)
        cprev = at(FT, 2, DEC)
        cout = at(FT, 2)
        couts = at(FT, 2, DEC)
        sq2 = at(KB, TOK)

        HS = 20480
        hm_hi = at_bytes("hm_hi", arena_base, HS, [P, KB, TOK])
        hm_lo = at_bytes("hm_lo", arena_base, HS + KB * TOK, [P, KB, TOK])
        hf_lo = at_bytes("hf_lo", arena_base, 0, [P, FT, TOK])
        hf_hi = at_bytes("hf_hi", arena_base, 14272, [P, FT, TOK])

        ps = ctx.enter_context(nc.psum_tensor("ps", [P, 8, 512], F32))

        names = ("arrive v_own a_own p_own params w_used evac_a evac_v gate_mm gate_ev norm_sq norm_mm "
                 "norm_v norm_a norm_h rs_x rs_act rs_lora rs_prep rs_mm rs_var rs_out gs_ready loads_s stores "
                 "rope_mm rope_ok nsa_ready w1_zero w1_ready vt_mm vt_ev cmpp_mm gelu_p kcp_ok at_mm pc_sub pc_exp "
                 "pc_ok pcp_ok sc_mm mx ex sc_v pt_mm pt_ev_a pt_ev_v pv o_ev qpad_ok ss_mm ss_v ss_a c_free "
                 "cmp_h cmp_act cmp_o cmp_k mixed ffn_c ffn_act ffn_h ffn_t w_hi w_lo s_hi s_lo trig_ok rs_stored phase_ok").split()
        S = {n: ctx.enter_context(nc.semaphore(n)) for n in names}
        T = {n: ctx.enter_context(nc.semaphore("rwkv_" + n)) for n in PER_SC}
        w_ready = [ctx.enter_context(nc.semaphore(f"w_ready{i}")) for i in range(RING)]
        c_ready = [ctx.enter_context(nc.semaphore(f"c_ready{i}")) for i in range(2)]
        go = {e: ctx.enter_context(nc.semaphore(f"go_{e}")) for e in ("pe", "v", "a", "p")}
        const_ok = ctx.enter_context(nc.semaphore("const_ok"))
        ones_ok = ctx.enter_context(nc.semaphore("ones_ok"))
        p_const = ctx.enter_context(nc.semaphore("p_const"))
        block = ctx.enter_context(nc.Block())

        def K(name, rows=P):
            lo, hi = CONST[name]
            return cst[0:rows, lo:hi]

        def C(name, i=None):
            lo, hi = COLS[name]
            return par[:, lo:hi] if i is None else par[:, lo + i:lo + i + 1]

        ident, blk = K("ident"), K("blk")
        eye = K("eye")

        def wide(col, n):
            return col.unsqueeze(2).to_broadcast((P, col.shape[1], n))

        def bank2(b):
            return ps[:, b:b + 2, 0:HALF]

        def halves(a):
            return a.rearrange("p (h n) -> p h n", h=2)

        def b4(i, n=SC):
            return ps[:, i, 0:RJ * n].rearrange("p (j n) -> p j n", j=RJ)

        HALVES = [(h, slice(h * HALF, (h + 1) * HALF)) for h in range(2)]
        CMP_U = DEC // 2
        N_UNIT = 1 + CMP_U + 4

        def tile_done(n):
            if n < NT + RP:
                return n + 1
            down = n - (NT + RP + KB + 2 * FT)
            return n + 2 if down < 0 else C_DOWN + 3 * (down + 1)

        def meet(eng, who, arrive):
            eng.sem_inc(arrive, 1)
            eng.wait_ge(go[who], 1)
            eng.sem_clear(go[who])

        @block.sync
        def _(sp):
            sp.dma_start(cst[:], I["consts"]).then_inc(const_ok, 16)
            sp.dma_start(pages[:], I["pages"]).then_inc(const_ok, 16)
            sp.dma_start(x[:], I["x"].rearrange("k p t -> p k t")).then_inc(const_ok, 16)

            def host_meet(arrive, sems):
                sp.wait_ge(arrive, 4)
                for s in sems:
                    sp.sem_clear(s)
                for e in go:
                    sp.sem_inc(go[e], 1)

            def compression_weights(l, w1, w2):
                for c in range(2):
                    for g in range(GROUPS):
                        r = slice(g * HD, (g + 1) * HD)
                        sp.dma_start(w1[r, c, :, r], I["w1"][l, c].rearrange("d (k e) -> d k e", k=BLOCK)).then_inc(S["w1_ready"], 16)
                        sp.dma_start(w2[r, c, r], I["w2"][l, c]).then_inc(S["w1_ready"], 16)

            with sp.Fori(0, DEPTH) as l:
                sp.dma_start(par[:], I["cols"][l]).then_inc(S["params"], 16)
                sp.dma_start(prev_s, I["shift"][l].rearrange("p (a b) -> p a b", a=RP)).then_inc(S["params"], 16)
                sp.dma_start(lora, I["lora"][l]).then_inc(S["params"], 16)

                def chunk(n):
                    if n >= RING:
                        sp.wait_ge(S["w_used"], n - RING + 1)
                    sp.dma_start(ring[:, n % RING, :], I["w"][l, n]).then_inc(w_ready[n % RING], 16)

                for n in range(C_OUT):
                    chunk(n)
                sp.wait_ge(S["w1_zero"], 1)
                compression_weights(l, w1, w2)
                for c in range(2):
                    for g in range(GROUPS):
                        sp.dma_start(pe_c[g * HD:(g + 1) * HD, c, :], I["pe"][l, c]).then_inc(S["w1_ready"], 16)
                sp.wait_ge(S["w_used"], NT + RP)
                sp.dma_start(trig, I["trig"].rearrange("p (a t) -> p a t", a=2)).then_inc(S["trig_ok"], 16)
                sp.dma_start(ss, I["wkv"][l].rearrange("p (a b c) -> p a b c", a=RJ, b=DEC)).then_inc(S["loads_s"], 16)
                for n in range(C_OUT, C_OUT + RING):
                    chunk(n)
                sp.wait_ge(S["nsa_ready"], 1)
                sp.dma_start(O["kv"][l].rearrange("p (a b) -> p a b", a=6), nsa[:, 4:NT, :]).then_inc(S["stores"], 16)
                for b in range(DEC):
                    sp.dma_start(O["win_old"][l, b], I["win"][l, b]).then_inc(S["stores"], 16)
                sp.wait_ge(S["rs_out"], 1)
                sp.dma_start(O["wkv_s"][l].rearrange("p (a b c) -> p a b c", a=RJ, b=DEC), ss).then_inc(S["rs_stored"], 16)
                sp.dma_start(O["shift"][l].rearrange("p (a b) -> p a b", a=RP), pr[:, :, SEQ:SEQ + 1 + DEC]).then_inc(S["rs_stored"], 16)
                sp.wait_ge(S["rs_stored"], 32)
                sp.wait_ge(S["gate_ev"], NQ + 1)
                sp.dma_start(gate_s[:], gates[0:DEC, NQ, :].rearrange("b (h n) -> b h n", n=3)).then_inc(S["gs_ready"], 16)
                sp.wait_ge(S["phase_ok"], 1)
                sp.dma_start(O["wkv_p"][l].rearrange("p (a b) -> p a b", a=RJ), state[:]).then_inc(S["stores"], 16)

                def page_regs(b):
                    _, pages_b = nc.values_load_multi_w_load_instructions(
                        pages[0:1, b * PAGES:(b + 1) * PAGES], engines=[mybir.EngineType.SP], min_val=0, max_val=N_POOL - 1)
                    return pages_b

                for u in range(N_UNIT):
                    if u == 1:
                        sp.wait_ge(S["w1_zero"], 2)
                        compression_weights(l, w1s, w2s)
                    if u >= 2:
                        sp.wait_ge(S["c_free"], u - 1)
                    slot, done = cache[:, u % 2, :], c_ready[u % 2]
                    if u == 0:
                        sp.dma_start(slot[:, 0:DEC * WIN].rearrange("p (b n) -> p b n", b=DEC),
                                     I["kwin"][l].rearrange("b p n -> p b n")).then_inc(done, 16)
                        sp.dma_start(slot[:, DEC * WIN:].rearrange("p (b n) -> p b n", b=DEC),
                                     I["vwin"][l].rearrange("b p n -> p b n")).then_inc(done, 16)
                    elif u <= CMP_U:
                        dst = slot.rearrange("p (c b n t) -> p c b n t", c=2, b=2, t=PAGE)
                        for b in range(2):
                            regs = page_regs(2 * (u - 1) + b)
                            for i, r in enumerate(regs):
                                sp.dma_start(dst[:, :, b, i, :], I["kv_cmp"][l * N_POOL + r].rearrange("p (c t) -> p c t", c=2)).then_inc(done, 16)
                    else:
                        src = I["k_sel"] if u < CMP_U + 3 else I["v_sel"]
                        dst = slot.rearrange("p (b n t) -> p b n t", b=4, t=PAGE)
                        for b in range(4):
                            regs = page_regs(4 * ((u - CMP_U - 1) % 2) + b)
                            for i, r in enumerate(regs):
                                sp.dma_start(dst[:, b, i, :], src[l * N_POOL + r]).then_inc(done, 16)
                for n in range(C_OUT + RING, C_UP):
                    chunk(n)
                sp.wait_ge(S["mixed"], 1)
                sp.dma_start(cprev, I["conv"][l].rearrange("p (a b c) -> p a b c", a=FT, b=2)).then_inc(S["loads_s"], 16)
                for n in range(C_UP, N_CHUNK):
                    chunk(n)
                sp.wait_ge(S["ffn_t"], FT)
                sp.dma_start(O["conv_p"][l].rearrange("p (a b) -> p a b", a=FT), cout).then_inc(S["stores"], 16)
                sp.dma_start(O["conv_s"][l].rearrange("p (a b c) -> p a b c", a=FT, b=2), couts).then_inc(S["stores"], 16)
                sp.wait_ge(S["stores"], 16 * (4 + DEC))
                host_meet(S["arrive"], list(S.values()) + list(T.values()) + w_ready + c_ready)
            sp.dma_start(O["y"].rearrange("k p t -> p k t"), x[:]).then_inc(const_ok, 16)
            sp.wait_ge(const_ok, 64)

        @block.tensor
        def _(pe):
            mmul = nc.tensor.matmul

            def w_wait(n):
                if n == C_GATE:
                    pe.wait_ge(w_ready[n % RING], 16 * (n // RING + 1))
                else:
                    pe.wait_ge(S["w_lo"], n + 1 - (n > C_GATE))

            dense_n = [0]

            def dense_tile(chunks, hi, lo, first=None):
                b = 2 * (dense_n[0] % 3)
                if dense_n[0] >= 3:
                    pe.wait_ge(S["evac_a"], dense_n[0] - 2)
                    pe.wait_ge(S["evac_v"], dense_n[0] - 2)
                for ci, (n, k0, k1) in enumerate(chunks):
                    w_wait(n)
                    for k in range(k0, k1):
                        if first is not None:
                            pe.wait_ge(S["s_lo"], first + k + 1)
                        w = slice((k - k0) * P, (k - k0 + 1) * P)
                        wh, wl = ring_hi[:, n % RING_HI, w], ring_lo[:, n % RING, w]
                        for h, cols in HALVES:
                            out = ps[:, b + h, 0:HALF]
                            mmul(out, wh, hi[:, k, cols], start=(k == 0), stop=False)
                            mmul(out, wh, lo[:, k, cols], start=False, stop=False)
                            last = mmul(out, wl, hi[:, k, cols], start=False, stop=(ci == len(chunks) - 1 and k == k1 - 1))
                    last.then_inc(S["w_used"], 1)
                dense_n[0] += 1

            norm_n = [0]

            def norm(src):
                pe.wait_ge(S["norm_sq"], norm_n[0] + 1)
                for h, cols in HALVES:
                    for k in range(KB):
                        last = mmul(ps[:, 6 + h, 0:HALF], ones[:], src[:, k, cols], start=(k == 0), stop=(k == KB - 1))
                last.then_inc(S["norm_mm"], 1)
                norm_n[0] += 1

            pe.wait_ge(ones_ok, 1)
            pe.wait_ge(const_ok, 48)
            with pe.Fori(0, DEPTH) as _l:
                dense_n[0] = norm_n[0] = 0
                norm(sq)
                for m in range(NT + RP):
                    dense_tile([(m, 0, KB)], hm_hi, hm_lo, 0 if m == 0 else None)
                w_wait(C_GATE)
                wg = ring[:, C_GATE % RING, 0:KB * 24].rearrange("p (k n) -> p k n", k=KB)
                for t in range(NQ + 1):
                    n = P if t < NQ else DEC
                    if t >= 1:
                        pe.wait_ge(S["gate_ev"], t)
                    for k in range(KB):
                        last = mmul(ps[0:n, 6, 0:24], hm[:, k, t * P:t * P + n], wg[:, k, :], start=(k == 0), stop=(k == KB - 1))
                    last.then_inc(S["gate_mm"], 1)
                pe.wait_ge(S["gate_mm"], NQ + 1)
                pe.sem_inc(S["w_used"], 1)

                pe.wait_ge(S["evac_a"], NT + RP)
                pe.wait_ge(S["evac_v"], NT + RP)
                for n, tile in enumerate((0, 1, 2, 3, 4, 6, 8)):
                    if n >= 1:
                        pe.wait_ge(S["rope_ok"], n)
                    for h, cols in HALVES:
                        last = mmul(ps[:, h, 0:HALF], K("rot"), nsa[:, tile, cols], start=True, stop=True)
                    last.then_inc(S["rope_mm"], 1)
                pe.wait_ge(S["rope_ok"], 7)
                for br in range(2):
                    for t in range(NQ):
                        last = nc.tensor.transpose(ps[:, br, t * P:(t + 1) * P], nsa[:, 7 + 2 * br, t * P:(t + 1) * P], ident)
                last.then_inc(S["vt_mm"], 1)
                pe.wait_ge(S["w1_ready"], 16 * 12)
                for c in range(2):
                    for k in range(BLOCK):
                        mmul(ps[:, 2, c:c + 1], w1[:, c, k, :], pe_c[:, c, k:k + 1], start=(k == 0), stop=(k == BLOCK - 1))
                    for k in range(BLOCK):
                        last = mmul(ps[:, 3, c * P:c * P + NCP], w1[:, c, k, :], nsa[:, 4 + c, k:k + STRIDE * (NCP - 1) + 1:STRIDE],
                                    start=(k == 0), stop=(k == BLOCK - 1))
                last.then_inc(S["cmpp_mm"], 1)
                pe.wait_ge(S["gelu_p"], 1)
                mmul(ps[:, 4, 0:NCP], w2[:, 0, :], hip[:, 0, :], start=True, stop=True)
                mmul(ps[0:NCP, 5, 0:P], hip[:, 1, :], w2[:, 1, :], start=True, stop=True).then_inc(S["cmpp_mm"], 1)
                pe.wait_ge(S["kcp_ok"], 1)
                pe.wait_ge(S["vt_ev"], 1)

                def lora_products(n, ready, done):
                    pe.wait_ge(*ready)
                    for j in range(RJ):
                        c = slice(j * P, (j + 1) * P)
                        mmul(ps[:, 0, j * n:(j + 1) * n], lora[0:HD, c], tanw[0:HD, 0:n], start=True, stop=True)
                        mmul(ps[:, 1, j * n:(j + 1) * n], lora[HD:P, c], xs[HD:P, 3 * RJ, 0:n], start=True, stop=True)
                        last = mmul(ps[:, 2, j * n:(j + 1) * n], lora[:, RW + j * P:RW + (j + 1) * P], siggl[:, 0:n], start=True, stop=True)
                    last.then_inc(done, 1)

                pe.wait_ge(S["params"], 48)
                pe.wait_ge(S["loads_s"], 16)
                lora_products(DEC, (S["rs_act"], 1), S["rs_lora"])
                pe.wait_ge(S["rs_x"], 1)
                mmul(ps[:, 3, 0:RJ * DEC], blk, t0[:, :, 0:DEC], start=True, stop=True).then_inc(S["rs_mm"], 1)
                pe.wait_ge(S["rs_prep"], 1)
                mmul(ps[:, 3, 0:RJ * DEC], blk, t1[:, :, 0:DEC], start=True, stop=True)
                for part in range(2):
                    for j in range(RJ):
                        for b in range(DEC):
                            for h in range(2):
                                r = slice(h * HD, (h + 1) * HD)
                                if part == 0:
                                    last = mmul(ps[r, 4 + j, b * CH:(b + 1) * CH],
                                                pex[r, j, b:b + 1].to_broadcast((HD, HD)), ss[r, j, b, :], start=True, stop=True)
                                else:
                                    last = mmul(ps[r, 4 + j, b * CH:(b + 1) * CH],
                                                xs[r, 2 * RJ + j, b:b + 1].to_broadcast((HD, HD)), eye[r, :], start=True, stop=True)
                    last.then_inc(S["rs_mm"], 1)
                    pe.wait_ge(S["rs_prep"], 2 + part)
                pe.wait_ge(S["rs_prep"], 4)
                for j in range(RJ):
                    for b in range(DEC):
                        for h in range(2):
                            r = slice(h * HD, (h + 1) * HD)
                            last = mmul(ps[r, 0, j * DEC + b:j * DEC + b + 1], ss[r, j, b, :], xs[r, j, b:b + 1], start=True, stop=True)
                last.then_inc(S["rs_mm"], 1)
                for i, src in ((5, kk), (6, t0)):
                    pe.wait_ge(S["rs_prep"], i)
                    mmul(ps[:, 1, 0:RJ * DEC], onesblk[:], src[:, :, 0:DEC], start=True, stop=True).then_inc(S["rs_mm"], 1)
                pe.wait_ge(S["rs_out"], 1)

                HP = [slice(h * HD, (h + 1) * HD) for h in range(2)]

                def rwkv(sc, stage):
                    at_sc = lambda name, n: (T[name], PER_SC[name] * sc + n)
                    lv = stage[1]
                    if stage == "lora":
                        lora_products(SC, at_sc("act1", 1), T["lora1"])
                        pe.wait_ge(*at_sc("x1", 2))
                        mmul(ps[:, 3, :], blk, t0, start=True, stop=True).then_inc(T["kk1"], 1)
                    elif stage == "keys":
                        pe.wait_ge(*at_sc("prep", 1))
                        mmul(ps[:, 3, :], blk, t1, start=True, stop=True).then_inc(T["kk1"], 1)
                    elif stage == "pairs":
                        pe.wait_ge(*at_sc("prep", 2))
                        for c in range(2):
                            cs = slice(c * CH, (c + 1) * CH)
                            for j in range(RJ):
                                for r in HP:
                                    mmul(ps[r, 2 * c, j * P:(j + 1) * P], bt[r, j, cs], ar[r, j, c, :, :], start=True, stop=True)
                                    last = mmul(ps[r, 2 * c + 1, j * P:(j + 1) * P], kt[r, j, cs], ar[r, j, c, :, :], start=True, stop=True)
                            last.then_inc(T["gmm"], 1)
                    elif stage == "turn":
                        pe.wait_ge(*at_sc("gmask", 1))
                        for cj in range(2 * RJ):
                            c, j = divmod(cj, RJ)
                            for r in HP:
                                last = mmul(ps[r, 0, cj * CH:(cj + 1) * CH], ar[r, j, c, 0, :], bt[r, j, c * CH:(c + 1) * CH], start=True, stop=True)
                        last.then_inc(T["nmm"], 1)
                        for n, src in ((1, bt), (2, kt), (3, xs[:, 2 * RJ:3 * RJ, :])):
                            if n == 2:
                                pe.wait_ge(*at_sc("gmask", 2))
                            for cj in range(2 * RJ):
                                c, j = divmod(cj, RJ)
                                for r in HP:
                                    last = mmul(ps[r, n, cj * CH:(cj + 1) * CH], src[r, j, c * CH:(c + 1) * CH], eye[r, :], start=True, stop=True)
                            last.then_inc(T["tm_mm"], 1)
                    elif stage[0] == "invert":
                        pe.wait_ge(*at_sc("inv_z", lv))
                        pe.wait_ge(*at_sc("mm_ok", lv))
                        for cj in range(2 * RJ):
                            c, j = divmod(cj, RJ)
                            for r in HP:
                                last = mmul(ps[r, 0, cj * CH:(cj + 1) * CH], mm[r, lv % 2, cj, :], ww[r, c, j, :], start=True, stop=True)
                        last.then_inc(T["inv_q"], 1)
                    elif stage[0] == "double":
                        if lv == 1:
                            pe.wait_ge(*at_sc("tm_ev", 3))
                        pe.wait_ge(*at_sc("inv_qc", lv))
                        for cj in range(2 * RJ):
                            c, j = divmod(cj, RJ)
                            for r in HP:
                                last = mmul(ps[r, 1, cj * CH:(cj + 1) * CH], qq[r, c, j, :], zz[r, c, j, :], start=True, stop=True)
                                if lv < LEVELS - 1:
                                    last = mmul(ps[r, 2, cj * CH:(cj + 1) * CH], zz[r, c, j, :], qq[r, c, j, :], start=True, stop=True)
                        last.then_inc(T["inv_d"], 1)
                    elif stage[0] == "rhs":
                        c = stage[1]
                        pe.wait_ge(*at_sc("inv_z", LEVELS))
                        if sc or c:
                            pe.wait_ge(T["s_ok"], 2 * sc + c)
                        for j in range(RJ):
                            for r in HP:
                                o = ps[r, 0, j * CH:(j + 1) * CH]
                                mmul(o, ar[r, j, c, 0, :], state[r, j, :], start=True, stop=False)
                                last = mmul(o, gk[r, c, j, 0, :], vtm[r, c, j, :], start=False, stop=True)
                        last.then_inc(T["rh_mm"], 1)
                    elif stage[0] == "solve":
                        c = stage[1]
                        pe.wait_ge(*at_sc("rh_ev", c + 1))
                        for j in range(RJ):
                            for r in HP:
                                last = mmul(ps[r, 1, j * CH:(j + 1) * CH], zz[r, c, j, :], rh[r, j, :], start=True, stop=True)
                        last.then_inc(T["u_mm"], 1)
                    elif stage[0] == "advance":
                        c = stage[1]
                        pe.wait_ge(*at_sc("u_ev", c + 1))
                        for j in range(RJ):
                            for r in HP:
                                o = ps[r, 2, j * SC + c * CH:j * SC + (c + 1) * CH]
                                mmul(o, state[r, j, :], ar[r, j, c, 1, :], start=True, stop=False)
                                mmul(o, uu[r, j, :], gb[r, c, j, 1, :], start=False, stop=False)
                                mmul(o, vtm[r, c, j, :], gk[r, c, j, 1, :], start=False, stop=True)
                                o = ps[r, 3, j * CH:(j + 1) * CH]
                                mmul(o, btm[r, c, j, :], uu[r, j, :], start=True, stop=False)
                                last = mmul(o, ktm[r, c, j, :], vtm[r, c, j, :], start=False, stop=True)
                        last.then_inc(T["ds_mm"], 1)
                    elif stage == "mean":
                        pe.wait_ge(*at_sc("y_ev", 1))
                        mmul(ps[:, 0, :], onesblk[:], kk, start=True, stop=True).then_inc(T["mean_mm"], 1)
                    elif stage == "var":
                        pe.wait_ge(*at_sc("yc", 1))
                        mmul(ps[:, 1, :], onesblk[:], t0, start=True, stop=True).then_inc(T["var_mm"], 1)

                def att(n, step):
                    t, i, g = UNITS[n]
                    r = slice(g * HD, (g + 1) * HD)
                    h = g * PER + i
                    if step == "cmp_scores":
                        t = n
                        for g in range(GROUPS):
                            if g:
                                pe.wait_ge(S["at_mm"], 3 * t + 1)
                            r = slice(g * HD, (g + 1) * HD)
                            for i in range(PER):
                                h = g * PER + i
                                last = mmul(ps[:, 6, h * NCP:(h + 1) * NCP], nsa[r, i, t * P:(t + 1) * P], kcp[r, :], start=True, stop=True)
                            last.then_inc(S["at_mm"], 1)
                    elif step == "cmp_turn":
                        pe.wait_ge(S["pc_ok"], n + 1)
                        for h in range(HEADS):
                            last = nc.tensor.transpose(ps[0:NCP, 6 - 2 * (h // 4), (h % 4) * P:(h % 4 + 1) * P], pc[:, h, :], ident)
                        last.then_inc(S["at_mm"], 1)
                    elif step == "scores":
                        if n % HEADS == 0:
                            pe.wait_ge(S["pcp_ok"], t + 1)
                        for br in range(2):
                            last = mmul(ps[:, 4 + br, 0:(t + 1) * P], nsa[r, i, t * P:(t + 1) * P],
                                        nsa[r, 6 + 2 * br, 0:(t + 1) * P], start=True, stop=True)
                        last.then_inc(S["sc_mm"], 1)
                    elif step == "turn":
                        pe.wait_ge(S["sc_v"], n + 1)
                        for br in range(2):
                            for k in range(t + 1):
                                last = nc.tensor.transpose(ps[:, 4 + br, k * P:(k + 1) * P], pp[:, br, k * P:(k + 1) * P], ident)
                        last.then_inc(S["pt_mm"], 1)
                    elif step == "values":
                        pe.wait_ge(S["pt_ev_a"], n + 1)
                        pe.wait_ge(S["pt_ev_v"], n + 1)
                        if n % HEADS == 0 and t:
                            pe.wait_ge(S["o_ev"], t)
                        o = ps[r, 7, i * P:(i + 1) * P]
                        mmul(o, vcp[0:NCP, r], pcp[0:NCP, h, :], start=True, stop=False)
                        for br in range(2):
                            for k in range(t + 1):
                                last = mmul(o, vt[:, br, k, r], ppt[:, br, k * P:(k + 1) * P], start=False, stop=(br == 1 and k == t))
                        last.then_inc(S["pv"], 1)

                for side, n, step in PAIRED:
                    (rwkv if side == "rwkv" else att)(n, step)

                unit_dmas = [2] + [2 * PAGES] * CMP_U + [4 * PAGES] * 4

                def unit(u):
                    pe.wait_ge(c_ready[u % 2], 16 * sum(unit_dmas[u % 2:u + 1:2]))
                    return cache[:, u % 2, :]

                sink = dict(start=False, skip_group_check=True)
                pe.wait_ge(S["qpad_ok"], 1)
                slot = unit(0)
                for b in range(DEC):
                    mmul(ps[0:ROWS, 0, 1:WIN], qpad[:, b, :], slot[:, b * WIN + 1:(b + 1) * WIN], start=(b == 0), stop=(b == DEC - 1))
                for b in range(DEC):
                    mmul(ps[0:ROWS, 1, 0:1], qpad[:, b, :], nsa[:, 8, SEQ + b:SEQ + b + 1], start=(b == 0), stop=(b == DEC - 1))
                for n in range(2):
                    last = nc.tensor.transpose(ps[0:DEC, 2, n * P:(n + 1) * P], nsa[:, 7 + 2 * n, SEQ:TOK], ident)
                last.then_inc(S["ss_mm"], 1)
                pe.wait_ge(S["ss_v"], 2)
                for k in range(4):
                    nc.tensor.transpose(ps[:, 3, k * ROWS:(k + 1) * ROWS], swin[0:ROWS, k * P:(k + 1) * P], ident[0:ROWS, 0:ROWS])
                mmul(ps[0:DEC, 4, 0:ROWS], K("selb", ROWS), diag[0:ROWS, 1, :], start=True, stop=True).then_inc(S["ss_mm"], 1)
                pe.wait_ge(S["ss_v"], 3)
                mmul(ps[:, 7, 0:ROWS], vnew[0:DEC, 1, :], pnew[0:DEC, 1, :], start=True, stop=False, skip_group_check=True)
                for b in range(DEC):
                    for k in range(4):
                        v0 = DEC * WIN + b * WIN + k * P
                        last = mmul(ps[:, 7, b * HEADS:(b + 1) * HEADS], slot[:, v0:v0 + P], ptw[:, k, b * HEADS:(b + 1) * HEADS], stop=False, **sink)
                last.then_inc(S["c_free"], 1)
                pe.wait_ge(S["w1_ready"], 16 * 20)
                for u in range(1, CMP_U + 1):
                    slot = unit(u).rearrange("p (c b n) -> p c b n", c=2, b=2)
                    for c in range(2):
                        for k in range(BLOCK):
                            last = mmul(ps[:, c, 0:2 * NCS], w1s[:, c, k, :], slot[:, c, :, k:k + STRIDE * (NCS - 1) + 1:STRIDE],
                                        start=(k == 0), stop=(k == BLOCK - 1))
                    last.then_inc(S["cmp_h"], 1)
                    pe.wait_ge(S["cmp_h"], u)
                    pe.sem_inc(S["c_free"], 1)
                    pe.wait_ge(S["cmp_act"], u)
                    if u >= 2:
                        pe.wait_ge(S["cmp_k"], u - 1)
                    mmul(ps[:, 2, 0:2 * NCS], w2s[:, 0, :], hid[:, 0, :, 0:NCS], start=True, stop=True)
                    for b in range(2):
                        last = mmul(ps[0:NCS, 3, b * P:(b + 1) * P], hid[:, 1, b, 0:NCS], w2s[:, 1, :], start=True, stop=True)
                    last.then_inc(S["cmp_o"], 1)
                pe.wait_ge(S["cmp_k"], CMP_U)
                for b in range(DEC):
                    last = mmul(ps[0:ROWS, 0, 0:NCS], qpad[:, b, :], kcs[:, b, :], start=(b == 0), stop=(b == DEC - 1))
                last.then_inc(S["ss_mm"], 1)
                pe.wait_ge(S["ss_v"], 5)
                mmul(ps[0:NCS, 1, 0:ROWS], pcs[0:ROWS, 0:NCS], K("same", ROWS), start=True, stop=True).then_inc(S["ss_mm"], 1)
                pe.wait_ge(S["ss_v"], 6)
                mmul(ps[0:ROWS, 2, 0:NSEL], impt[0:NCS, :], K("hit", NCS), start=True, stop=True)
                nc.tensor.transpose(ps[0:NCS, 3, 0:ROWS], pcs[0:ROWS, 0:NCS], ident[0:ROWS, 0:ROWS]).then_inc(S["ss_mm"], 1)
                pe.wait_ge(S["ss_v"], 7)
                for b in range(DEC):
                    mmul(ps[:, 7, b * HEADS:(b + 1) * HEADS], vcs[0:NCS, b, :], pct[0:NCS, b * HEADS:(b + 1) * HEADS], stop=False, **sink)
                for half in range(2):
                    slot = unit(CMP_U + 1 + half).rearrange("p (b n) -> p b n", b=4)
                    for b in range(4):
                        for k in range(4):
                            last = mmul(ps[0:ROWS, k, :], qpad[:, 4 * half + b, :], slot[:, b, k * 512:(k + 1) * 512],
                                        start=(half == 0 and b == 0), stop=(half == 1 and b == 3))
                    last.then_inc(S["c_free"], 1)
                for b in range(DEC):
                    last = mmul(ps[0:ROWS, 4, 0:1], qpad[:, b, :], nsa[:, 6, SEQ + b:SEQ + b + 1], start=(b == 0), stop=(b == DEC - 1))
                last.then_inc(S["ss_mm"], 1)
                pe.wait_ge(S["ss_v"], 9)
                flat = ssel.rearrange("p a b -> p (a b)")
                for k in range(PAGES):
                    nc.tensor.transpose(ps[:, k // 8, (k % 8) * ROWS:(k % 8 + 1) * ROWS], flat[0:ROWS, k * P:(k + 1) * P], ident[0:ROWS, 0:ROWS])
                mmul(ps[0:DEC, 2, 0:ROWS], K("selb", ROWS), diag[0:ROWS, 0, :], start=True, stop=True).then_inc(S["ss_mm"], 1)
                pe.wait_ge(S["ss_v"], 10)
                mmul(ps[:, 7, 0:ROWS], vnew[0:DEC, 0, :], pnew[0:DEC, 0, :], stop=False, **sink)
                for half in range(2):
                    slot = unit(CMP_U + 3 + half).rearrange("p (b n t) -> p b n t", b=4, t=PAGE)
                    for b in range(4):
                        s = 4 * half + b
                        for k in range(PAGES):
                            last = mmul(ps[:, 7, s * HEADS:(s + 1) * HEADS], slot[:, b, k, :], pt_s[:, k, s * HEADS:(s + 1) * HEADS],
                                        stop=(s == DEC - 1 and k == PAGES - 1), **sink)
                last.then_inc(S["ss_mm"], 1)
                pe.wait_ge(S["mixed"], 1)

                for m in range(KB):
                    dense_tile([(C_OUT + m, 0, KB)], hm_hi, hm_lo, KB if m == 0 else None)
                norm(sq2)
                norm(sq2)
                for m in range(2 * FT):
                    dense_tile([(C_UP + m, 0, KB)], hm_hi, hm_lo, 2 * KB if m == 0 else None)
                for m in range(KB):
                    dense_tile([(C_DOWN + 3 * m + i, a, b) for i, (a, b) in enumerate(DCH)], hf_hi, hf_lo, 3 * KB if m == 0 else None)
                norm(sq2)
                pe.wait_ge(S["norm_mm"], 4)
                meet(pe, "pe", S["arrive"])

        @block.scalar
        def _(act):
            o = Order(act, S["a_own"])
            A = nc.scalar.activation
            act.wait_ge(const_ok, 48)
            with act.Fori(0, DEPTH) as _l:
                o.n = 0
                n_dense = [0]

                def norm_root(n):
                    act.wait_ge(S["norm_v"], n)
                    o.do(A(rstd[:], rstd[:], ACT.Sqrt))
                    o.tell(S["norm_a"])

                def evac(dst):
                    n = n_dense[0]
                    act.wait_ge(S["w_used"], tile_done(n))
                    A(dst, ps[:, 2 * (n % 3), 0:HALF], ACT.Copy).then_inc(S["evac_a"], 1)
                    n_dense[0] += 1

                def split_w(*chunks):
                    for n in chunks:
                        if n != C_GATE and n < N_CHUNK:
                            act.wait_ge(w_ready[n % RING], 16 * (n // RING + 1))
                            if n >= RING_HI:
                                act.wait_ge(S["w_used"], n - RING_HI + 1)
                            A(ring_hi[:, n % RING_HI, :], ring[:, n % RING, :], ACT.Copy).then_inc(S["w_hi"], 1)

                def split_s(dst, src, k):
                    A(dst[:, k, :], src[:, k, :], ACT.Copy).then_inc(S["s_hi"], 1)

                def squares(dst, src):
                    for k in range(KB):
                        o.go(A(dst[:, k, :], src[:, k, :], ACT.Square))
                    o.tell(S["norm_sq"])

                squares(sq, x)
                split_w(0, 1)
                norm_root(1)
                for k in range(KB):
                    act.wait_ge(S["norm_h"], k + 1)
                    split_s(hm_hi, hm, k)
                for m in range(NT + RP):
                    if m + 2 < C_GATE:
                        split_w(m + 2)
                    evac(nsa[:, m, 0:HALF] if m < NT else pr[:, m - NT, 1:1 + HALF])
                for t in range(NQ + 1):
                    n = P if t < NQ else DEC
                    act.wait_ge(S["gate_mm"], t + 1)
                    o.do(A(gates[0:n, t, :], ps[0:n, 6, 0:24], ACT.Sigmoid))
                    o.tell(S["gate_ev"])

                act.wait_ge(S["vt_mm"], 1)
                for br in range(2):
                    o.go(A(vt[:, br, :, :].rearrange("p t n -> p (t n)"), ps[:, br, :], ACT.Copy))
                o.tell(S["vt_ev"])
                act.wait_ge(S["cmpp_mm"], 1)
                o.do(A(cb[:], ps[:, 2, 0:2], ACT.Copy))
                for c in range(2):
                    o.go(A(hip[:, c, :], ps[:, 3, c * P:c * P + NCP], ACT.Gelu_apprx_tanh, bias=cb[:, c:c + 1]))
                o.tell(S["gelu_p"])
                act.wait_ge(S["cmpp_mm"], 2)
                o.go(A(kcp, ps[:, 4, 0:NCP], ACT.Copy))
                o.go(A(vcp[0:NCP, :], ps[0:NCP, 5, 0:P], ACT.Copy))
                o.tell(S["kcp_ok"])

                act.wait_ge(S["params"], 48)
                act.wait_ge(S["rs_x"], 1)
                o.go(A(tanw[0:HD, 0:DEC], xs[0:HD, 3 * RJ, 0:DEC], ACT.Tanh))
                o.go(A(siggl[:, 0:DEC], xs[:, 3 * RJ + 1, 0:DEC], ACT.Sigmoid))
                o.tell(S["rs_act"])
                act.wait_ge(S["rs_lora"], 1)
                for j in range(RJ):
                    o.go(A(sw[:, j, 0:DEC], ps[:, 0, j * DEC:(j + 1) * DEC], ACT.Sigmoid, bias=C("w0", j)))
                    o.go(A(aa[:, j, 0:DEC], ps[:, 1, j * DEC:(j + 1) * DEC], ACT.Sigmoid, bias=C("a0", j)))
                    o.go(A(gg[:, j, 0:DEC], ps[:, 2, j * DEC:(j + 1) * DEC], ACT.Copy))
                act.wait_ge(S["rs_mm"], 1)
                o.go(A(t1[:, :, 0:DEC], b4(3, DEC), ACT.Sqrt))
                o.settle()
                o.go(A(pin[:, :, 0:DEC], sw[:, :, 0:DEC], ACT.Exp, scale=-math.exp(-0.5)))
                o.tell(S["rs_act"])
                act.wait_ge(S["rs_var"], 1)
                o.go(A(t1[:, :, 0:DEC], t1[:, :, 0:DEC], ACT.Sqrt))
                o.tell(S["rs_act"])
                act.wait_ge(S["rs_out"], 1)

                wide_copy = lambda dst, b, n=2 * RJ * CH: o.go(A(dst, ps[:, b, 0:n], ACT.Copy))

                def rwkv(sc, stage):
                    at_sc = lambda name, n: (T[name], PER_SC[name] * sc + n)
                    if stage == "squares":
                        act.wait_ge(*at_sc("x1", 1))
                        o.go(A(tanw[0:HD, :], xs[0:HD, 3 * RJ, :], ACT.Tanh))
                        o.go(A(siggl, xs[:, 3 * RJ + 1, :], ACT.Sigmoid))
                        o.tell(T["act1"])
                    elif stage == "lora":
                        act.wait_ge(*at_sc("lora1", 1))
                        for j in range(RJ):
                            o.go(A(sw[:, j, :], ps[:, 0, j * SC:(j + 1) * SC], ACT.Sigmoid, bias=C("w0", j)))
                            o.go(A(aa[:, j, :], ps[:, 1, j * SC:(j + 1) * SC], ACT.Sigmoid, bias=C("a0", j)))
                        o.tell(T["sig1"])
                        o.go(A(gg, b4(2), ACT.Copy))
                        act.wait_ge(*at_sc("kk1", 1))
                        o.go(A(t1, b4(3), ACT.Sqrt))
                        o.tell(T["root1"])
                    elif stage == "decay":
                        act.wait_ge(*at_sc("ld_ok", 1))
                        o.go(A(pin, cum, ACT.Exp))
                        o.go(A(pex, pex, ACT.Exp))
                        o.go(A(piv, cum, ACT.Exp, scale=-1.0))
                        o.tell(T["exp1"])
                    elif stage == "turn":
                        for n, (b, dst) in enumerate(((1, btm), (2, ktm), (3, vtm))):
                            act.wait_ge(*at_sc("tm_mm", n + 1))
                            wide_copy(dst.rearrange("p c j t -> p (c j t)"), b)
                            o.tell(T["tm_ev"])
                    elif stage[0] == "invert":
                        act.wait_ge(*at_sc("inv_q", stage[1]))
                        wide_copy(qq.rearrange("p c j t -> p (c j t)"), 0)
                        o.tell(T["inv_qc"])
                    elif stage[0] == "rhs":
                        act.wait_ge(*at_sc("rh_mm", stage[1] + 1))
                        wide_copy(rh.rearrange("p j t -> p (j t)"), 0, RJ * CH)
                        o.tell(T["rh_ev"])
                    elif stage[0] == "solve":
                        act.wait_ge(*at_sc("u_mm", stage[1] + 1))
                        wide_copy(uu.rearrange("p j t -> p (j t)"), 1, RJ * CH)
                        o.tell(T["u_ev"])
                    elif stage == ("advance", 1):
                        act.wait_ge(*at_sc("ds_mm", 2))
                        o.go(A(kk, b4(2), ACT.Copy))
                        o.tell(T["y_ev"])
                    elif stage == "var":
                        act.wait_ge(*at_sc("var_v", 1))
                        o.go(A(t1, t1, ACT.Sqrt))
                        o.tell(T["var_a"])

                def att(n, step):
                    w = (UNITS[n][0] + 1) * P
                    if step == "cmp_scores":
                        act.wait_ge(S["pc_sub"], n + 1)
                        o.go(A(pc, pc, ACT.Exp))
                        o.tell(S["pc_exp"])
                    elif step == "scores":
                        act.wait_ge(S["mx"], n + 1)
                        for br in range(2):
                            o.go(A(pp[:, br, 0:w], ps[:, 4 + br, 0:w], ACT.Exp, bias=nm[:, br:br + 1], accum_out=sums[:, br:br + 1]))
                        o.tell(S["ex"])
                    elif step == "values":
                        act.wait_ge(S["pt_mm"], n + 1)
                        o.go(A(ppt[:, 0, 0:w], ps[:, 4, 0:w], ACT.Copy))
                        o.tell(S["pt_ev_a"])

                for side, n, step in PAIRED:
                    (rwkv if side == "rwkv" else att)(n, step)

                act.wait_ge(S["ss_v"], 1)
                o.go(A(swin[0:ROWS, :], swin[0:ROWS, :], ACT.Exp, bias=sm[0:ROWS, 0:1], accum_out=sm[0:ROWS, 1:2]))
                o.tell(S["ss_a"])
                for u in range(1, CMP_U + 1):
                    act.wait_ge(S["cmp_h"], u)
                    if u >= 2:
                        act.wait_ge(S["cmp_o"], u - 1)
                    for c in range(2):
                        o.go(A(hid[:, c, :, 0:NCS], ps[:, c, 0:2 * NCS].rearrange("p (b n) -> p b n", b=2), ACT.Gelu_apprx_tanh, bias=cb[:, c:c + 1]))
                    o.tell(S["cmp_act"])
                act.wait_ge(S["ss_v"], 4)
                o.go(A(pcs[0:ROWS, 0:NCS], ps[0:ROWS, 0, 0:NCS], ACT.Exp, bias=sm[0:ROWS, 4:5], accum_out=sm[0:ROWS, 5:6]))
                o.tell(S["ss_a"])
                act.wait_ge(S["ss_v"], 8)
                flat = ssel.rearrange("p a b -> p (a b)")
                o.go(A(flat[0:ROWS, 0:PAST + 1], flat[0:ROWS, 0:PAST + 1], ACT.Exp, bias=sm[0:ROWS, 8:9], accum_out=sm[0:ROWS, 9:10]))
                o.tell(S["ss_a"])

                split_w(C_OUT, C_OUT + 1)
                act.wait_ge(S["mixed"], 1)
                for k in range(KB):
                    split_s(hm_hi, hm, k)
                for m in range(KB):
                    split_w(C_OUT + m + 2)
                    evac(hf[:, m, 0:HALF])
                act.wait_ge(S["evac_a"], NT + RP + KB)
                act.wait_ge(S["evac_v"], NT + RP + KB)
                squares(sq2, hf)
                norm_root(2)
                act.wait_ge(S["norm_h"], KB + 1)
                squares(sq2, x)
                norm_root(3)
                for k in range(KB):
                    act.wait_ge(S["norm_h"], KB + 1 + k + 1)
                    split_s(hm_hi, hm, k)
                for m in range(2 * FT):
                    split_w(C_UP + m + 2)
                    i, n = m // 2, n_dense[0]
                    n_dense[0] += 1
                    if m % 2:
                        act.sem_inc(S["evac_a"], 1)
                        continue
                    if i >= 2:
                        act.wait_ge(S["ffn_c"], i - 1)
                        act.wait_ge(S["ffn_t"], i - 1)
                    act.wait_ge(S["w_used"], tile_done(n))
                    for h in range(2):
                        o.go(A(gx[:, i % 2, 2 + h * HALF:2 + (h + 1) * HALF], ps[:, 2 * (n % 3) + h, 0:HALF], ACT.Copy))
                    o.tell(S["evac_a"])
                    act.wait_ge(S["ffn_c"], i + 1)
                    o.go(A(cv[:, i % 2, :], cv[:, i % 2, :], ACT.Gelu_apprx_tanh))
                    o.tell(S["ffn_act"])
                act.wait_ge(S["w_used"], C_DOWN)
                for k in range(FT):
                    act.wait_ge(S["ffn_h"], k + 1)
                    split_s(hf_hi, hf, k)
                for m in range(KB):
                    split_w(*(C_DOWN + 3 * m + i for i in (2, 3, 4)))
                    evac(hm[:, m, 0:HALF])
                act.wait_ge(S["evac_a"], NT + RP + 2 * KB + 2 * FT)
                act.wait_ge(S["evac_v"], NT + RP + 2 * KB + 2 * FT)
                squares(sq2, hm)
                norm_root(4)
                meet(act, "a", S["arrive"])

        @block.gpsimd
        def _(pool):
            o = Order(pool, S["p_own"])
            g = nc.gpsimd
            g.memset(ones[:], 1.0 / D_MODEL).then_inc(p_const, 1)
            pool.wait_ge(p_const, 1)
            pool.sem_inc(ones_ok, 1)
            pool.wait_ge(const_ok, 48)
            with pool.Fori(0, DEPTH) as _l:
                o.n = 0
                o.go(g.memset(w1, 0.0))
                o.go(g.memset(w2, 0.0))
                o.tell(S["w1_zero"])
                for sc in range(SEQ // SC):
                    for lv in range(1, LEVELS):
                        if lv == 1:
                            pool.wait_ge(T["gmask"], 2 * sc + 2)
                        if lv > 2:
                            pool.wait_ge(T["inv_q"], (LEVELS - 1) * sc + lv - 2)
                        lo = CONST["lev"][0] + lv * CH
                        m = cst[:, lo:lo + CH].unsqueeze(1).to_broadcast((P, RJ, CH))
                        for c in range(2):
                            o.go(g.tensor_tensor(mm[:, lv % 2, c * RJ:(c + 1) * RJ, :], gb[:, c, :, 0, :], m, ALU.mult))
                        o.tell(T["mm_ok"])
                pool.wait_ge(S["phase_ok"], 1)
                o.go(g.memset(w1s, 0.0))
                o.go(g.memset(w2s, 0.0))
                o.tell(S["w1_zero"])
                for i in range(FT):
                    pool.wait_ge(S["evac_a"], NT + RP + KB + 2 * i + 1)
                    if i == 0:
                        pool.wait_ge(S["loads_s"], 32)
                    o.go(g.tensor_copy(cout[:, i, :], gx[:, i % 2, SEQ:SEQ + 2]))
                    o.go(g.tensor_copy(couts[:, i, 0, :], cprev[:, i, 1, :]))
                    o.go(g.tensor_copy(couts[:, i, 1, :], gx[:, i % 2, 2 + SEQ:2 + TOK]))
                    o.tell(S["ffn_t"])
                meet(pool, "p", S["arrive"])

        @block.vector
        def _(dve):
            o = Order(dve, S["v_own"])
            v = nc.vector
            MUL, ADD, SUB, MAX = ALU.mult, ALU.add, ALU.subtract, ALU.max
            LD = -math.exp(-0.5)
            dve.wait_ge(const_ok, 48)
            o.do(v.tensor_scalar(onesblk[:], blk, 1.0 / HD, None, MUL))
            with dve.Fori(0, DEPTH) as _l:
                dve.sem_clear(S["v_own"])
                o.n = 0
                n_dense = [0]

                def norm_inv(n):
                    dve.wait_ge(S["norm_mm"], n)
                    o.do(v.tensor_scalar(rstd[:], bank2(6), EPS, None, ADD))
                    o.do(v.reciprocal(rstd[:], rstd[:]))
                    o.tell(S["norm_v"])
                    dve.wait_ge(S["norm_a"], n)

                rs = rstd[:].rearrange("p h n -> p (h n)")

                def evac(dst):
                    n = n_dense[0]
                    dve.wait_ge(S["w_used"], tile_done(n))
                    v.tensor_copy(dst, ps[:, 2 * (n % 3) + 1, 0:HALF]).then_inc(S["evac_v"], 1)
                    n_dense[0] += 1

                n_split = [0, 0]

                def split_w(*chunks):
                    for n in chunks:
                        if n != C_GATE and n < N_CHUNK:
                            n_split[0] += 1
                            dve.wait_ge(S["w_hi"], n_split[0])
                            r = ring[:, n % RING, :]
                            v.tensor_tensor(ring_lo[:, n % RING, :], r, ring_hi[:, n % RING_HI, :], SUB).then_inc(S["w_lo"], 1)

                def split_s(dst, src, hi, blocks):
                    for k in range(blocks):
                        n_split[1] += 1
                        dve.wait_ge(S["s_hi"], n_split[1])
                        v.tensor_tensor(dst[:, k, :], src[:, k, :], hi[:, k, :], SUB).then_inc(S["s_lo"], 1)

                dve.wait_ge(S["params"], 48)
                split_w(0, 1)
                norm_inv(1)
                for k in range(KB):
                    v.scalar_tensor_tensor(hm[:, k, :], x[:, k, :], C("mix_pre", k), rs, MUL, MUL).then_inc(S["norm_h"], 1)
                split_s(hm_lo, hm, hm_hi, KB)
                o.go(v.memset(pr[:, :, 0:1], 0.0))
                o.go(v.memset(state[:], 0.0))
                for m in range(NT + RP):
                    if m + 2 < C_GATE:
                        split_w(m + 2)
                    evac(nsa[:, m, HALF:TOK] if m < NT else pr[:, m - NT, 1 + HALF:1 + TOK])

                def mix(q, n, cur, prev):
                    q.do(v.tensor_tensor(dif[:, :, 0:n], prev, cur, SUB))
                    q.do(v.tensor_tensor(dif[:, :, 0:n], dif[:, :, 0:n], wide(C("mu"), n), MUL))
                    q.do(v.tensor_tensor(xs[:, :, 0:n], dif[:, :, 0:n], cur, ADD))

                def key_squares(q, n):
                    q.do(v.tensor_tensor(kk[:, :, 0:n], xs[:, RJ:2 * RJ, 0:n], wide(C("k_k"), n), MUL))
                    q.do(v.tensor_tensor(t0[:, :, 0:n], kk[:, :, 0:n], kk[:, :, 0:n], MUL))

                def keys(q, n, b_out):
                    q.do(v.tensor_scalar(t1[:, :, 0:n], t1[:, :, 0:n], 1e-12, None, MAX))
                    q.do(v.reciprocal(t1[:, :, 0:n], t1[:, :, 0:n]))
                    q.do(v.tensor_tensor(kk[:, :, 0:n], kk[:, :, 0:n], t1[:, :, 0:n], MUL))
                    q.do(v.scalar_tensor_tensor(t0[:, :, 0:n], aa[:, :, 0:n], -1.0, wide(C("k_a"), n), ADD, MUL))
                    q.do(v.scalar_tensor_tensor(km[:, :, 0:n], t0[:, :, 0:n], 1.0, xs[:, RJ:2 * RJ, 0:n], ADD, MUL))
                    q.go(v.tensor_tensor(b_out, kk[:, :, 0:n], aa[:, :, 0:n], MUL))
                    q.do(v.tensor_tensor(t1[:, :, 0:n], xs[:, 0:RJ, 0:n], km[:, :, 0:n], MUL))
                    q.do(v.tensor_tensor(t1[:, :, 0:n], t1[:, :, 0:n], wide(C("r_k"), n), MUL))

                def finish(q, n, rkv, dst):
                    q.do(v.tensor_tensor(kk[:, :, 0:n], kk[:, :, 0:n], t1[:, :, 0:n], MUL))
                    q.do(v.tensor_tensor(kk[:, :, 0:n], kk[:, :, 0:n], wide(C("lnw"), n), MUL))
                    q.do(v.tensor_tensor(kk[:, :, 0:n], kk[:, :, 0:n], wide(C("lnb"), n), ADD))
                    q.do(v.tensor_tensor(t0[:, :, 0:n], rkv, xs[:, 2 * RJ:3 * RJ, 0:n], MUL))
                    q.do(v.tensor_tensor(kk[:, :, 0:n], kk[:, :, 0:n], t0[:, :, 0:n], ADD))
                    q.do(v.tensor_tensor(dst, kk[:, :, 0:n], gg[:, :, 0:n], MUL))

                dve.wait_ge(S["evac_a"], NT + RP)
                dve.wait_ge(S["evac_v"], NT + RP)
                dve.wait_ge(S["trig_ok"], 16)
                for n, tile in enumerate((0, 1, 2, 3, 4, 6, 8)):
                    scale = HD ** -0.5 if tile < 4 else 1.0
                    o.go(v.scalar_tensor_tensor(tr, nsa[:, tile, :], scale, trig[:, 0, :], MUL, MUL))
                    dve.wait_ge(S["rope_mm"], n + 1)
                    o.do(v.scalar_tensor_tensor(halves(tr2), bank2(0), scale, halves(trig[:, 1, :]), MUL, MUL))
                    o.do(v.tensor_tensor(nsa[:, tile, :], tr, tr2, ADD))
                    o.tell(S["rope_ok"])
                o.tell(S["nsa_ready"])

                dve.wait_ge(S["kcp_ok"], 1)
                dve.wait_ge(S["evac_a"], NT + RP)
                dve.wait_ge(S["evac_v"], NT + RP)
                mix(o, DEC, pr[:, :, 1 + SEQ:1 + TOK], prev_s)
                key_squares(o, DEC)
                o.tell(S["rs_x"])
                dve.wait_ge(S["rs_act"], 2)
                bs = cum[:, :, 0:DEC]
                keys(o, DEC, bs)
                o.do(v.tensor_scalar(pex[:, :, 0:DEC], kk[:, :, 0:DEC], -1.0, None, MUL))
                o.tell(S["rs_prep"])
                rks = dif[:, 0:RJ, 0:DEC]
                over = lambda a: a.unsqueeze(3).to_broadcast((P, RJ, DEC, CH))
                b47 = ps[:, 4:8, :].rearrange("p j (b n) -> p j b n", b=DEC)
                dve.wait_ge(S["rs_mm"], 2)
                dve.wait_ge(S["loads_s"], 16)
                o.go(v.tensor_copy(rks, b4(3, DEC)))
                o.go(v.tensor_tensor(s1, b47, over(bs), MUL))
                o.tell(S["rs_prep"])
                o.do(v.tensor_tensor(ss, ss, over(pin[:, :, 0:DEC]), MUL))
                o.do(v.tensor_tensor(ss, ss, s1, ADD))
                dve.wait_ge(S["rs_mm"], 3)
                o.do(v.tensor_tensor(s1, b47, over(km[:, :, 0:DEC]), MUL))
                o.tell(S["rs_prep"])
                o.do(v.tensor_tensor(ss, ss, s1, ADD))
                o.tell(S["rs_prep"])
                dve.wait_ge(S["rs_mm"], 4)
                o.go(v.tensor_copy(kk[:, :, 0:DEC], b4(0, DEC)))
                o.tell(S["rs_prep"])
                dve.wait_ge(S["rs_mm"], 5)
                o.do(v.tensor_tensor(kk[:, :, 0:DEC], kk[:, :, 0:DEC], b4(1, DEC), SUB))
                o.do(v.tensor_tensor(t0[:, :, 0:DEC], kk[:, :, 0:DEC], kk[:, :, 0:DEC], MUL))
                o.tell(S["rs_prep"])
                dve.wait_ge(S["rs_mm"], 6)
                o.do(v.tensor_scalar(t1[:, :, 0:DEC], b4(1, DEC), LNX_EPS, None, ADD))
                o.do(v.reciprocal(t1[:, :, 0:DEC], t1[:, :, 0:DEC]))
                o.tell(S["rs_var"])
                dve.wait_ge(S["rs_act"], 3)
                finish(o, DEC, rks, hm[:, RJ:2 * RJ, SEQ:TOK])
                o.tell(S["rs_out"])
                dve.wait_ge(S["rs_stored"], 32)
                dve.wait_ge(S["gate_ev"], NQ + 1)

                flat = lambda a: a.rearrange("p j t -> p (j t)")
                in2 = lambda a: a.rearrange("p j (c t) -> p j c t", c=2)
                bb = sw
                gm = K("gmask").unsqueeze(1).to_broadcast((P, RJ, P))
                lo = CONST["lev"][0]
                lev0 = cst[:, lo:lo + CH].unsqueeze(1).to_broadcast((P, RJ, CH))
                eye8 = eye.unsqueeze(1).to_broadcast((P, 2 * RJ, CH))
                z8, w8 = (a.rearrange("p c j t -> p (c j) t") for a in (zz, ww))
                bank8 = lambda b: ps[:, b, :].rearrange("p (a t) -> p a t", t=CH)

                def rwkv(sc, stage):
                    at_sc = lambda name, n: (T[name], PER_SC[name] * sc + n)
                    if stage == "mix":
                        mix(o, SC, pr[:, :, sc * SC + 1:(sc + 1) * SC + 1], pr[:, :, sc * SC:(sc + 1) * SC])
                        o.tell(T["x1"])
                    elif stage == "squares":
                        key_squares(o, SC)
                        o.tell(T["x1"])
                    elif stage == "decay":
                        dve.wait_ge(*at_sc("sig1", 1))
                        o.do(v.tensor_scalar(sw, sw, LD, None, MUL))
                        o.do(v.tensor_tensor_scan(flat(cum), K("scan"), flat(sw), 0.0, MUL, ADD))
                        o.go(v.tensor_tensor(pex, cum, sw, SUB))
                        o.tell(T["ld_ok"])
                    elif stage == "keys":
                        dve.wait_ge(*at_sc("root1", 1))
                        keys(o, SC, bb)
                        o.tell(T["prep"])
                    elif stage == "scaled":
                        dve.wait_ge(*at_sc("exp1", 1))
                        o.go(v.scalar_tensor_tensor(ar[:, :, :, 0, :], in2(kk), -1.0, in2(pex), MUL, MUL))
                        o.go(v.tensor_tensor(ar[:, :, :, 1, :], in2(xs[:, 0:RJ, :]), in2(pin), MUL))
                        o.go(v.tensor_tensor(bt, bb, piv, MUL))
                        o.go(v.tensor_tensor(kt, km, piv, MUL))
                        dve.wait_ge(*at_sc("kk1", 2))
                        o.go(v.tensor_copy(rk, b4(3)))
                        o.tell(T["prep"])
                    elif stage == "pairs":
                        for c in range(2):
                            dve.wait_ge(*at_sc("gmm", c + 1))
                            for n, dst in ((0, gb), (1, gk)):
                                o.go(v.tensor_tensor(dst[:, c, :, :, :].rearrange("p j a t -> p j (a t)"), b4(n + 2 * c), gm, MUL))
                            o.tell(T["gmask"])
                    elif stage == "turn":
                        for c in range(2):
                            o.go(v.tensor_tensor(zz[:, c, :, :], gb[:, c, :, 0, :], lev0, MUL))
                        dve.wait_ge(*at_sc("nmm", 1))
                        o.do(v.tensor_tensor(w8, bank8(0), K("lev0t").unsqueeze(1).to_broadcast((P, 2 * RJ, CH)), MUL))
                        o.go(v.tensor_tensor(z8, z8, eye8, ADD))
                        o.go(v.tensor_tensor(w8, w8, eye8, ADD))
                        o.tell(T["inv_z"])
                    elif stage[0] == "double":
                        lv = stage[1]
                        dve.wait_ge(*at_sc("inv_d", lv))
                        o.go(v.tensor_tensor(z8, z8, bank8(1), ADD))
                        if lv < LEVELS - 1:
                            o.go(v.tensor_tensor(w8, w8, bank8(2), ADD))
                        o.tell(T["inv_z"])
                    elif stage[0] == "advance":
                        c = stage[1]
                        dve.wait_ge(*at_sc("ds_mm", c + 1))
                        o.do(v.tensor_tensor(state[:], state[:], b4(3, CH), ADD))
                        e = c * CH + CH - 1
                        o.go(v.tensor_tensor(state[:], state[:], pin[:, :, e:e + 1].to_broadcast((P, RJ, CH)), MUL))
                        o.tell(T["s_ok"])
                    elif stage == "mean":
                        dve.wait_ge(*at_sc("mean_mm", 1))
                        o.do(v.tensor_tensor(kk, kk, b4(0), SUB))
                        o.go(v.tensor_tensor(t0, kk, kk, MUL))
                        o.tell(T["yc"])
                    elif stage == "var":
                        dve.wait_ge(*at_sc("var_mm", 1))
                        o.do(v.tensor_scalar(t1, b4(1), LNX_EPS, None, ADD))
                        o.go(v.reciprocal(t1, t1))
                        o.tell(T["var_v"])
                    elif stage == "out":
                        dve.wait_ge(*at_sc("var_a", 1))
                        finish(o, SC, rk, hm[:, RJ:2 * RJ, sc * SC:(sc + 1) * SC])

                def att(n, step):
                    t, i, g = UNITS[n]
                    h, w = g * PER + i, (t + 1) * P
                    if step == "cmp_scores":
                        dve.wait_ge(S["at_mm"], 3 * n + 2)
                        lo = CONST["cmask"][0] + n * NCP
                        mask = cst[:, lo:lo + NCP].unsqueeze(1).to_broadcast((P, HEADS, NCP))
                        o.do(v.tensor_tensor(pc, ps[:, 6, 0:HEADS * NCP].rearrange("p (h n) -> p h n", h=HEADS), mask, ADD))
                        o.do(v.tensor_reduce(cm[:, 0, :], pc, AX, MAX))
                        o.do(v.tensor_scalar(cm[:, 0, :], cm[:, 0, :], NEG / 10, None, MAX))
                        o.go(v.tensor_tensor(pc, pc, wide(cm[:, 0, :], NCP), SUB))
                        o.tell(S["pc_sub"])
                    elif step == "cmp_turn":
                        dve.wait_ge(S["pc_exp"], n + 1)
                        o.do(v.tensor_reduce(cm[:, 1, :], pc, AX, ADD))
                        o.do(v.tensor_scalar(cm[:, 1, :], cm[:, 1, :], 1e-30, None, MAX))
                        o.do(v.reciprocal(cm[:, 2, :], cm[:, 1, :]))
                        o.do(v.tensor_tensor(cm[:, 2, :], cm[:, 2, :], gates[:, n, 0:24:3], MUL))
                        o.go(v.tensor_tensor(pc, pc, wide(cm[:, 2, :], NCP), MUL))
                        o.tell(S["pc_ok"])
                    elif step == "cmp_done":
                        dve.wait_ge(S["at_mm"], 3 * n + 3)
                        for half in range(2):
                            o.go(v.tensor_copy(pcp[0:NCP, 4 * half:4 * half + 4, :], ps[0:NCP, 6 - 2 * half, :].rearrange("p (h n) -> p h n", h=4)))
                        o.tell(S["pcp_ok"])
                    elif step == "scores":
                        dve.wait_ge(S["sc_mm"], n + 1)
                        d = ps[:, 4:6, t * P:(t + 1) * P]
                        o.do(v.tensor_tensor(d, d, K("causal").unsqueeze(1).to_broadcast((P, 2, P)), ADD))
                        o.go(v.tensor_reduce(nm, ps[:, 4:6, 0:w], AX, MAX, negate=True))
                        o.tell(S["mx"])
                    elif step == "turn":
                        dve.wait_ge(S["ex"], n + 1)
                        o.do(v.tensor_scalar(sums, sums, 1e-30, None, MAX))
                        o.do(v.reciprocal(rr, sums))
                        o.do(v.tensor_tensor(rr, rr, gates[:, t, 3 * h + 1:3 * h + 3], MUL))
                        o.go(v.tensor_tensor(pp[:, :, 0:w], pp[:, :, 0:w], wide(rr, w), MUL))
                        o.tell(S["sc_v"])
                    elif step == "values":
                        dve.wait_ge(S["pt_mm"], n + 1)
                        o.go(v.tensor_copy(ppt[:, 1, 0:w], ps[:, 5, 0:w]))
                        o.tell(S["pt_ev_v"])
                    elif step == "heads_out":
                        dve.wait_ge(S["pv"], HEADS * (n + 1))
                        o.go(v.tensor_copy(hm[:, 0:PER, n * P:(n + 1) * P], b4(7)))
                        o.tell(S["o_ev"])

                for side, n, step in PAIRED:
                    (rwkv if side == "rwkv" else att)(n, step)
                o.tell(S["phase_ok"])

                o.do(v.memset(qpad, 0.0))
                qflat = qpad.rearrange("p b n -> p (b n)")
                for i in range(PER):
                    for g in range(GROUPS):
                        r = slice(g * HD, (g + 1) * HD)
                        h = g * PER + i
                        step = ROWS + HEADS
                        o.go(v.tensor_copy(qflat[r, h:h + step * (DEC - 1) + 1:step], nsa[r, i, SEQ:TOK]))
                o.tell(S["qpad_ok"])
                R = slice(0, ROWS)
                dve.wait_ge(S["gs_ready"], 16)

                def weigh(p, den, col, gate):
                    o.do(v.tensor_scalar(sm[R, den:den + 1], sm[R, den:den + 1], 1e-30, None, MAX))
                    o.do(v.reciprocal(sm[R, col:col + 1], sm[R, den:den + 1]))
                    if gate is not None:
                        o.do(v.tensor_tensor(sm[R, col:col + 1], sm[R, col:col + 1], gate_s[:, gate:gate + 1], MUL))
                    o.do(v.tensor_scalar(p, p, sm[R, col:col + 1], None, MUL))

                dve.wait_ge(S["ss_mm"], 1)
                o.go(v.tensor_copy(swin[R, 1:WIN], ps[R, 0, 1:WIN]))
                o.go(v.tensor_copy(swin[R, 0:1], ps[R, 1, 0:1]))
                o.go(v.tensor_copy(vnew[0:DEC, :, :], ps[0:DEC, 2, 0:2 * P].rearrange("p (a n) -> p a n", a=2)))
                o.settle()
                o.go(v.tensor_reduce(sm[R, 0:1], swin[R, :], AX, MAX, negate=True))
                o.tell(S["ss_v"])
                dve.wait_ge(S["ss_a"], 1)
                weigh(swin[R, :], 1, 2, 2)
                o.do(v.tensor_scalar(diag[R, 1, :], ident[R, 0:ROWS], swin[R, 0:1], None, MUL))
                o.go(v.memset(swin[R, 0:1], 0.0))
                o.tell(S["ss_v"])
                dve.wait_ge(S["ss_mm"], 2)
                o.go(v.tensor_copy(ptw.rearrange("p k n -> p (k n)"), ps[:, 3, 0:4 * ROWS]))
                o.go(v.tensor_copy(pnew[0:DEC, 1, :], ps[0:DEC, 4, 0:ROWS]))
                o.tell(S["ss_v"])
                for u in range(1, CMP_U + 1):
                    dve.wait_ge(S["cmp_o"], u)
                    b = 2 * (u - 1)
                    o.go(v.tensor_copy(kcs[:, b:b + 2, :], ps[:, 2, 0:2 * NCS].rearrange("p (b n) -> p b n", b=2)))
                    o.go(v.tensor_copy(vcs[0:NCS, b:b + 2, :], ps[0:NCS, 3, 0:2 * P].rearrange("p (b n) -> p b n", b=2)))
                    o.tell(S["cmp_k"])
                dve.wait_ge(S["ss_mm"], 3)
                o.go(v.tensor_reduce(sm[R, 4:5], ps[R, 0, 0:NCS], AX, MAX, negate=True))
                o.tell(S["ss_v"])
                dve.wait_ge(S["ss_a"], 2)
                weigh(pcs[R, 0:NCS], 5, 6, None)
                o.tell(S["ss_v"])
                dve.wait_ge(S["ss_mm"], 4)
                o.go(v.tensor_copy(impt[0:NCS, :], ps[0:NCS, 1, 0:ROWS]))
                o.go(v.tensor_scalar(pcs[R, 0:NCS], pcs[R, 0:NCS], gate_s[:, 0:1], None, MUL))
                o.tell(S["ss_v"])
                dve.wait_ge(S["ss_mm"], 5)
                o.go(v.tensor_copy(pct[0:NCS, :], ps[0:NCS, 3, 0:ROWS]))
                o.do(v.tensor_tensor(work[R, :], ps[R, 2, 0:NSEL], K("keep", ROWS), MUL))
                o.tell(S["ss_v"])
                o.do(v.tensor_tensor(work[R, :], work[R, :], K("force", ROWS), ADD))
                for _ in range(2):
                    o.do(v.max(top[R, :], work[R, :]))
                    o.do(v.match_replace(work[R, :], top[R, :], work[R, :], 2 * NEG))
                o.do(v.tensor_scalar(imp[R, :], work[R, :], 1.5 * NEG, NEG, ALU.is_ge, MUL))
                dve.wait_ge(S["ss_mm"], 6)
                for k in range(4):
                    bias = imp[R, 8 * k:8 * k + 8].unsqueeze(2).to_broadcast((ROWS, 8, SELB))
                    o.go(v.tensor_tensor(ssel[R, 8 * k:8 * k + 8, :], ps[R, k, :].rearrange("p (a b) -> p a b", b=SELB), bias, ADD))
                fs = ssel.rearrange("p a b -> p (a b)")
                o.do(v.tensor_tensor(fs[R, PAST:PAST + 1], ps[R, 4, 0:1], imp[R, NSEL - 1:NSEL], ADD))
                o.do(v.tensor_reduce(sm[R, 8:9], fs[R, 0:PAST + 1], AX, MAX, negate=True))
                o.tell(S["ss_v"])
                dve.wait_ge(S["ss_a"], 3)
                weigh(fs[R, 0:PAST + 1], 9, 10, 1)
                o.do(v.tensor_scalar(diag[R, 0, :], ident[R, 0:ROWS], fs[R, PAST:PAST + 1], None, MUL))
                o.tell(S["ss_v"])
                dve.wait_ge(S["ss_mm"], 7)
                o.go(v.tensor_copy(pt_s.rearrange("p (a k) n -> p a (k n)", a=2), ps[:, 0:2, :]))
                o.go(v.tensor_copy(pnew[0:DEC, 0, :], ps[0:DEC, 2, 0:ROWS]))
                o.tell(S["ss_v"])
                dve.wait_ge(S["ss_mm"], 8)
                for g in range(GROUPS):
                    r = slice(g * HD, (g + 1) * HD)
                    src = ps[r, 7, 0:ROWS].rearrange("p (b h) -> p h b", h=HEADS)[:, g * PER:(g + 1) * PER, :]
                    o.go(v.tensor_copy(hm[r, 0:PER, SEQ:TOK], src))
                o.tell(S["mixed"])

                split_w(C_OUT, C_OUT + 1)
                split_s(hm_lo, hm, hm_hi, KB)
                for m in range(KB):
                    split_w(C_OUT + m + 2)
                    evac(hf[:, m, HALF:TOK])

                def add_normed(src, g):
                    for k in range(KB):
                        o.go(v.scalar_tensor_tensor(src[:, k, :], src[:, k, :], C(g, k), rs, MUL, MUL))
                    o.settle()
                    for k in range(KB):
                        o.go(v.tensor_tensor(x[:, k, :], x[:, k, :], src[:, k, :], ADD))
                    o.settle()

                norm_inv(2)
                add_normed(hf, "mix_post")
                o.tell(S["norm_h"])
                norm_inv(3)
                for k in range(KB):
                    v.scalar_tensor_tensor(hm[:, k, :], x[:, k, :], C("ffn_pre", k), rs, MUL, MUL).then_inc(S["norm_h"], 1)
                split_s(hm_lo, hm, hm_hi, KB)
                o.do(v.memset(gx[:, :, 0:2], 0.0))
                dve.wait_ge(S["loads_s"], 32)

                def conv(i):
                    s = i % 2
                    n = NT + RP + KB + 2 * i + 1
                    dve.wait_ge(S["evac_a"], n)
                    if i >= 2:
                        dve.wait_ge(S["ffn_h"], i - 1)
                    p_, s_ = cv[:, s, 0:SEQ], cv[:, s, SEQ:TOK]
                    o.go(v.tensor_scalar(p_, gx[:, s, 0:SEQ], C("cw0", i), C("cb", i), MUL, ADD))
                    o.do(v.tensor_scalar(s_, cprev[:, i, 0, :], C("cw0", i), C("cb", i), MUL, ADD))
                    o.go(v.scalar_tensor_tensor(p_, gx[:, s, 1:1 + SEQ], C("cw1", i), p_, MUL, ADD))
                    o.do(v.scalar_tensor_tensor(s_, cprev[:, i, 1, :], C("cw1", i), s_, MUL, ADD))
                    o.go(v.scalar_tensor_tensor(cv[:, s, :], gx[:, s, 2:2 + TOK], C("cw2", i), cv[:, s, :], MUL, ADD))
                    o.tell(S["ffn_c"])

                for i in range(FT):
                    split_w(C_UP + 2 * i + 2)
                    dve.sem_inc(S["evac_v"], 1)
                    conv(i)
                    n_dense[0] += 1
                    n = n_dense[0]
                    split_w(C_UP + 2 * i + 3)
                    dve.wait_ge(S["w_used"], tile_done(n))
                    dve.wait_ge(S["ffn_act"], i + 1)
                    o.do(v.tensor_tensor(halves(hf[:, i, :]), halves(cv[:, i % 2, :]), bank2(2 * (n % 3)), MUL))
                    dve.sem_inc(S["evac_v"], 1)
                    dve.sem_inc(S["ffn_h"], 1)
                    n_dense[0] += 1
                split_s(hf_lo, hf, hf_hi, FT)
                for m in range(KB):
                    split_w(*(C_DOWN + 3 * m + i for i in (2, 3, 4)))
                    evac(hm[:, m, HALF:TOK])
                norm_inv(4)
                add_normed(hm, "ffn_post")
                meet(dve, "v", S["arrive"])


HEAD_ORDER = [g * PER + i for i in range(PER) for g in range(GROUPS)]


def tiles(a):
    return np.swapaxes(a.reshape(a.shape[:-1] + (-1, P)), -1, -2)


def weight_chunks(w_in, w_out, w_up, w_down):
    q_cols = np.concatenate([np.arange(h * HD, (h + 1) * HD) for h in HEAD_ORDER])
    nsa_w = HEADS * HD
    kv_w = 6 * P
    out = np.zeros((DEPTH, N_CHUNK, P, KB, P), w_in.dtype)

    def put(at, w):
        k, m = w.shape[1] // P, w.shape[2] // P
        t = w.reshape(DEPTH, k, P, m, P).transpose(0, 3, 2, 1, 4)
        for i in range(m):
            for c in range(-(-k // KB)):
                part = t[:, i, :, c * KB:(c + 1) * KB]
                out[:, at, :, 0:part.shape[2]] = part
                at += 1
        return at

    wq = w_in[:, :, q_cols]
    rest = w_in[:, :, nsa_w:nsa_w + kv_w]
    gate = w_in[:, :, nsa_w + kv_w:nsa_w + kv_w + 24]
    n = put(0, np.concatenate([wq, rest, w_in[:, :, nsa_w + kv_w + 24:]], 2))
    flat = out.reshape(DEPTH, N_CHUNK, P, KB * P)
    flat[:, n, :, 0:KB * 24] = gate.reshape(DEPTH, KB, P, 24).transpose(0, 2, 1, 3).reshape(DEPTH, P, KB * 24)
    n = put(n + 1, np.concatenate([w_out[:, q_cols], w_out[:, nsa_w:]], 1))
    up = np.stack([w_up[:, :, 0:FF].reshape(DEPTH, D_MODEL, FT, P), w_up[:, :, FF:].reshape(DEPTH, D_MODEL, FT, P)], 3)
    n = put(n, up.reshape(DEPTH, D_MODEL, 2 * FF))
    n = put(n, w_down)
    assert n == N_CHUNK
    return flat


OUTS = {
    "y": (KB, P, TOK), "kv": (DEPTH, P, 6 * TOK), "win_old": (DEPTH, DEC, (WIN - 1) * 2 * P),
    "wkv_p": (DEPTH, P, RJ * CH), "wkv_s": (DEPTH, P, RJ * DEC * CH), "shift": (DEPTH, P, RP * (1 + DEC)),
    "conv_p": (DEPTH, P, FT * 2), "conv_s": (DEPTH, P, FT * 2 * DEC),
}


def kernel(x_prompt, x_sample, cache_kv, page_table, state_win, state_wkv, state_shift, state_conv,
           norm_mix_pre, norm_mix_post, norm_ffn_pre, norm_ffn_post, w_in, w_out,
           cmp_pe, cmp_w1, cmp_w2, rwkv_mu, rwkv_w0, rwkv_w_up, rwkv_a0, rwkv_a_up, rwkv_g_up,
           rwkv_k_k, rwkv_k_a, rwkv_r_k, rwkv_lnx_w, rwkv_lnx_b,
           ffn_w_up, ffn_conv_w, ffn_conv_b, ffn_w_down):
    import concourse.bacc as bacc
    from concourse.bass_utils import run_bass_kernel_spmd

    arr = lambda a: np.asarray(a)
    xp, xs = arr(x_prompt)[0], arr(x_sample)[:, 0]
    cache = arr(cache_kv).reshape(DEPTH * N_POOL, PAGE, 4, P)
    win = arr(state_win)
    fm = cache.transpose(0, 3, 2, 1)
    conv_w = arr(ffn_conv_w)
    lora = np.concatenate([np.concatenate([arr(rwkv_w_up), arr(rwkv_a_up)], 1), arr(rwkv_g_up)], 2)
    wkv = arr(state_wkv).reshape(DEPTH, DEC, RJ, 2, HD, HD)
    cols = {"mix_pre": norm_mix_pre, "mix_post": norm_mix_post, "ffn_pre": norm_ffn_pre, "ffn_post": norm_ffn_post,
            "mu": rwkv_mu, "w0": rwkv_w0, "a0": rwkv_a0, "k_k": rwkv_k_k, "k_a": rwkv_k_a,
            "r_k": arr(rwkv_r_k).reshape(DEPTH, RW), "lnw": rwkv_lnx_w, "lnb": rwkv_lnx_b,
            "cw0": conv_w[:, 0], "cw1": conv_w[:, 1], "cw2": conv_w[:, 2], "cb": ffn_conv_b}
    inputs = {
        "consts": constants()[0],
        "trig": constants()[1],
        "pages": arr(page_table).reshape(1, -1),
        "x": np.concatenate([xp, xs], 0).T.reshape(KB, P, TOK),
        "cols": np.concatenate([tiles(arr(cols[n])) for n in COLS], 2),
        "shift": arr(state_shift).reshape(DEPTH, DEC, RP, P).transpose(0, 3, 2, 1).reshape(DEPTH, P, -1),
        "lora": lora,
        "w": weight_chunks(arr(w_in), arr(w_out), arr(ffn_w_up), arr(ffn_w_down)),
        "wkv": wkv.transpose(0, 3, 5, 2, 1, 4).reshape(DEPTH, P, -1),
        "w1": arr(cmp_w1).transpose(0, 1, 3, 2, 4).reshape(DEPTH, 2, HD, -1),
        "w2": arr(cmp_w2),
        "pe": arr(cmp_pe).transpose(0, 1, 3, 2),
        "win": win[:, :, 1:].reshape(DEPTH, DEC, -1),
        "kwin": win[:, :, :, 0].reshape(DEPTH, DEC, WIN, P).transpose(0, 1, 3, 2),
        "vwin": win[:, :, :, 1].reshape(DEPTH, DEC, 4, P, P).transpose(0, 1, 3, 2, 4).reshape(DEPTH, DEC, P, WIN),
        "kv_cmp": fm[:, :, 0:2].reshape(DEPTH * N_POOL, P, 2 * PAGE),
        "k_sel": fm[:, :, 2],
        "v_sel": cache[:, :, 3],
        "conv": arr(state_conv).reshape(DEPTH, DEC, 2, FT, P).transpose(0, 4, 3, 2, 1).reshape(DEPTH, P, -1),
    }
    nc = bacc.Bacc("TRN2", target_bir_lowering=False, num_devices=1)
    arrays, I, O = {}, {}, {}
    for name, a in inputs.items():
        a = np.ascontiguousarray(a)
        arrays["in_" + name] = a
        I[name] = nc.dram_tensor("in_" + name, a.shape, mybir.dt.from_np(a.dtype), kind="ExternalInput").ap()
    for name, shape in OUTS.items():
        O[name] = nc.dram_tensor("out_" + name, shape, F32, kind="ExternalOutput").ap()
    build(nc, I, O)
    res = run_bass_kernel_spmd(nc, [arrays], core_ids=[0]).results[0]
    r = {n: np.asarray(res["out_" + n]) for n in OUTS}

    y = r["y"].reshape(D_MODEL, TOK).T
    kv = r["kv"].reshape(DEPTH, GROUPS, HD, 6, TOK).transpose(0, 4, 3, 1, 2)
    win_new = np.concatenate([r["win_old"].reshape(DEPTH, DEC, WIN - 1, 2, GROUPS, HD), kv[:, SEQ:, None, 4:6]], 2)
    back = lambda a: a.reshape(DEPTH, 2, HD, RJ, -1, HD).transpose(0, 4, 3, 1, 5, 2).reshape(DEPTH, -1, HEADS, HD, HD)
    shift = r["shift"].reshape(DEPTH, P, RP, 1 + DEC).transpose(0, 3, 2, 1).reshape(DEPTH, 1 + DEC, RP * P)
    conv_p = r["conv_p"].reshape(DEPTH, P, FT, 2).transpose(0, 3, 2, 1).reshape(DEPTH, 1, 2, FF)
    conv_s = r["conv_s"].reshape(DEPTH, P, FT, 2, DEC).transpose(0, 4, 3, 2, 1).reshape(DEPTH, DEC, 2, FF)
    outs = (y[None, 0:SEQ], y[SEQ:, None], kv[:, None, 0:SEQ, 0:4], kv[:, SEQ:, None, 0:4],
            kv[:, None, 0:SEQ, 4:6], win_new, back(r["wkv_p"]), back(r["wkv_s"]),
            shift[:, 0:1], shift[:, 1:], conv_p, conv_s)
    return tuple(np.ascontiguousarray(a) for a in outs)
```

```python
from contextlib import ExitStack
import math

import numpy as np
import concourse.bass as bass
from concourse import mybir

F32 = mybir.dt.float32
F32R = mybir.dt.float32r
I32 = mybir.dt.int32
ALU = mybir.AluOpType
ACT = mybir.ActivationFunctionType
AX = mybir.AxisListType.X

P = 128
D_MODEL, SEQ, DEPTH, DEC, PAST, PAGE = 1024, 512, 2, 8, 2048, 128
HD, HEADS, GROUPS = 64, 8, 2
PER = HEADS // GROUPS
TOK = SEQ + DEC
HALF = TOK // 2
KB = D_MODEL // P
PAGES = PAST // PAGE
N_POOL = (DEC * PAGES) + (DEC * PAGES) // 4
STRIDE, BLOCK = 16, 32
NCP = SEQ // STRIDE - 1
NCS = (PAST + 1) // STRIDE - 1
SELB = 64
NSEL = -(-(PAST + 1) // SELB)
WIN = 512
ROPE, THETA = HD // 4, 500000.0
RW = 512
RJ = RW // P
RP = 3 * RJ + 2
FF = 2816
FT = FF // P
NT = 10
CH = 64
SC = 128
NQ = SEQ // P
NEG = -1e30
ROWS = DEC * HEADS
EPS, LNX_EPS = 1e-6, 64e-5

C_IN, C_GATE = 0, NT + RP
C_OUT = C_GATE + 1
C_UP = C_OUT + KB
C_DOWN = C_UP + 2 * FT
DCH = [(0, 8), (8, 16), (16, FT)]
N_CHUNK = C_DOWN + 3 * KB
RING = 3
RING_HI = 2

COLS = {}
_n = 0
for _name, _w in [("mix_pre", KB), ("mix_post", KB), ("ffn_pre", KB), ("ffn_post", KB), ("mu", RP),
                  ("w0", RJ), ("a0", RJ), ("k_k", RJ), ("k_a", RJ), ("r_k", RJ), ("lnw", RJ),
                  ("lnb", RJ), ("cw0", FT), ("cw1", FT), ("cw2", FT), ("cb", FT)]:
    COLS[_name] = (_n, _n + _w)
    _n += _w
NCOL = _n

LEVELS = 6
CONST = {}
_n = 0
for _name, _w in [("ident", P), ("blk", P), ("causal", P), ("rot", P), ("gmask", P), ("scan", RJ * SC), ("eye", CH), ("lev", LEVELS * CH), ("lev0t", CH),
                  ("cmask", NQ * NCP), ("hit", NSEL), ("same", ROWS), ("selb", DEC),
                  ("keep", NSEL), ("force", NSEL)]:
    CONST[_name] = (_n, _n + _w)
    _n += _w
NCONST = _n


def constants():
    c = np.zeros((P, NCONST), np.float32)

    def put(name, a):
        lo, hi = CONST[name]
        c[:a.shape[0], lo:hi] = a

    p = np.arange(P)
    s64, t64 = np.arange(CH)[:, None], np.arange(CH)[None, :]
    two = lambda a: np.concatenate([a, a], 0)
    put("ident", np.eye(P))
    put("blk", (p[:, None] // HD == p[None, :] // HD).astype(np.float32))
    put("causal", np.where(p[None, :] <= p[:, None], 0.0, NEG))
    rot = np.zeros((P, P))
    half = ROPE // 2
    for g in range(GROUPS):
        for i in range(half):
            rot[g * HD + half + i, g * HD + i] = -1.0
            rot[g * HD + i, g * HD + half + i] = 1.0
    put("rot", rot)
    put("gmask", two(np.concatenate([s64 < t64, s64 <= t64], 1).astype(np.float32)))
    inv = np.float32(THETA) ** (-np.arange(half, dtype=np.float32) / np.float32(half))
    pos = np.concatenate([np.arange(SEQ), np.full(DEC, PAST)]).astype(np.float32)
    ang = (pos[None, :] * inv.astype(np.float32)[:, None]).astype(np.float32)
    cos, sin = np.ones((P, TOK), np.float32), np.zeros((P, TOK), np.float32)
    for g in range(GROUPS):
        for k in range(2):
            r = slice(g * HD + k * half, g * HD + (k + 1) * half)
            cos[r], sin[r] = np.cos(ang), np.sin(ang)
    put("scan", np.tile((np.arange(RJ * SC) % CH != 0).astype(np.float32), (P, 1)))
    put("eye", two(np.eye(CH)))
    lev = [(s64 // (2 << i) == t64 // (2 << i)) & (s64 // (1 << i) % 2 == 0) & (t64 // (1 << i) % 2 == 1)
           for i in range(LEVELS)]
    put("lev", two(np.concatenate(lev, 1).astype(np.float32)))
    put("lev0t", two(lev[0].T.astype(np.float32)))
    q = np.arange(SEQ).reshape(NQ, P).T
    end = np.arange(NCP) * STRIDE + BLOCK - 1
    put("cmask", np.where(end[None, None, :] <= q[:, :, None], 0.0, NEG).reshape(P, -1))
    c0, s0 = np.arange(NCS) * STRIDE, np.arange(NSEL) * SELB
    put("hit", ((c0[:, None] < s0 + SELB) & (c0[:, None] + BLOCK > s0)).astype(np.float32))
    r = np.arange(ROWS)
    put("same", (r[:, None] // PER == r[None, :] // PER).astype(np.float32))
    put("selb", (r[:, None] // HEADS == np.arange(DEC)[None, :]).astype(np.float32))
    cur = PAST // SELB
    forced = np.isin(np.arange(NSEL), [0, cur, cur - 1]).astype(np.float32)
    put("keep", np.tile(1.0 - forced, (ROWS, 1)))
    put("force", np.tile(forced * 1e9, (ROWS, 1)))
    return c, np.concatenate([cos, sin], 1)


PER_SC = {"x1": 2, "act1": 1, "lora1": 1, "sig1": 1, "ld_ok": 1, "kk1": 2, "root1": 1, "exp1": 1, "prep": 2,
          "gmm": 2, "gmask": 2, "nmm": 1, "mm_ok": LEVELS - 1, "inv_q": LEVELS - 1, "inv_qc": LEVELS - 1,
          "inv_d": LEVELS - 1, "inv_z": LEVELS, "tm_mm": 3, "tm_ev": 3, "rh_mm": 2, "rh_ev": 2, "u_mm": 2,
          "u_ev": 2, "ds_mm": 2, "s_ok": 2, "y_ev": 1, "mean_mm": 1, "yc": 1, "var_mm": 1, "var_v": 1, "var_a": 1}
UNITS = [(t, i, g) for t in range(NQ) for i in range(PER) for g in range(GROUPS)]


def paired():
    stages = [("mix", 0.5), ("squares", 1), ("lora", 0.5), ("decay", 0.5), ("keys", 1),
              ("scaled", 0.5), ("pairs", 2), ("turn", 2)]
    for lv, (a, b) in enumerate(((1.5, 3), (1, 2), (0.5, 3), (2, 1.5), (1.5, 1)), 1):
        stages += [(("invert", lv), a), (("double", lv), b)]
    for c, (a, b, d) in enumerate(((0.5, 3, 2), (2, 0, 2))):
        stages += [(("rhs", c), a), (("solve", c), b), (("advance", c), d)]
    stages += [("mean", 0.5), ("var", 3), ("out", 1)]
    att = []
    for t in range(NQ):
        att += [("att", t, "cmp_scores"), ("att", t, "cmp_turn"), ("att", t, "cmp_done")]
        for u in range(HEADS * t, HEADS * (t + 1)):
            if u == HEADS * t:
                att += [("att", u, "scores")]
            att += [("att", u, "turn"), ("att", u, "evac")]
            if u + 1 < HEADS * (t + 1):
                att += [("att", u + 1, "scores")]
            att += [("att", u, "values")]
        att += [("att", t, "heads_out")]
    total = SEQ // SC * sum(share for _, share in stages)
    out, share_so_far, done = [], 0, 0
    for sc in range(SEQ // SC):
        for stage, share in stages:
            out.append(("rwkv", sc, stage))
            share_so_far += share
            upto = round(len(att) * share_so_far / total)
            out += att[done:upto]
            done = max(done, upto)
    return out + att[done:]


PAIRED = paired()


class Order:

    def __init__(self, eng, sem):
        self.eng, self.sem, self.n = eng, sem, 0

    def go(self, ins):
        self.n += 1
        ins.then_inc(self.sem, 1)

    def settle(self):
        self.eng.wait_ge(self.sem, self.n)

    def do(self, ins):
        self.go(ins)
        self.settle()

    def tell(self, sem):
        self.settle()
        self.eng.sem_inc(sem, 1)


def build(nc, I, O):
    with ExitStack() as ctx:
        def sb(name, shape, dt=F32):
            return ctx.enter_context(nc.sbuf_tensor(name, shape, dt))

        def at_bytes(name, base, floats, shape):
            return nc.alloc_sbuf_tensor_at(name, shape, F32R, offset=base + 4 * floats)

        x = sb("x", [P, KB, TOK])
        hm = sb("hm", [P, KB, TOK])
        nsa = sb("nsa", [P, NT, TOK])
        ring_base = nc.sbuf_base
        ring = sb("ring", [P, RING, KB * P])
        ring_lo = at_bytes("ring_lo", ring_base, 0, [P, RING, KB * P])
        ring_hi = sb("ring_hi", [P, RING_HI, KB * P], F32R)
        cst = sb("cst", [P, NCONST])
        par = sb("par", [P, NCOL])
        cb = sb("cb", [P, 2])
        gates = sb("gates", [P, NQ + 1, 24])
        gate_s = sb("gate_s", [ROWS, 3])
        state = sb("state", [P, RJ, CH])
        rstd = sb("rstd", [P, 2, HALF])
        pages = sb("pages", [1, DEC * PAGES], I32)
        ones = sb("ones", [P, P])
        onesblk = sb("onesblk", [P, P])

        ARENA = 30900
        arena_base = nc.sbuf_base
        arena = sb("arena", [P, ARENA])
        where = [0]

        def at(*shape, reset=None):
            if reset is not None:
                where[0] = reset
            n = int(np.prod(shape))
            a = arena[:, where[0]:where[0] + n]
            where[0] += n
            assert where[0] <= ARENA, where[0]
            if len(shape) > 1:
                names = "abcde"[:len(shape)]
                a = a.rearrange(f"p ({' '.join(names)}) -> p {' '.join(names)}",
                                **{k: s for k, s in zip(names[1:], shape[1:])})
            return a

        sq = at(KB, TOK, reset=0)
        pr = at(RP, 1 + TOK, reset=0)
        prev_s = at(RP, DEC)
        lora = at(2 * RW)
        work0 = where[0]
        xs = at(RP, SC)
        dif = at(RP, SC)
        zz = at(2, RJ, CH, reset=where[0] - RP * SC)
        ww = at(2, RJ, CH)
        qq = at(2, RJ, CH)
        tanw = at(SC, reset=work0 + 2 * RP * SC)
        siggl = at(SC)
        gg = at(RJ, SC)
        kk = at(RJ, SC)
        t0 = at(RJ, SC)
        t1 = at(RJ, SC)
        rk = at(RJ, SC)
        pin = at(RJ, SC)
        dead = where[0]
        sw = at(RJ, SC)
        aa = at(RJ, SC)
        cum = at(RJ, SC)
        pex = at(RJ, SC)
        km = at(RJ, SC)
        piv = at(RJ, SC)
        gb = at(2, RJ, 2, CH, reset=dead)
        gk = at(2, RJ, 2, CH)
        btm = at(2, RJ, CH)
        ktm = at(2, RJ, CH)
        vtm = at(2, RJ, CH)
        ar = at(RJ, 2, 2, CH)
        bt = at(RJ, SC)
        kt = at(RJ, SC)
        mm = at(2, 2 * RJ, CH)
        rh = at(RJ, CH)
        uu = at(RJ, CH)
        side = where[0] + 50
        ss = at(RJ, DEC, CH, reset=dead + 6 * RJ * SC)
        s1 = at(RJ, DEC, CH)
        assert where[0] <= side
        w1 = at(2, BLOCK, P, reset=work0)
        w2 = at(2, P)
        pe_c = at(2, BLOCK)
        assert where[0] <= dead + 6 * RJ * SC
        trig = at(2, TOK, reset=20480)
        tr = at(TOK)
        tr2 = at(TOK)
        assert where[0] <= side
        vt = at(2, NQ, P, reset=side)
        kcp = at(NCP)
        vcp = at(P)
        hip = at(2, NCP)
        pp = at(2, WIN)
        ppt = at(2, WIN)
        staged = at(2, BLOCK, NCP + 1, reset=where[0] - 4 * WIN)
        pc = at(HEADS, NCP)
        pcp = at(HEADS, P)
        rows_p = pcp[:, 0:2, :]
        nm = at(2)
        sums = at(2)
        rr = at(2)
        cm = at(3, HEADS)
        cache = at(2, 8192, reset=0)
        w1s = at(2, STRIDE // 2, P)
        w2s = at(2, P)
        n0 = where[0]
        kcs = at(DEC, NCS)
        vcs = at(DEC, P)
        hid = at(2, 2, NCS + 1)
        ssel = at(NSEL, SELB, reset=n0)
        vo = at(DEC * P, reset=n0)
        at(72 + 512, reset=n0 + NSEL * SELB)
        qpad = at(DEC, ROWS)
        pt_s = at(PAGES, ROWS)
        swin = at(WIN)
        ptw = at(4, ROWS)
        pcs = at(NCS + 1)
        pct = at(ROWS)
        imp = at(NSEL)
        work = at(NSEL)
        top = at(8)
        diag = at(2, ROWS)
        pnew = at(2, ROWS)
        vnew = at(2, P)
        impt = at(ROWS)
        sm = at(16)
        part2 = at(GROUPS, 2, 2, NCS + 1)
        hf = at(FT, TOK, reset=0)
        gx = at(2, 2 + TOK)
        cv = at(2, TOK)
        cprev = at(FT, 2, DEC)
        cout = at(FT, 2)
        couts = at(FT, 2, DEC)
        sq2 = at(KB, TOK)

        sq3 = at(KB, TOK, reset=14272 + FT * TOK)

        HS = 20480
        hm_hi = at_bytes("hm_hi", arena_base, HS, [P, KB, TOK])
        hm_lo = at_bytes("hm_lo", arena_base, HS + KB * TOK, [P, KB, TOK])
        hf_lo = at_bytes("hf_lo", arena_base, 0, [P, FT, TOK])
        hf_hi = at_bytes("hf_hi", arena_base, 14272, [P, FT, TOK])

        ps = ctx.enter_context(nc.psum_tensor("ps", [P, 8, 512], F32))

        names = ("arrive v_own a_own p_own params w_used evac_a evac_v gate_mm gate_ev norm_sq norm_mm "
                 "norm_v norm_a norm_h rs_x rs_act rs_lora rs_prep rs_mm rs_var rs_out gs_ready loads_s stores "
                 "rope_mm rope_ok nsa_ready w1_zero w1_ready vt_mm vt_ev cmpp_mm gelu_p kcp_ok at_mm pc_sub pc_exp "
                 "pc_ok pcp_ok sc_mm mx ex sc_v pt_mm pt_ev pv o_ev qpad_ok ss_mm ss_v ss_a c_free "
                 "cmp_h cmp_act cmp_o cmp_k mixed ffn_c ffn_act ffn_h ffn_t w_hi w_lo s_hi s_lo trig_ok rs_stored phase_ok dif_ok cmp_b cmp_sum staged_a staged_v vwin_ready").split()
        S = {n: ctx.enter_context(nc.semaphore(n)) for n in names}
        T = {n: ctx.enter_context(nc.semaphore("rwkv_" + n)) for n in PER_SC}
        w_ready = [ctx.enter_context(nc.semaphore(f"w_ready{i}")) for i in range(RING)]
        c_ready = [ctx.enter_context(nc.semaphore(f"c_ready{i}")) for i in range(2)]
        go = {e: ctx.enter_context(nc.semaphore(f"go_{e}")) for e in ("pe", "v", "a", "p")}
        const_ok = ctx.enter_context(nc.semaphore("const_ok"))
        ones_ok = ctx.enter_context(nc.semaphore("ones_ok"))
        p_const = ctx.enter_context(nc.semaphore("p_const"))
        block = ctx.enter_context(nc.Block())

        def K(name, rows=P):
            lo, hi = CONST[name]
            return cst[0:rows, lo:hi]

        def C(name, i=None):
            lo, hi = COLS[name]
            return par[:, lo:hi] if i is None else par[:, lo + i:lo + i + 1]

        ident, blk = K("ident"), K("blk")
        eye = K("eye")

        def wide(col, n):
            return col.unsqueeze(2).to_broadcast((P, col.shape[1], n))

        def bank2(b):
            return ps[:, b:b + 2, 0:HALF]

        def halves(a):
            return a.rearrange("p (h n) -> p h n", h=2)

        def b4(i, n=SC):
            return ps[:, i, 0:RJ * n].rearrange("p (j n) -> p j n", j=RJ)

        HALVES = [(h, slice(h * HALF, (h + 1) * HALF)) for h in range(2)]
        CMP_U = DEC // 2
        N_UNIT = 1 + CMP_U + 4

        def tile_done(n):
            if n < NT + RP:
                return n + 1
            down = n - (NT + RP + KB + 2 * FT)
            return n + 2 if down < 0 else C_DOWN + 3 * (down + 1)

        def meet(eng, who, arrive):
            eng.sem_inc(arrive, 1)
            eng.wait_ge(go[who], 1)
            eng.sem_clear(go[who])

        def stage_views(c):
            for h in range(2):
                a = nsa[:, 4 + c, STRIDE * h:STRIDE * (h + NCP)].rearrange("p (n k) -> p k n", k=STRIDE)
                yield a, staged[:, c, STRIDE * h:STRIDE * (h + 1), 0:NCP]
            yield pe_c[:, c, :], staged[:, c, :, NCP]

        def cmp_half(u, c, g):
            return ps[:, (0 if u % 2 else 5) + c, g * 2 * P:(g + 1) * 2 * P]

        def cmp_part(u, g, part):
            b = 0 if u % 2 else 5
            a = ps[part * HD:(part + 1) * HD, b:b + 2, g * 2 * P:(g + 1) * 2 * P]
            return a.rearrange("p c (b n) -> p c b n", b=2)[:, :, :, part:part + NCS]

        def slot_free(eng, u):
            if u - 2 == 0:
                eng.wait_ge(S["c_free"], 1)
            elif 0 < u - 2 <= CMP_U:
                eng.wait_ge(S["cmp_h"], u - 2)
            elif u - 2 > CMP_U:
                eng.wait_ge(S["c_free"], 1 + u - 2 - CMP_U)

        def page_loads(eng, kind, l, u, half):
            slot, done = cache[:, u % 2, :], c_ready[u % 2]
            per = 1 if u <= CMP_U else 2
            for b in range(per * half, per * half + per):
                if u <= CMP_U:
                    sample, src = 2 * (u - 1) + b, I["kv_cmp"]
                    dst = slot.rearrange("p (b n t) -> p b n t", b=2, n=PAGES)
                else:
                    sample, src = 4 * ((u - CMP_U - 1) % 2) + b, I["k_sel"] if u < CMP_U + 3 else I["v_sel"]
                    dst = slot.rearrange("p (b n t) -> p b n t", b=4, n=PAGES)
                _, regs = nc.values_load_multi_w_load_instructions(
                    pages[0:1, sample * PAGES:(sample + 1) * PAGES], engines=[kind], min_val=0, max_val=N_POOL - 1)
                for i, r in enumerate(regs):
                    eng.dma_start(dst[:, b, i, :], src[l * N_POOL + r]).then_inc(done, 16)

        @block.sync
        def _(sp):
            sp.dma_start(cst[:], I["consts"]).then_inc(const_ok, 16)
            sp.dma_start(pages[:], I["pages"]).then_inc(const_ok, 16)
            sp.dma_start(x[:], I["x"].rearrange("k p t -> p k t")).then_inc(const_ok, 16)

            def host_meet(arrive, sems):
                sp.wait_ge(arrive, 4)
                for s in sems:
                    sp.sem_clear(s)
                for e in go:
                    sp.sem_inc(go[e], 1)

            def compression_weights(l):
                for c in range(2):
                    for g in range(GROUPS):
                        r = slice(g * HD, (g + 1) * HD)
                        sp.dma_start(w1[r, c, :, r], I["w1"][l, c].rearrange("d (k e) -> d k e", k=BLOCK)).then_inc(S["w1_ready"], 16)
                        sp.dma_start(w2[r, c, r], I["w2"][l, c]).then_inc(S["w1_ready"], 16)

            with sp.Fori(0, DEPTH) as l:
                sp.dma_start(par[:], I["cols"][l]).then_inc(S["params"], 16)
                sp.dma_start(prev_s, I["shift"][l].rearrange("p (a b) -> p a b", a=RP)).then_inc(S["params"], 16)
                sp.dma_start(lora, I["lora"][l]).then_inc(S["params"], 16)

                def chunk(n):
                    if n >= RING:
                        sp.wait_ge(S["w_used"], n - RING + 1)
                    sp.dma_start(ring[:, n % RING, :], I["w"][l, n]).then_inc(w_ready[n % RING], 16)

                for n in range(C_OUT):
                    chunk(n)
                sp.wait_ge(S["w1_zero"], 1)
                compression_weights(l)
                for c in range(2):
                    for g in range(GROUPS):
                        sp.dma_start(pe_c[g * HD:(g + 1) * HD, c, :], I["pe"][l, c]).then_inc(S["w1_ready"], 16)
                sp.wait_ge(S["w_used"], NT + RP)
                sp.dma_start(trig, I["trig"].rearrange("p (a t) -> p a t", a=2)).then_inc(S["trig_ok"], 16)
                sp.dma_start(ss, I["wkv"][l].rearrange("p (a b c) -> p a b c", a=RJ, b=DEC)).then_inc(S["loads_s"], 16)
                for n in range(C_OUT, C_OUT + RING):
                    chunk(n)
                sp.wait_ge(S["nsa_ready"], 1)
                sp.dma_start(O["kv"][l].rearrange("p (a b) -> p a b", a=6), nsa[:, 4:NT, :]).then_inc(S["stores"], 16)
                for b in range(DEC):
                    sp.dma_start(O["win_old"][l, b], I["win"][l, b]).then_inc(S["stores"], 16)
                sp.wait_ge(S["rs_out"], 1)
                sp.dma_start(O["wkv_s"][l].rearrange("p (a b c) -> p a b c", a=RJ, b=DEC), ss).then_inc(S["rs_stored"], 16)
                sp.dma_start(O["shift"][l].rearrange("p (a b) -> p a b", a=RP), pr[:, :, SEQ:SEQ + 1 + DEC]).then_inc(S["rs_stored"], 16)
                sp.wait_ge(S["rs_stored"], 32)
                sp.wait_ge(S["gate_ev"], NQ + 1)
                sp.dma_start(gate_s[:], gates[0:DEC, NQ, :].rearrange("b (h n) -> b h n", n=3)).then_inc(S["gs_ready"], 16)
                sp.wait_ge(S["phase_ok"], 1)
                sp.dma_start(O["wkv_p"][l].rearrange("p (a b) -> p a b", a=RJ), state[:]).then_inc(S["stores"], 16)

                for u in range(N_UNIT):
                    if u == 1:
                        sp.wait_ge(S["w1_zero"], 2)
                        sp.dma_start(w1s, I["w1_pairs"][l].rearrange("p (c k e) -> p c k e", c=2, e=P)).then_inc(S["w1_ready"], 16)
                        for c in range(2):
                            for g in range(GROUPS):
                                r = slice(g * HD, (g + 1) * HD)
                                sp.dma_start(w2s[r, c, r], I["w2"][l, c]).then_inc(S["w1_ready"], 16)
                    slot_free(sp, u)
                    slot, done = cache[:, u % 2, :], c_ready[u % 2]
                    if u == 0:
                        sp.dma_start(slot[:, 0:DEC * WIN].rearrange("p (b n) -> p b n", b=DEC),
                                     I["kwin"][l].rearrange("b p n -> p b n")).then_inc(done, 16)
                        sp.dma_start(slot[:, DEC * WIN:].rearrange("p (b n) -> p b n", b=DEC),
                                     I["vwin"][l].rearrange("b p n -> p b n")).then_inc(S["vwin_ready"], 16)
                    else:
                        page_loads(sp, mybir.EngineType.SP, l, u, 0)
                for n in range(C_OUT + RING, C_UP):
                    chunk(n)
                sp.wait_ge(S["mixed"], 1)
                sp.dma_start(cprev, I["conv"][l].rearrange("p (a b c) -> p a b c", a=FT, b=2)).then_inc(S["loads_s"], 16)
                for n in range(C_UP, N_CHUNK):
                    chunk(n)
                sp.wait_ge(S["ffn_t"], FT)
                sp.dma_start(O["conv_p"][l].rearrange("p (a b) -> p a b", a=FT), cout).then_inc(S["stores"], 16)
                sp.dma_start(O["conv_s"][l].rearrange("p (a b c) -> p a b c", a=FT, b=2), couts).then_inc(S["stores"], 16)
                sp.wait_ge(S["stores"], 16 * (4 + DEC))
                host_meet(S["arrive"], list(S.values()) + list(T.values()) + w_ready + c_ready)
            sp.dma_start(O["y"].rearrange("k p t -> p k t"), x[:]).then_inc(const_ok, 16)
            sp.wait_ge(const_ok, 64)

        @block.tensor
        def _(pe):
            mmul = nc.tensor.matmul

            def w_wait(n):
                if n == C_GATE:
                    pe.wait_ge(w_ready[n % RING], 16 * (n // RING + 1))
                else:
                    pe.wait_ge(S["w_lo"], n + 1 - (n > C_GATE))

            dense_n = [0]

            def dense_tile(chunks, hi, lo, first=None):
                b = 2 * (dense_n[0] % 3)
                if dense_n[0] >= 3:
                    pe.wait_ge(S["evac_a"], dense_n[0] - 2)
                    pe.wait_ge(S["evac_v"], dense_n[0] - 2)
                for ci, (n, k0, k1) in enumerate(chunks):
                    w_wait(n)
                    for k in range(k0, k1):
                        if first is not None:
                            pe.wait_ge(S["s_lo"], first + k + 1)
                        w = slice((k - k0) * P, (k - k0 + 1) * P)
                        wh, wl = ring_hi[:, n % RING_HI, w], ring_lo[:, n % RING, w]
                        for h, cols in HALVES:
                            out = ps[:, b + h, 0:HALF]
                            mmul(out, wh, hi[:, k, cols], start=(k == 0), stop=False)
                            mmul(out, wh, lo[:, k, cols], start=False, stop=False)
                            last = mmul(out, wl, hi[:, k, cols], start=False, stop=(ci == len(chunks) - 1 and k == k1 - 1))
                    last.then_inc(S["w_used"], 1)
                dense_n[0] += 1

            norm_n = [0]

            def norm(src):
                for k in range(KB):
                    norm_part(src, k)

            def norm_part(src, k):
                pe.wait_ge(S["norm_sq"], KB * norm_n[0] + k + 1)
                for h, cols in HALVES:
                    last = mmul(ps[:, 6 + h, 0:HALF], ones[:], src[:, k, cols], start=(k == 0), stop=(k == KB - 1))
                if k == KB - 1:
                    last.then_inc(S["norm_mm"], 1)
                    norm_n[0] += 1

            pe.wait_ge(ones_ok, 1)
            pe.wait_ge(const_ok, 48)
            with pe.Fori(0, DEPTH) as _l:
                dense_n[0] = norm_n[0] = 0
                norm(sq)
                for m in range(NT + RP):
                    dense_tile([(m, 0, KB)], hm_hi, hm_lo, 0 if m == 0 else None)
                w_wait(C_GATE)
                wg = ring[:, C_GATE % RING, 0:KB * 24].rearrange("p (k n) -> p k n", k=KB)
                for t in range(NQ + 1):
                    n = P if t < NQ else DEC
                    if t >= 1:
                        pe.wait_ge(S["gate_ev"], t)
                    for k in range(KB):
                        last = mmul(ps[0:n, 6, 0:24], hm[:, k, t * P:t * P + n], wg[:, k, :], start=(k == 0), stop=(k == KB - 1))
                    last.then_inc(S["gate_mm"], 1)
                pe.wait_ge(S["gate_mm"], NQ + 1)
                pe.sem_inc(S["w_used"], 1)

                pe.wait_ge(S["evac_a"], NT + RP)
                pe.wait_ge(S["evac_v"], NT + RP)
                for n, tile in enumerate((4, 0, 1, 2, 3, 6, 8)):
                    if n >= 3:
                        pe.wait_ge(S["rope_ok"], n - 2)
                    for h, cols in HALVES:
                        last = mmul(ps[:, 2 * (n % 3) + h, 0:HALF], K("rot"), nsa[:, tile, cols], start=True, stop=True)
                    last.then_inc(S["rope_mm"], 1)
                pe.wait_ge(S["gate_ev"], NQ + 1)
                for br in range(2):
                    for t in range(NQ):
                        last = nc.tensor.transpose(ps[:, 6 + br, t * P:(t + 1) * P], nsa[:, 7 + 2 * br, t * P:(t + 1) * P], ident)
                last.then_inc(S["vt_mm"], 1)
                pe.wait_ge(S["w1_ready"], 16 * 12)
                pe.wait_ge(S["rope_ok"], 7)
                pe.wait_ge(S["staged_v"], 1)
                pe.wait_ge(S["staged_a"], 1)
                for c in range(2):
                    for k in range(BLOCK):
                        last = mmul(ps[0:NCP + 1, 3, c * P:(c + 1) * P], staged[:, c, k, :], w1[:, c, k, :], start=(k == 0), stop=(k == BLOCK - 1))
                last.then_inc(S["cmpp_mm"], 1)
                pe.wait_ge(S["gelu_p"], 1)
                for c in range(2):
                    last = nc.tensor.transpose(ps[:, 2, c * (NCP + 1):(c + 1) * (NCP + 1)], rows_p[0:NCP + 1, c, :], ident[0:NCP + 1, 0:NCP + 1])
                last.then_inc(S["cmpp_mm"], 1)
                pe.wait_ge(S["gelu_p"], 2)
                mmul(ps[:, 4, 0:NCP], w2[:, 0, :], hip[:, 0, :], start=True, stop=True)
                mmul(ps[0:NCP, 5, 0:P], hip[:, 1, :], w2[:, 1, :], start=True, stop=True).then_inc(S["cmpp_mm"], 1)
                pe.wait_ge(S["kcp_ok"], 1)
                pe.wait_ge(S["vt_ev"], 1)

                def lora_products(n, ready, done):
                    pe.wait_ge(*ready)
                    for j in range(RJ):
                        c = slice(j * P, (j + 1) * P)
                        mmul(ps[:, 0, j * n:(j + 1) * n], lora[0:HD, c], tanw[0:HD, 0:n], start=True, stop=True)
                        mmul(ps[:, 1, j * n:(j + 1) * n], lora[HD:P, c], xs[HD:P, 3 * RJ, 0:n], start=True, stop=True)
                        last = mmul(ps[:, 2, j * n:(j + 1) * n], lora[:, RW + j * P:RW + (j + 1) * P], siggl[:, 0:n], start=True, stop=True)
                    last.then_inc(done, 1)

                pe.wait_ge(S["params"], 48)
                pe.wait_ge(S["loads_s"], 16)
                lora_products(DEC, (S["rs_act"], 1), S["rs_lora"])
                pe.wait_ge(S["rs_x"], 1)
                mmul(ps[:, 3, 0:RJ * DEC], blk, t0[:, :, 0:DEC], start=True, stop=True).then_inc(S["rs_mm"], 1)
                pe.wait_ge(S["rs_prep"], 1)
                mmul(ps[:, 3, 0:RJ * DEC], blk, t1[:, :, 0:DEC], start=True, stop=True)
                for part in range(2):
                    for j in range(RJ):
                        for b in range(DEC):
                            for h in range(2):
                                r = slice(h * HD, (h + 1) * HD)
                                if part == 0:
                                    last = mmul(ps[r, 4 + j, b * CH:(b + 1) * CH],
                                                pex[r, j, b:b + 1].to_broadcast((HD, HD)), ss[r, j, b, :], start=True, stop=True)
                                else:
                                    last = mmul(ps[r, 4 + j, b * CH:(b + 1) * CH],
                                                xs[r, 2 * RJ + j, b:b + 1].to_broadcast((HD, HD)), eye[r, :], start=True, stop=True)
                    last.then_inc(S["rs_mm"], 1)
                    pe.wait_ge(S["rs_prep"], 2 + part)
                pe.wait_ge(S["rs_prep"], 4)
                for j in range(RJ):
                    for b in range(DEC):
                        for h in range(2):
                            r = slice(h * HD, (h + 1) * HD)
                            last = mmul(ps[r, 0, j * DEC + b:j * DEC + b + 1], ss[r, j, b, :], xs[r, j, b:b + 1], start=True, stop=True)
                last.then_inc(S["rs_mm"], 1)
                for i, src in ((5, kk), (6, t0)):
                    pe.wait_ge(S["rs_prep"], i)
                    mmul(ps[:, 1, 0:RJ * DEC], onesblk[:], src[:, :, 0:DEC], start=True, stop=True).then_inc(S["rs_mm"], 1)
                pe.wait_ge(S["rs_out"], 1)

                HP = [slice(h * HD, (h + 1) * HD) for h in range(2)]

                def rwkv(sc, stage):
                    at_sc = lambda name, n: (T[name], PER_SC[name] * sc + n)
                    lv = stage[1]
                    if stage == "lora":
                        lora_products(SC, at_sc("act1", 1), T["lora1"])
                        pe.wait_ge(*at_sc("x1", 2))
                        mmul(ps[:, 3, :], blk, t0, start=True, stop=True).then_inc(T["kk1"], 1)
                    elif stage == "pairs":
                        pe.wait_ge(*at_sc("prep", 2))
                        for c in range(2):
                            cs = slice(c * CH, (c + 1) * CH)
                            for j in range(RJ):
                                for r in HP:
                                    mmul(ps[r, 2 * c, j * P:(j + 1) * P], bt[r, j, cs], ar[r, j, c, :, :], start=True, stop=True)
                                    last = mmul(ps[r, 2 * c + 1, j * P:(j + 1) * P], kt[r, j, cs], ar[r, j, c, :, :], start=True, stop=True)
                            last.then_inc(T["gmm"], 1)
                    elif stage == "turn":
                        pe.wait_ge(*at_sc("gmask", 1))
                        for cj in range(2 * RJ):
                            c, j = divmod(cj, RJ)
                            for r in HP:
                                last = mmul(ps[r, 0, cj * CH:(cj + 1) * CH], ar[r, j, c, 0, :], bt[r, j, c * CH:(c + 1) * CH], start=True, stop=True)
                        last.then_inc(T["nmm"], 1)
                        for n, src in ((1, bt), (2, kt), (3, xs[:, 2 * RJ:3 * RJ, :])):
                            if n == 2:
                                pe.wait_ge(*at_sc("gmask", 2))
                            for cj in range(2 * RJ):
                                c, j = divmod(cj, RJ)
                                for r in HP:
                                    last = mmul(ps[r, n, cj * CH:(cj + 1) * CH], src[r, j, c * CH:(c + 1) * CH], eye[r, :], start=True, stop=True)
                            last.then_inc(T["tm_mm"], 1)
                    elif stage[0] == "invert":
                        pe.wait_ge(*at_sc("inv_z", lv))
                        pe.wait_ge(*at_sc("mm_ok", lv))
                        for cj in range(2 * RJ):
                            c, j = divmod(cj, RJ)
                            for r in HP:
                                last = mmul(ps[r, 0, cj * CH:(cj + 1) * CH], mm[r, lv % 2, cj, :], ww[r, c, j, :], start=True, stop=True)
                        last.then_inc(T["inv_q"], 1)
                    elif stage[0] == "double":
                        if lv == 1:
                            pe.wait_ge(*at_sc("tm_ev", 3))
                        pe.wait_ge(*at_sc("inv_qc", lv))
                        for cj in range(2 * RJ):
                            c, j = divmod(cj, RJ)
                            for r in HP:
                                last = mmul(ps[r, 1, cj * CH:(cj + 1) * CH], qq[r, c, j, :], zz[r, c, j, :], start=True, stop=True)
                                if lv < LEVELS - 1:
                                    last = mmul(ps[r, 2, cj * CH:(cj + 1) * CH], zz[r, c, j, :], qq[r, c, j, :], start=True, stop=True)
                        last.then_inc(T["inv_d"], 1)
                        if lv == 1:
                            mmul(ps[:, 3, :], blk, t1, start=True, stop=True).then_inc(T["kk1"], 1)
                    elif stage[0] == "rhs":
                        c = stage[1]
                        pe.wait_ge(*at_sc("inv_z", LEVELS))
                        if sc or c:
                            pe.wait_ge(T["s_ok"], 2 * sc + c)
                        for j in range(RJ):
                            for r in HP:
                                o = ps[r, 0, j * CH:(j + 1) * CH]
                                mmul(o, ar[r, j, c, 0, :], state[r, j, :], start=True, stop=False)
                                last = mmul(o, gk[r, c, j, 0, :], vtm[r, c, j, :], start=False, stop=True)
                        last.then_inc(T["rh_mm"], 1)
                    elif stage[0] == "solve":
                        c = stage[1]
                        pe.wait_ge(*at_sc("rh_ev", c + 1))
                        for j in range(RJ):
                            for r in HP:
                                last = mmul(ps[r, 1, j * CH:(j + 1) * CH], zz[r, c, j, :], rh[r, j, :], start=True, stop=True)
                        last.then_inc(T["u_mm"], 1)
                    elif stage[0] == "advance":
                        c = stage[1]
                        pe.wait_ge(*at_sc("u_ev", c + 1))
                        for j in range(RJ):
                            for r in HP:
                                o = ps[r, 2, j * SC + c * CH:j * SC + (c + 1) * CH]
                                mmul(o, state[r, j, :], ar[r, j, c, 1, :], start=True, stop=False)
                                mmul(o, uu[r, j, :], gb[r, c, j, 1, :], start=False, stop=False)
                                mmul(o, vtm[r, c, j, :], gk[r, c, j, 1, :], start=False, stop=True)
                                o = ps[r, 3, j * CH:(j + 1) * CH]
                                mmul(o, btm[r, c, j, :], uu[r, j, :], start=True, stop=False)
                                last = mmul(o, ktm[r, c, j, :], vtm[r, c, j, :], start=False, stop=True)
                        last.then_inc(T["ds_mm"], 1)
                    elif stage == "mean":
                        pe.wait_ge(*at_sc("y_ev", 1))
                        mmul(ps[:, 0, :], onesblk[:], kk, start=True, stop=True).then_inc(T["mean_mm"], 1)
                    elif stage == "var":
                        pe.wait_ge(*at_sc("yc", 1))
                        mmul(ps[:, 1, :], onesblk[:], t0, start=True, stop=True).then_inc(T["var_mm"], 1)

                def att(n, step):
                    t, i, g = UNITS[n]
                    r = slice(g * HD, (g + 1) * HD)
                    h = g * PER + i
                    if step == "cmp_scores":
                        t = n
                        for g in range(GROUPS):
                            if g:
                                pe.wait_ge(S["at_mm"], 3 * t + 1)
                            r = slice(g * HD, (g + 1) * HD)
                            for i in range(PER):
                                h = g * PER + i
                                last = mmul(ps[:, 6, h * NCP:(h + 1) * NCP], nsa[r, i, t * P:(t + 1) * P], kcp[r, :], start=True, stop=True)
                            last.then_inc(S["at_mm"], 1)
                    elif step == "cmp_turn":
                        pe.wait_ge(S["pc_ok"], n + 1)
                        for h in range(HEADS):
                            last = nc.tensor.transpose(ps[0:NCP, 6 - 2 * (h // 4), (h % 4) * P:(h % 4 + 1) * P], pc[:, h, :], ident)
                        last.then_inc(S["at_mm"], 1)
                    elif step == "scores":
                        if n % HEADS == 0:
                            pe.wait_ge(S["pcp_ok"], t + 1)
                        if n:
                            pe.wait_ge(S["pt_ev"], n)
                        for br in range(2):
                            last = mmul(ps[:, 4 + br, 0:(t + 1) * P], nsa[r, i, t * P:(t + 1) * P],
                                        nsa[r, 6 + 2 * br, 0:(t + 1) * P], start=True, stop=True)
                        last.then_inc(S["sc_mm"], 1)
                    elif step == "turn":
                        pe.wait_ge(S["sc_v"], n + 1)
                        for br in range(2):
                            for k in range(t + 1):
                                last = nc.tensor.transpose(ps[:, 4 + br, k * P:(k + 1) * P], pp[:, br, k * P:(k + 1) * P], ident)
                        last.then_inc(S["pt_mm"], 1)
                    elif step == "values":
                        pe.wait_ge(S["pt_ev"], n + 1)
                        if n % HEADS == 0 and t:
                            pe.wait_ge(S["o_ev"], t)
                        o = ps[r, 7, i * P:(i + 1) * P]
                        mmul(o, vcp[0:NCP, r], pcp[0:NCP, h, :], start=True, stop=False)
                        for br in range(2):
                            for k in range(t + 1):
                                last = mmul(o, vt[:, br, k, r], ppt[:, br, k * P:(k + 1) * P], start=False, stop=(br == 1 and k == t))
                        last.then_inc(S["pv"], 1)

                for side, n, step in PAIRED:
                    (rwkv if side == "rwkv" else att)(n, step)

                unit_dmas = [1] + [2 * PAGES] * CMP_U + [4 * PAGES] * 4

                def unit(u):
                    pe.wait_ge(c_ready[u % 2], 16 * sum(unit_dmas[u % 2:u + 1:2]))
                    return cache[:, u % 2, :]

                sink = dict(start=False, skip_group_check=True)
                pe.wait_ge(S["qpad_ok"], 1)
                slot = unit(0)
                for b in range(DEC):
                    mmul(ps[0:ROWS, 0, 1:WIN], qpad[:, b, :], slot[:, b * WIN + 1:(b + 1) * WIN], start=(b == 0), stop=(b == DEC - 1))
                for b in range(DEC):
                    mmul(ps[0:ROWS, 1, 0:1], qpad[:, b, :], nsa[:, 8, SEQ + b:SEQ + b + 1], start=(b == 0), stop=(b == DEC - 1))
                for n in range(2):
                    last = nc.tensor.transpose(ps[0:DEC, 2, n * P:(n + 1) * P], nsa[:, 7 + 2 * n, SEQ:TOK], ident)
                last.then_inc(S["ss_mm"], 1)
                pe.wait_ge(S["ss_v"], 2)
                for k in range(4):
                    nc.tensor.transpose(ps[:, 3, k * ROWS:(k + 1) * ROWS], swin[0:ROWS, k * P:(k + 1) * P], ident[0:ROWS, 0:ROWS])
                mmul(ps[0:DEC, 4, 0:ROWS], K("selb", ROWS), diag[0:ROWS, 1, :], start=True, stop=True).then_inc(S["ss_mm"], 1)
                pe.wait_ge(S["ss_v"], 3)
                mmul(ps[:, 7, 0:ROWS], vnew[0:DEC, 1, :], pnew[0:DEC, 1, :], start=True, stop=False, skip_group_check=True)
                pe.wait_ge(S["vwin_ready"], 16)
                for b in range(DEC):
                    for k in range(4):
                        v0 = DEC * WIN + b * WIN + k * P
                        last = mmul(ps[:, 7, b * HEADS:(b + 1) * HEADS], slot[:, v0:v0 + P], ptw[:, k, b * HEADS:(b + 1) * HEADS], stop=False, **sink)
                last.then_inc(S["c_free"], 1)
                pe.wait_ge(S["w1_ready"], 16 * 17)
                for u in range(1, CMP_U + 2):
                    if u <= CMP_U:
                        slot = unit(u).rearrange("p (n c g t) -> p n c g t", c=2, g=GROUPS, t=PAGE // 2)
                        for c in range(2):
                            for g in range(GROUPS):
                                for k in range(STRIDE // 2):
                                    last = mmul(cmp_half(u, c, g), w1s[:, c, k, :], slot[:, :, c, g, k::STRIDE // 2],
                                                start=(k == 0), stop=(k == STRIDE // 2 - 1))
                        last.then_inc(S["cmp_h"], 1)
                    if u > 1:
                        pe.wait_ge(S["cmp_act"], u - 1)
                        if u > 2:
                            pe.wait_ge(S["cmp_k"], u - 2)
                        mmul(ps[:, 2, 0:2 * NCS], w2s[:, 0, :], hid[:, 0, :, 0:NCS], start=True, stop=True)
                        for b in range(2):
                            last = mmul(ps[0:NCS, 3, b * P:(b + 1) * P], hid[:, 1, b, 0:NCS], w2s[:, 1, :], start=True, stop=True)
                        last.then_inc(S["cmp_o"], 1)
                pe.wait_ge(S["cmp_k"], CMP_U)
                for b in range(DEC):
                    last = mmul(ps[0:ROWS, 0, 0:NCS], qpad[:, b, :], kcs[:, b, :], start=(b == 0), stop=(b == DEC - 1))
                last.then_inc(S["ss_mm"], 1)
                pe.wait_ge(S["ss_v"], 5)
                mmul(ps[0:NCS, 1, 0:ROWS], pcs[0:ROWS, 0:NCS], K("same", ROWS), start=True, stop=True).then_inc(S["ss_mm"], 1)
                pe.wait_ge(S["ss_v"], 6)
                mmul(ps[0:ROWS, 2, 0:NSEL], impt[0:NCS, :], K("hit", NCS), start=True, stop=True)
                nc.tensor.transpose(ps[0:NCS, 3, 0:ROWS], pcs[0:ROWS, 0:NCS], ident[0:ROWS, 0:ROWS]).then_inc(S["ss_mm"], 1)
                pe.wait_ge(S["ss_v"], 7)
                for b in range(DEC):
                    mmul(ps[:, 7, b * HEADS:(b + 1) * HEADS], vcs[0:NCS, b, :], pct[0:NCS, b * HEADS:(b + 1) * HEADS], stop=False, **sink)
                for half in range(2):
                    slot = unit(CMP_U + 1 + half).rearrange("p (b n) -> p b n", b=4)
                    for b in range(4):
                        for k in range(4):
                            last = mmul(ps[0:ROWS, k, :], qpad[:, 4 * half + b, :], slot[:, b, k * 512:(k + 1) * 512],
                                        start=(half == 0 and b == 0), stop=(half == 1 and b == 3))
                    last.then_inc(S["c_free"], 1)
                for b in range(DEC):
                    last = mmul(ps[0:ROWS, 4, 0:1], qpad[:, b, :], nsa[:, 6, SEQ + b:SEQ + b + 1], start=(b == 0), stop=(b == DEC - 1))
                last.then_inc(S["ss_mm"], 1)
                pe.wait_ge(S["ss_v"], 9)
                flat = ssel.rearrange("p a b -> p (a b)")
                for k in range(PAGES):
                    nc.tensor.transpose(ps[:, k // 8, (k % 8) * ROWS:(k % 8 + 1) * ROWS], flat[0:ROWS, k * P:(k + 1) * P], ident[0:ROWS, 0:ROWS])
                mmul(ps[0:DEC, 2, 0:ROWS], K("selb", ROWS), diag[0:ROWS, 0, :], start=True, stop=True).then_inc(S["ss_mm"], 1)
                pe.wait_ge(S["ss_v"], 10)
                mmul(ps[:, 7, 0:ROWS], vnew[0:DEC, 0, :], pnew[0:DEC, 0, :], stop=False, **sink)
                for half in range(2):
                    slot = unit(CMP_U + 3 + half).rearrange("p (b n t) -> p b n t", b=4, t=PAGE)
                    for b in range(4):
                        s = 4 * half + b
                        for k in range(PAGES):
                            last = mmul(ps[0:HEADS, 5 + half, b * P:(b + 1) * P], pt_s[:, k, s * HEADS:(s + 1) * HEADS], slot[:, b, k, :],
                                        start=(k == 0), stop=(k == PAGES - 1))
                last.then_inc(S["ss_mm"], 1)
                pe.wait_ge(S["ss_v"], 11)
                for s in range(DEC):
                    last = mmul(ps[:, 7, s * HEADS:(s + 1) * HEADS], vo[0:HEADS, s * P:(s + 1) * P], ident[0:HEADS, 0:HEADS],
                                stop=(s == DEC - 1), **sink)
                last.then_inc(S["ss_mm"], 1)
                pe.wait_ge(S["mixed"], 1)

                for m in range(KB):
                    dense_tile([(C_OUT + m, 0, KB)], hm_hi, hm_lo, KB if m == 0 else None)
                    if m >= 2:
                        norm_part(sq2, m - 2)
                norm_part(sq2, KB - 2)
                norm_part(sq2, KB - 1)
                norm(sq2)
                for m in range(2 * FT):
                    dense_tile([(C_UP + m, 0, KB)], hm_hi, hm_lo, 2 * KB if m == 0 else None)
                for m in range(KB):
                    dense_tile([(C_DOWN + 3 * m + i, a, b) for i, (a, b) in enumerate(DCH)], hf_hi, hf_lo, 3 * KB if m == 0 else None)
                    if m >= 2:
                        norm_part(sq3, m - 2)
                norm_part(sq3, KB - 2)
                norm_part(sq3, KB - 1)
                pe.wait_ge(S["norm_mm"], 4)
                meet(pe, "pe", S["arrive"])

        @block.scalar
        def _(act):
            o = Order(act, S["a_own"])
            A = nc.scalar.activation
            act.wait_ge(const_ok, 48)
            with act.Fori(0, DEPTH) as l:
                o.n = 0
                n_dense = [0]

                def norm_root(n):
                    act.wait_ge(S["norm_v"], n)
                    o.do(A(rstd[:], rstd[:], ACT.Sqrt))
                    o.tell(S["norm_a"])

                def evac(dst):
                    n = n_dense[0]
                    act.wait_ge(S["w_used"], tile_done(n))
                    A(dst, ps[:, 2 * (n % 3), 0:HALF], ACT.Copy).then_inc(S["evac_a"], 1)
                    n_dense[0] += 1

                def split_w(*chunks):
                    for n in chunks:
                        if n != C_GATE and n < N_CHUNK:
                            act.wait_ge(w_ready[n % RING], 16 * (n // RING + 1))
                            if n >= RING_HI:
                                act.wait_ge(S["w_used"], n - RING_HI + 1)
                            A(ring_hi[:, n % RING_HI, :], ring[:, n % RING, :], ACT.Copy).then_inc(S["w_hi"], 1)

                def split_s(dst, src, k):
                    A(dst[:, k, :], src[:, k, :], ACT.Copy).then_inc(S["s_hi"], 1)

                def squares(dst, src, ready=None):
                    for k in range(KB):
                        if ready is not None:
                            act.wait_ge(S["norm_h"], ready + k + 1)
                        A(dst[:, k, :], src[:, k, :], ACT.Square).then_inc(S["norm_sq"], 1)

                def tile_squares(dst, src, k, before):
                    act.wait_ge(S["evac_a"], before + k + 1)
                    act.wait_ge(S["evac_v"], before + k + 1)
                    A(dst[:, k, :], src[:, k, :], ACT.Square).then_inc(S["norm_sq"], 1)

                squares(sq, x)
                split_w(0, 1)
                norm_root(1)
                for k in range(KB):
                    act.wait_ge(S["norm_h"], k + 1)
                    split_s(hm_hi, hm, k)
                for m in range(NT + RP):
                    if m + 2 < C_GATE:
                        split_w(m + 2)
                    evac(nsa[:, m, 0:HALF] if m < NT else pr[:, m - NT, 1:1 + HALF])
                for t in range(NQ + 1):
                    n = P if t < NQ else DEC
                    act.wait_ge(S["gate_mm"], t + 1)
                    o.do(A(gates[0:n, t, :], ps[0:n, 6, 0:24], ACT.Sigmoid))
                    o.tell(S["gate_ev"])

                act.wait_ge(S["evac_v"], NT + RP)
                act.wait_ge(S["evac_a"], NT + RP)
                act.wait_ge(S["w1_ready"], 16 * 12)
                for src, dst in stage_views(1):
                    o.go(A(dst, src, ACT.Copy))
                o.tell(S["staged_a"])
                act.wait_ge(S["vt_mm"], 1)
                for br in range(2):
                    o.go(A(vt[:, br, :, :].rearrange("p t n -> p (t n)"), ps[:, 6 + br, :], ACT.Copy))
                o.tell(S["vt_ev"])
                act.wait_ge(S["cmpp_mm"], 1)
                o.go(A(rows_p[0:NCP + 1, :, :], ps[0:NCP + 1, 3, 0:2 * P].rearrange("p (c n) -> p c n", c=2), ACT.Copy))
                o.tell(S["gelu_p"])
                act.wait_ge(S["cmpp_mm"], 2)
                o.do(A(cb[:], ps[:, 2, NCP:2 * NCP + 2:NCP + 1], ACT.Copy))
                for c in range(2):
                    o.go(A(hip[:, c, :], ps[:, 2, c * (NCP + 1):c * (NCP + 1) + NCP], ACT.Gelu_apprx_tanh, bias=cb[:, c:c + 1]))
                o.tell(S["gelu_p"])
                act.wait_ge(S["cmpp_mm"], 3)
                o.go(A(kcp, ps[:, 4, 0:NCP], ACT.Copy))
                o.go(A(vcp[0:NCP, :], ps[0:NCP, 5, 0:P], ACT.Copy))
                o.tell(S["kcp_ok"])

                act.wait_ge(S["params"], 48)
                act.wait_ge(S["rs_x"], 1)
                o.go(A(tanw[0:HD, 0:DEC], xs[0:HD, 3 * RJ, 0:DEC], ACT.Tanh))
                o.go(A(siggl[:, 0:DEC], xs[:, 3 * RJ + 1, 0:DEC], ACT.Sigmoid))
                o.tell(S["rs_act"])
                act.wait_ge(S["rs_lora"], 1)
                for j in range(RJ):
                    o.go(A(sw[:, j, 0:DEC], ps[:, 0, j * DEC:(j + 1) * DEC], ACT.Sigmoid, bias=C("w0", j)))
                    o.go(A(aa[:, j, 0:DEC], ps[:, 1, j * DEC:(j + 1) * DEC], ACT.Sigmoid, bias=C("a0", j)))
                    o.go(A(gg[:, j, 0:DEC], ps[:, 2, j * DEC:(j + 1) * DEC], ACT.Copy))
                act.wait_ge(S["rs_mm"], 1)
                o.go(A(t1[:, :, 0:DEC], b4(3, DEC), ACT.Sqrt))
                o.settle()
                o.go(A(pin[:, :, 0:DEC], sw[:, :, 0:DEC], ACT.Exp, scale=-math.exp(-0.5)))
                o.tell(S["rs_act"])
                act.wait_ge(S["rs_var"], 1)
                o.go(A(t1[:, :, 0:DEC], t1[:, :, 0:DEC], ACT.Sqrt))
                o.tell(S["rs_act"])
                act.wait_ge(S["rs_out"], 1)

                wide_copy = lambda dst, b, n=2 * RJ * CH: o.go(A(dst, ps[:, b, 0:n], ACT.Copy))

                def rwkv(sc, stage):
                    at_sc = lambda name, n: (T[name], PER_SC[name] * sc + n)
                    if stage == "squares":
                        act.wait_ge(*at_sc("x1", 1))
                        o.go(A(tanw[0:HD, :], xs[0:HD, 3 * RJ, :], ACT.Tanh))
                        o.go(A(siggl, xs[:, 3 * RJ + 1, :], ACT.Sigmoid))
                        o.tell(T["act1"])
                    elif stage == "lora":
                        act.wait_ge(*at_sc("lora1", 1))
                        for j in range(RJ):
                            o.go(A(sw[:, j, :], ps[:, 0, j * SC:(j + 1) * SC], ACT.Sigmoid, bias=C("w0", j)))
                            o.go(A(aa[:, j, :], ps[:, 1, j * SC:(j + 1) * SC], ACT.Sigmoid, bias=C("a0", j)))
                        o.tell(T["sig1"])
                        o.go(A(gg, b4(2), ACT.Copy))
                        act.wait_ge(*at_sc("kk1", 1))
                        o.go(A(t1, b4(3), ACT.Sqrt))
                        o.tell(T["root1"])
                    elif stage == "decay":
                        act.wait_ge(*at_sc("ld_ok", 1))
                        o.go(A(pin, cum, ACT.Exp))
                        o.go(A(pex, pex, ACT.Exp))
                        o.go(A(piv, cum, ACT.Exp, scale=-1.0))
                        o.tell(T["exp1"])
                    elif stage == "turn":
                        for n, (b, dst) in enumerate(((1, btm), (2, ktm), (3, vtm))):
                            act.wait_ge(*at_sc("tm_mm", n + 1))
                            wide_copy(dst.rearrange("p c j t -> p (c j t)"), b)
                            o.tell(T["tm_ev"])
                    elif stage[0] == "invert":
                        act.wait_ge(*at_sc("inv_q", stage[1]))
                        wide_copy(qq.rearrange("p c j t -> p (c j t)"), 0)
                        o.tell(T["inv_qc"])
                    elif stage[0] == "rhs":
                        act.wait_ge(*at_sc("rh_mm", stage[1] + 1))
                        wide_copy(rh.rearrange("p j t -> p (j t)"), 0, RJ * CH)
                        o.tell(T["rh_ev"])
                    elif stage[0] == "solve":
                        act.wait_ge(*at_sc("u_mm", stage[1] + 1))
                        wide_copy(uu.rearrange("p j t -> p (j t)"), 1, RJ * CH)
                        o.tell(T["u_ev"])
                    elif stage == ("advance", 1):
                        act.wait_ge(*at_sc("ds_mm", 2))
                        o.go(A(kk, b4(2), ACT.Copy))
                        o.tell(T["y_ev"])
                    elif stage == "var":
                        act.wait_ge(*at_sc("var_v", 1))
                        o.go(A(t1, t1, ACT.Sqrt))
                        o.tell(T["var_a"])

                def att(n, step):
                    w = (UNITS[n][0] + 1) * P
                    if step == "cmp_scores":
                        act.wait_ge(S["pc_sub"], n + 1)
                        o.go(A(pc, pc, ACT.Exp))
                        o.tell(S["pc_exp"])
                    elif step == "scores":
                        act.wait_ge(S["mx"], n + 1)
                        if n:
                            act.wait_ge(S["pt_mm"], n)
                        for br in range(2):
                            o.go(A(pp[:, br, 0:w], ps[:, 4 + br, 0:w], ACT.Exp, bias=nm[:, br:br + 1], accum_out=sums[:, br:br + 1]))
                        o.tell(S["ex"])
                    elif step == "evac":
                        act.wait_ge(S["pt_mm"], n + 1)
                        if n:
                            act.wait_ge(S["pv"], n)
                        o.go(A(ppt[:, :, 0:w], ps[:, 4:6, 0:w], ACT.Copy))
                        o.tell(S["pt_ev"])

                for side, n, step in PAIRED:
                    (rwkv if side == "rwkv" else att)(n, step)

                def load_half(u):
                    slot_free(act, u)
                    page_loads(act, mybir.EngineType.Activation, l, u, 1)

                act.wait_ge(S["phase_ok"], 1)
                load_half(1)
                act.wait_ge(S["ss_v"], 1)
                o.go(A(swin[0:ROWS, :], swin[0:ROWS, :], ACT.Exp, bias=sm[0:ROWS, 0:1], accum_out=sm[0:ROWS, 1:2]))
                o.tell(S["ss_a"])
                load_half(2)
                for u in range(1, CMP_U + 1):
                    act.wait_ge(S["cmp_h"], u)
                    if u >= 2:
                        act.wait_ge(S["cmp_sum"], u - 1)
                    for g in range(GROUPS):
                        o.go(A(part2[0:HD, g, :, :, 0:NCS], cmp_part(u, g, 1), ACT.Copy))
                    o.tell(S["cmp_b"])
                    act.wait_ge(S["cmp_sum"], u)
                    for c in range(2):
                        o.go(A(hid[:, c, :, 0:NCS], hid[:, c, :, 0:NCS], ACT.Gelu_apprx_tanh, bias=cb[:, c:c + 1]))
                    o.tell(S["cmp_act"])
                    if u < CMP_U:
                        load_half(u + 2)
                act.wait_ge(S["ss_v"], 4)
                o.go(A(pcs[0:ROWS, 0:NCS], ps[0:ROWS, 0, 0:NCS], ACT.Exp, bias=sm[0:ROWS, 4:5], accum_out=sm[0:ROWS, 5:6]))
                o.tell(S["ss_a"])
                load_half(CMP_U + 2)
                load_half(CMP_U + 3)
                act.wait_ge(S["ss_v"], 8)
                flat = ssel.rearrange("p a b -> p (a b)")
                o.go(A(flat[0:ROWS, 0:PAST + 1], flat[0:ROWS, 0:PAST + 1], ACT.Exp, bias=sm[0:ROWS, 8:9], accum_out=sm[0:ROWS, 9:10]))
                o.tell(S["ss_a"])
                load_half(CMP_U + 4)

                split_w(C_OUT, C_OUT + 1)
                act.wait_ge(S["mixed"], 1)
                for k in range(KB):
                    split_s(hm_hi, hm, k)
                for m in range(KB):
                    split_w(C_OUT + m + 2)
                    evac(hf[:, m, 0:HALF])
                    if m:
                        tile_squares(sq2, hf, m - 1, NT + RP)
                tile_squares(sq2, hf, KB - 1, NT + RP)
                norm_root(2)
                squares(sq2, x, KB)
                norm_root(3)
                for k in range(KB):
                    act.wait_ge(S["norm_h"], 2 * KB + k + 1)
                    split_s(hm_hi, hm, k)
                for m in range(2 * FT):
                    split_w(C_UP + m + 2)
                    i, n = m // 2, n_dense[0]
                    n_dense[0] += 1
                    if m % 2:
                        act.sem_inc(S["evac_a"], 1)
                        continue
                    if i >= 2:
                        act.wait_ge(S["ffn_c"], i - 1)
                        act.wait_ge(S["ffn_t"], i - 1)
                    act.wait_ge(S["w_used"], tile_done(n))
                    for h in range(2):
                        o.go(A(gx[:, i % 2, 2 + h * HALF:2 + (h + 1) * HALF], ps[:, 2 * (n % 3) + h, 0:HALF], ACT.Copy))
                    o.tell(S["evac_a"])
                    act.wait_ge(S["ffn_c"], i + 1)
                    o.go(A(cv[:, i % 2, :], cv[:, i % 2, :], ACT.Gelu_apprx_tanh))
                    o.tell(S["ffn_act"])
                act.wait_ge(S["w_used"], C_DOWN)
                for k in range(FT):
                    act.wait_ge(S["ffn_h"], k + 1)
                    split_s(hf_hi, hf, k)
                for m in range(KB):
                    split_w(*(C_DOWN + 3 * m + i for i in (2, 3, 4)))
                    evac(hm[:, m, 0:HALF])
                    if m:
                        tile_squares(sq3, hm, m - 1, NT + RP + KB + 2 * FT)
                tile_squares(sq3, hm, KB - 1, NT + RP + KB + 2 * FT)
                norm_root(4)
                meet(act, "a", S["arrive"])

        @block.gpsimd
        def _(pool):
            o = Order(pool, S["p_own"])
            g = nc.gpsimd
            g.memset(ones[:], 1.0 / D_MODEL).then_inc(p_const, 1)
            pool.wait_ge(p_const, 1)
            pool.sem_inc(ones_ok, 1)
            pool.wait_ge(const_ok, 48)
            with pool.Fori(0, DEPTH) as _l:
                o.n = 0
                o.go(g.memset(w1, 0.0))
                o.go(g.memset(w2, 0.0))
                o.tell(S["w1_zero"])
                for sc in range(SEQ // SC):
                    for lv in range(1, LEVELS):
                        if lv == 1:
                            pool.wait_ge(T["gmask"], 2 * sc + 2)
                        if lv > 2:
                            pool.wait_ge(T["inv_q"], (LEVELS - 1) * sc + lv - 2)
                        lo = CONST["lev"][0] + lv * CH
                        m = cst[:, lo:lo + CH].unsqueeze(1).to_broadcast((P, RJ, CH))
                        for c in range(2):
                            o.go(g.tensor_tensor(mm[:, lv % 2, c * RJ:(c + 1) * RJ, :], gb[:, c, :, 0, :], m, ALU.mult))
                        o.tell(T["mm_ok"])
                    if sc + 1 < SEQ // SC:
                        pool.wait_ge(T["u_mm"], 2 * sc + 2)
                        lo = (sc + 1) * SC
                        o.do(g.tensor_tensor(dif, pr[:, :, lo:lo + SC], pr[:, :, lo + 1:lo + SC + 1], ALU.subtract))
                        o.go(g.tensor_tensor(dif, dif, wide(C("mu"), SC), ALU.mult))
                        o.tell(S["dif_ok"])
                pool.wait_ge(S["phase_ok"], 1)
                o.go(g.memset(w2s, 0.0))
                o.tell(S["w1_zero"])
                for i in range(FT):
                    pool.wait_ge(S["evac_a"], NT + RP + KB + 2 * i + 1)
                    if i == 0:
                        pool.wait_ge(S["loads_s"], 32)
                    o.go(g.tensor_copy(cout[:, i, :], gx[:, i % 2, SEQ:SEQ + 2]))
                    o.go(g.tensor_copy(couts[:, i, 0, :], cprev[:, i, 1, :]))
                    o.go(g.tensor_copy(couts[:, i, 1, :], gx[:, i % 2, 2 + SEQ:2 + TOK]))
                    o.tell(S["ffn_t"])
                meet(pool, "p", S["arrive"])

        @block.vector
        def _(dve):
            o = Order(dve, S["v_own"])
            v = nc.vector
            MUL, ADD, SUB, MAX = ALU.mult, ALU.add, ALU.subtract, ALU.max
            LD = -math.exp(-0.5)
            dve.wait_ge(const_ok, 48)
            o.do(v.tensor_scalar(onesblk[:], blk, 1.0 / HD, None, MUL))
            with dve.Fori(0, DEPTH) as _l:
                dve.sem_clear(S["v_own"])
                o.n = 0
                n_dense = [0]

                def norm_inv(n):
                    dve.wait_ge(S["norm_mm"], n)
                    o.do(v.tensor_scalar(rstd[:], bank2(6), EPS, None, ADD))
                    o.do(v.reciprocal(rstd[:], rstd[:]))
                    o.tell(S["norm_v"])
                    dve.wait_ge(S["norm_a"], n)

                rs = rstd[:].rearrange("p h n -> p (h n)")

                def evac(dst):
                    n = n_dense[0]
                    dve.wait_ge(S["w_used"], tile_done(n))
                    v.tensor_copy(dst, ps[:, 2 * (n % 3) + 1, 0:HALF]).then_inc(S["evac_v"], 1)
                    n_dense[0] += 1

                n_split = [0, 0]

                def split_w(*chunks):
                    for n in chunks:
                        if n != C_GATE and n < N_CHUNK:
                            n_split[0] += 1
                            dve.wait_ge(S["w_hi"], n_split[0])
                            r = ring[:, n % RING, :]
                            v.tensor_tensor(ring_lo[:, n % RING, :], r, ring_hi[:, n % RING_HI, :], SUB).then_inc(S["w_lo"], 1)

                def split_s(dst, src, hi, blocks):
                    for k in range(blocks):
                        n_split[1] += 1
                        dve.wait_ge(S["s_hi"], n_split[1])
                        v.tensor_tensor(dst[:, k, :], src[:, k, :], hi[:, k, :], SUB).then_inc(S["s_lo"], 1)

                dve.wait_ge(S["params"], 48)
                split_w(0, 1)
                norm_inv(1)
                for k in range(KB):
                    v.scalar_tensor_tensor(hm[:, k, :], x[:, k, :], C("mix_pre", k), rs, MUL, MUL).then_inc(S["norm_h"], 1)
                split_s(hm_lo, hm, hm_hi, KB)
                o.go(v.memset(pr[:, :, 0:1], 0.0))
                o.go(v.memset(state[:], 0.0))
                for m in range(NT + RP):
                    if m + 2 < C_GATE:
                        split_w(m + 2)
                    evac(nsa[:, m, HALF:TOK] if m < NT else pr[:, m - NT, 1 + HALF:1 + TOK])

                def mix(q, n, cur, prev, prepared=False, tiles=slice(0, RP)):
                    if not prepared:
                        q.do(v.tensor_tensor(dif[:, :, 0:n], prev, cur, SUB))
                        q.do(v.tensor_tensor(dif[:, :, 0:n], dif[:, :, 0:n], wide(C("mu"), n), MUL))
                    q.do(v.tensor_tensor(xs[:, tiles, 0:n], dif[:, tiles, 0:n], cur[:, tiles, :], ADD))

                def key_squares(q, n):
                    q.do(v.tensor_tensor(kk[:, :, 0:n], xs[:, RJ:2 * RJ, 0:n], wide(C("k_k"), n), MUL))
                    q.do(v.tensor_tensor(t0[:, :, 0:n], kk[:, :, 0:n], kk[:, :, 0:n], MUL))

                def keys(q, n, b_out):
                    q.do(v.tensor_scalar(t1[:, :, 0:n], t1[:, :, 0:n], 1e-12, None, MAX))
                    q.do(v.reciprocal(t1[:, :, 0:n], t1[:, :, 0:n]))
                    q.do(v.tensor_tensor(kk[:, :, 0:n], kk[:, :, 0:n], t1[:, :, 0:n], MUL))
                    q.do(v.scalar_tensor_tensor(t0[:, :, 0:n], aa[:, :, 0:n], -1.0, wide(C("k_a"), n), ADD, MUL))
                    q.do(v.scalar_tensor_tensor(km[:, :, 0:n], t0[:, :, 0:n], 1.0, xs[:, RJ:2 * RJ, 0:n], ADD, MUL))
                    q.go(v.tensor_tensor(b_out, kk[:, :, 0:n], aa[:, :, 0:n], MUL))
                    q.do(v.tensor_tensor(t1[:, :, 0:n], xs[:, 0:RJ, 0:n], km[:, :, 0:n], MUL))
                    q.do(v.tensor_tensor(t1[:, :, 0:n], t1[:, :, 0:n], wide(C("r_k"), n), MUL))

                def finish(q, n, rkv, dst):
                    q.do(v.tensor_tensor(kk[:, :, 0:n], kk[:, :, 0:n], t1[:, :, 0:n], MUL))
                    q.do(v.tensor_tensor(kk[:, :, 0:n], kk[:, :, 0:n], wide(C("lnw"), n), MUL))
                    q.do(v.tensor_tensor(kk[:, :, 0:n], kk[:, :, 0:n], wide(C("lnb"), n), ADD))
                    q.do(v.tensor_tensor(t0[:, :, 0:n], rkv, xs[:, 2 * RJ:3 * RJ, 0:n], MUL))
                    q.do(v.tensor_tensor(kk[:, :, 0:n], kk[:, :, 0:n], t0[:, :, 0:n], ADD))
                    q.do(v.tensor_tensor(dst, kk[:, :, 0:n], gg[:, :, 0:n], MUL))

                dve.wait_ge(S["evac_a"], NT + RP)
                dve.wait_ge(S["evac_v"], NT + RP)
                dve.wait_ge(S["trig_ok"], 16)
                for n, tile in enumerate((4, 0, 1, 2, 3, 6, 8)):
                    scale = HD ** -0.5 if tile < 4 else 1.0
                    o.go(v.scalar_tensor_tensor(tr, nsa[:, tile, :], scale, trig[:, 0, :], MUL, MUL))
                    dve.wait_ge(S["rope_mm"], n + 1)
                    o.do(v.scalar_tensor_tensor(halves(tr2), bank2(2 * (n % 3)), scale, halves(trig[:, 1, :]), MUL, MUL))
                    o.do(v.tensor_tensor(nsa[:, tile, :], tr, tr2, ADD))
                    o.tell(S["rope_ok"])
                    if tile == 4:
                        dve.wait_ge(S["w1_ready"], 16 * 12)
                        for src, dst in stage_views(0):
                            o.go(v.tensor_copy(dst, src))
                        o.tell(S["staged_v"])
                o.tell(S["nsa_ready"])

                dve.wait_ge(S["kcp_ok"], 1)
                dve.wait_ge(S["evac_a"], NT + RP)
                dve.wait_ge(S["evac_v"], NT + RP)
                mix(o, DEC, pr[:, :, 1 + SEQ:1 + TOK], prev_s)
                key_squares(o, DEC)
                o.tell(S["rs_x"])
                dve.wait_ge(S["rs_act"], 2)
                bs = cum[:, :, 0:DEC]
                keys(o, DEC, bs)
                o.do(v.tensor_scalar(pex[:, :, 0:DEC], kk[:, :, 0:DEC], -1.0, None, MUL))
                o.tell(S["rs_prep"])
                rks = dif[:, 0:RJ, 0:DEC]
                over = lambda a: a.unsqueeze(3).to_broadcast((P, RJ, DEC, CH))
                b47 = ps[:, 4:8, :].rearrange("p j (b n) -> p j b n", b=DEC)
                dve.wait_ge(S["rs_mm"], 2)
                dve.wait_ge(S["loads_s"], 16)
                o.go(v.tensor_copy(rks, b4(3, DEC)))
                o.go(v.tensor_tensor(s1, b47, over(bs), MUL))
                o.tell(S["rs_prep"])
                o.do(v.tensor_tensor(ss, ss, over(pin[:, :, 0:DEC]), MUL))
                o.do(v.tensor_tensor(ss, ss, s1, ADD))
                dve.wait_ge(S["rs_mm"], 3)
                o.do(v.tensor_tensor(s1, b47, over(km[:, :, 0:DEC]), MUL))
                o.tell(S["rs_prep"])
                o.do(v.tensor_tensor(ss, ss, s1, ADD))
                o.tell(S["rs_prep"])
                dve.wait_ge(S["rs_mm"], 4)
                o.go(v.tensor_copy(kk[:, :, 0:DEC], b4(0, DEC)))
                o.tell(S["rs_prep"])
                dve.wait_ge(S["rs_mm"], 5)
                o.do(v.tensor_tensor(kk[:, :, 0:DEC], kk[:, :, 0:DEC], b4(1, DEC), SUB))
                o.do(v.tensor_tensor(t0[:, :, 0:DEC], kk[:, :, 0:DEC], kk[:, :, 0:DEC], MUL))
                o.tell(S["rs_prep"])
                dve.wait_ge(S["rs_mm"], 6)
                o.do(v.tensor_scalar(t1[:, :, 0:DEC], b4(1, DEC), LNX_EPS, None, ADD))
                o.do(v.reciprocal(t1[:, :, 0:DEC], t1[:, :, 0:DEC]))
                o.tell(S["rs_var"])
                dve.wait_ge(S["rs_act"], 3)
                finish(o, DEC, rks, hm[:, RJ:2 * RJ, SEQ:TOK])
                o.tell(S["rs_out"])
                dve.wait_ge(S["rs_stored"], 32)
                dve.wait_ge(S["gate_ev"], NQ + 1)

                flat = lambda a: a.rearrange("p j t -> p (j t)")
                in2 = lambda a: a.rearrange("p j (c t) -> p j c t", c=2)
                bb = sw
                gm = K("gmask").unsqueeze(1).to_broadcast((P, RJ, P))
                lo = CONST["lev"][0]
                lev0 = cst[:, lo:lo + CH].unsqueeze(1).to_broadcast((P, RJ, CH))
                eye8 = eye.unsqueeze(1).to_broadcast((P, 2 * RJ, CH))
                z8, w8 = (a.rearrange("p c j t -> p (c j) t") for a in (zz, ww))
                bank8 = lambda b: ps[:, b, :].rearrange("p (a t) -> p a t", t=CH)

                def rwkv(sc, stage):
                    at_sc = lambda name, n: (T[name], PER_SC[name] * sc + n)
                    if stage == "mix":
                        if sc:
                            dve.wait_ge(S["dif_ok"], sc)
                        cur = pr[:, :, sc * SC + 1:(sc + 1) * SC + 1]
                        mix(o, SC, cur, pr[:, :, sc * SC:(sc + 1) * SC], prepared=sc > 0, tiles=slice(3 * RJ, RP))
                        o.tell(T["x1"])
                        low = slice(0, 3 * RJ)
                        o.do(v.tensor_tensor(xs[:, low, :], dif[:, low, :], cur[:, low, :], ADD))
                    elif stage == "squares":
                        key_squares(o, SC)
                        o.tell(T["x1"])
                    elif stage == "decay":
                        dve.wait_ge(*at_sc("sig1", 1))
                        o.do(v.tensor_scalar(sw, sw, LD, None, MUL))
                        o.do(v.tensor_tensor_scan(flat(cum), K("scan"), flat(sw), 0.0, MUL, ADD))
                        o.go(v.tensor_tensor(pex, cum, sw, SUB))
                        o.tell(T["ld_ok"])
                    elif stage == "keys":
                        dve.wait_ge(*at_sc("root1", 1))
                        keys(o, SC, bb)
                        o.tell(T["prep"])
                    elif stage == "scaled":
                        dve.wait_ge(*at_sc("exp1", 1))
                        o.go(v.scalar_tensor_tensor(ar[:, :, :, 0, :], in2(kk), -1.0, in2(pex), MUL, MUL))
                        o.go(v.tensor_tensor(ar[:, :, :, 1, :], in2(xs[:, 0:RJ, :]), in2(pin), MUL))
                        o.go(v.tensor_tensor(bt, bb, piv, MUL))
                        o.go(v.tensor_tensor(kt, km, piv, MUL))
                        o.tell(T["prep"])
                    elif stage == "pairs":
                        for c in range(2):
                            dve.wait_ge(*at_sc("gmm", c + 1))
                            for n, dst in ((0, gb), (1, gk)):
                                o.go(v.tensor_tensor(dst[:, c, :, :, :].rearrange("p j a t -> p j (a t)"), b4(n + 2 * c), gm, MUL))
                            o.tell(T["gmask"])
                    elif stage == "turn":
                        for c in range(2):
                            o.go(v.tensor_tensor(zz[:, c, :, :], gb[:, c, :, 0, :], lev0, MUL))
                        dve.wait_ge(*at_sc("nmm", 1))
                        o.do(v.tensor_tensor(w8, bank8(0), K("lev0t").unsqueeze(1).to_broadcast((P, 2 * RJ, CH)), MUL))
                        o.go(v.tensor_tensor(z8, z8, eye8, ADD))
                        o.go(v.tensor_tensor(w8, w8, eye8, ADD))
                        o.tell(T["inv_z"])
                    elif stage[0] == "double":
                        lv = stage[1]
                        dve.wait_ge(*at_sc("inv_d", lv))
                        if lv == 2:
                            dve.wait_ge(*at_sc("kk1", 2))
                            o.go(v.tensor_copy(rk, b4(3)))
                        o.go(v.tensor_tensor(z8, z8, bank8(1), ADD))
                        if lv < LEVELS - 1:
                            o.go(v.tensor_tensor(w8, w8, bank8(2), ADD))
                        o.tell(T["inv_z"])
                    elif stage[0] == "advance":
                        c = stage[1]
                        dve.wait_ge(*at_sc("ds_mm", c + 1))
                        o.do(v.tensor_tensor(state[:], state[:], b4(3, CH), ADD))
                        e = c * CH + CH - 1
                        o.go(v.tensor_tensor(state[:], state[:], pin[:, :, e:e + 1].to_broadcast((P, RJ, CH)), MUL))
                        o.tell(T["s_ok"])
                    elif stage == "mean":
                        dve.wait_ge(*at_sc("mean_mm", 1))
                        o.do(v.tensor_tensor(kk, kk, b4(0), SUB))
                        o.go(v.tensor_tensor(t0, kk, kk, MUL))
                        o.tell(T["yc"])
                    elif stage == "var":
                        dve.wait_ge(*at_sc("var_mm", 1))
                        o.do(v.tensor_scalar(t1, b4(1), LNX_EPS, None, ADD))
                        o.go(v.reciprocal(t1, t1))
                        o.tell(T["var_v"])
                    elif stage == "out":
                        dve.wait_ge(*at_sc("var_a", 1))
                        finish(o, SC, rk, hm[:, RJ:2 * RJ, sc * SC:(sc + 1) * SC])

                def att(n, step):
                    t, i, g = UNITS[n]
                    h, w = g * PER + i, (t + 1) * P
                    if step == "cmp_scores":
                        dve.wait_ge(S["at_mm"], 3 * n + 2)
                        lo = CONST["cmask"][0] + n * NCP
                        mask = cst[:, lo:lo + NCP].unsqueeze(1).to_broadcast((P, HEADS, NCP))
                        o.do(v.tensor_tensor(pc, ps[:, 6, 0:HEADS * NCP].rearrange("p (h n) -> p h n", h=HEADS), mask, ADD))
                        o.do(v.tensor_reduce(cm[:, 0, :], pc, AX, MAX))
                        o.do(v.tensor_scalar(cm[:, 0, :], cm[:, 0, :], NEG / 10, None, MAX))
                        o.go(v.tensor_tensor(pc, pc, wide(cm[:, 0, :], NCP), SUB))
                        o.tell(S["pc_sub"])
                    elif step == "cmp_turn":
                        dve.wait_ge(S["pc_exp"], n + 1)
                        o.do(v.tensor_reduce(cm[:, 1, :], pc, AX, ADD))
                        o.do(v.tensor_scalar(cm[:, 1, :], cm[:, 1, :], 1e-30, None, MAX))
                        o.do(v.reciprocal(cm[:, 2, :], cm[:, 1, :]))
                        o.do(v.tensor_tensor(cm[:, 2, :], cm[:, 2, :], gates[:, n, 0:24:3], MUL))
                        o.go(v.tensor_tensor(pc, pc, wide(cm[:, 2, :], NCP), MUL))
                        o.tell(S["pc_ok"])
                    elif step == "cmp_done":
                        dve.wait_ge(S["at_mm"], 3 * n + 3)
                        for half in range(2):
                            o.go(v.tensor_copy(pcp[0:NCP, 4 * half:4 * half + 4, :], ps[0:NCP, 6 - 2 * half, :].rearrange("p (h n) -> p h n", h=4)))
                        o.tell(S["pcp_ok"])
                    elif step == "scores":
                        dve.wait_ge(S["sc_mm"], n + 1)
                        d = ps[:, 4:6, t * P:(t + 1) * P]
                        o.do(v.tensor_tensor(d, d, K("causal").unsqueeze(1).to_broadcast((P, 2, P)), ADD))
                        o.go(v.tensor_reduce(nm, ps[:, 4:6, 0:w], AX, MAX, negate=True))
                        o.tell(S["mx"])
                    elif step == "turn":
                        dve.wait_ge(S["ex"], n + 1)
                        o.do(v.tensor_scalar(sums, sums, 1e-30, None, MAX))
                        o.do(v.reciprocal(rr, sums))
                        o.do(v.tensor_tensor(rr, rr, gates[:, t, 3 * h + 1:3 * h + 3], MUL))
                        o.go(v.tensor_tensor(pp[:, :, 0:w], pp[:, :, 0:w], wide(rr, w), MUL))
                        o.tell(S["sc_v"])
                    elif step == "heads_out":
                        dve.wait_ge(S["pv"], HEADS * (n + 1))
                        o.go(v.tensor_copy(hm[:, 0:PER, n * P:(n + 1) * P], b4(7)))
                        o.tell(S["o_ev"])

                for side, n, step in PAIRED:
                    (rwkv if side == "rwkv" else att)(n, step)
                o.tell(S["phase_ok"])

                o.do(v.memset(qpad, 0.0))
                qflat = qpad.rearrange("p b n -> p (b n)")
                for i in range(PER):
                    for g in range(GROUPS):
                        r = slice(g * HD, (g + 1) * HD)
                        h = g * PER + i
                        step = ROWS + HEADS
                        o.go(v.tensor_copy(qflat[r, h:h + step * (DEC - 1) + 1:step], nsa[r, i, SEQ:TOK]))
                o.tell(S["qpad_ok"])
                R = slice(0, ROWS)
                dve.wait_ge(S["gs_ready"], 16)

                def weigh(p, den, col, gate):
                    o.do(v.tensor_scalar(sm[R, den:den + 1], sm[R, den:den + 1], 1e-30, None, MAX))
                    o.do(v.reciprocal(sm[R, col:col + 1], sm[R, den:den + 1]))
                    if gate is not None:
                        o.do(v.tensor_tensor(sm[R, col:col + 1], sm[R, col:col + 1], gate_s[:, gate:gate + 1], MUL))
                    o.do(v.tensor_scalar(p, p, sm[R, col:col + 1], None, MUL))

                dve.wait_ge(S["ss_mm"], 1)
                o.go(v.tensor_copy(swin[R, 1:WIN], ps[R, 0, 1:WIN]))
                o.go(v.tensor_copy(swin[R, 0:1], ps[R, 1, 0:1]))
                o.go(v.tensor_copy(vnew[0:DEC, :, :], ps[0:DEC, 2, 0:2 * P].rearrange("p (a n) -> p a n", a=2)))
                o.settle()
                o.go(v.tensor_reduce(sm[R, 0:1], swin[R, :], AX, MAX, negate=True))
                o.tell(S["ss_v"])
                dve.wait_ge(S["ss_a"], 1)
                weigh(swin[R, :], 1, 2, 2)
                o.do(v.tensor_scalar(diag[R, 1, :], ident[R, 0:ROWS], swin[R, 0:1], None, MUL))
                o.go(v.memset(swin[R, 0:1], 0.0))
                o.tell(S["ss_v"])
                dve.wait_ge(S["ss_mm"], 2)
                o.go(v.tensor_copy(ptw.rearrange("p k n -> p (k n)"), ps[:, 3, 0:4 * ROWS]))
                o.go(v.tensor_copy(pnew[0:DEC, 1, :], ps[0:DEC, 4, 0:ROWS]))
                o.tell(S["ss_v"])
                for u in range(1, CMP_U + 2):
                    if u <= CMP_U:
                        dve.wait_ge(S["cmp_b"], u)
                        if u > 1:
                            dve.wait_ge(S["cmp_o"], u - 1)
                        for g in range(GROUPS):
                            o.go(v.tensor_tensor(hid[g * HD:(g + 1) * HD, :, :, 0:NCS], cmp_part(u, g, 0), part2[0:HD, g, :, :, 0:NCS], ADD))
                        o.tell(S["cmp_sum"])
                    if u == 1:
                        continue
                    dve.wait_ge(S["cmp_o"], u - 1)
                    b = 2 * (u - 2)
                    o.go(v.tensor_copy(kcs[:, b:b + 2, :], ps[:, 2, 0:2 * NCS].rearrange("p (b n) -> p b n", b=2)))
                    o.go(v.tensor_copy(vcs[0:NCS, b:b + 2, :], ps[0:NCS, 3, 0:2 * P].rearrange("p (b n) -> p b n", b=2)))
                    o.tell(S["cmp_k"])
                dve.wait_ge(S["ss_mm"], 3)
                o.go(v.tensor_reduce(sm[R, 4:5], ps[R, 0, 0:NCS], AX, MAX, negate=True))
                o.tell(S["ss_v"])
                dve.wait_ge(S["ss_a"], 2)
                weigh(pcs[R, 0:NCS], 5, 6, None)
                o.tell(S["ss_v"])
                dve.wait_ge(S["ss_mm"], 4)
                o.go(v.tensor_copy(impt[0:NCS, :], ps[0:NCS, 1, 0:ROWS]))
                o.go(v.tensor_scalar(pcs[R, 0:NCS], pcs[R, 0:NCS], gate_s[:, 0:1], None, MUL))
                o.tell(S["ss_v"])
                dve.wait_ge(S["ss_mm"], 5)
                o.go(v.tensor_copy(pct[0:NCS, :], ps[0:NCS, 3, 0:ROWS]))
                o.do(v.tensor_tensor(work[R, :], ps[R, 2, 0:NSEL], K("keep", ROWS), MUL))
                o.tell(S["ss_v"])
                o.do(v.tensor_tensor(work[R, :], work[R, :], K("force", ROWS), ADD))
                for _ in range(2):
                    o.do(v.max(top[R, :], work[R, :]))
                    o.do(v.match_replace(work[R, :], top[R, :], work[R, :], 2 * NEG))
                o.do(v.tensor_scalar(imp[R, :], work[R, :], 1.5 * NEG, NEG, ALU.is_ge, MUL))
                dve.wait_ge(S["ss_mm"], 6)
                for k in range(4):
                    bias = imp[R, 8 * k:8 * k + 8].unsqueeze(2).to_broadcast((ROWS, 8, SELB))
                    o.go(v.tensor_tensor(ssel[R, 8 * k:8 * k + 8, :], ps[R, k, :].rearrange("p (a b) -> p a b", b=SELB), bias, ADD))
                fs = ssel.rearrange("p a b -> p (a b)")
                o.do(v.tensor_tensor(fs[R, PAST:PAST + 1], ps[R, 4, 0:1], imp[R, NSEL - 1:NSEL], ADD))
                o.do(v.tensor_reduce(sm[R, 8:9], fs[R, 0:PAST + 1], AX, MAX, negate=True))
                o.tell(S["ss_v"])
                dve.wait_ge(S["ss_a"], 3)
                weigh(fs[R, 0:PAST + 1], 9, 10, 1)
                o.do(v.tensor_scalar(diag[R, 0, :], ident[R, 0:ROWS], fs[R, PAST:PAST + 1], None, MUL))
                o.tell(S["ss_v"])
                dve.wait_ge(S["ss_mm"], 7)
                o.go(v.tensor_copy(pt_s.rearrange("p (a k) n -> p a (k n)", a=2), ps[:, 0:2, :]))
                o.go(v.tensor_copy(pnew[0:DEC, 0, :], ps[0:DEC, 2, 0:ROWS]))
                o.tell(S["ss_v"])
                dve.wait_ge(S["ss_mm"], 8)
                o.go(v.tensor_copy(vo[0:HEADS, :].rearrange("p (a n) -> p a n", a=2), ps[0:HEADS, 5:7, :]))
                o.tell(S["ss_v"])
                dve.wait_ge(S["ss_mm"], 9)
                for g in range(GROUPS):
                    r = slice(g * HD, (g + 1) * HD)
                    src = ps[r, 7, 0:ROWS].rearrange("p (b h) -> p h b", h=HEADS)[:, g * PER:(g + 1) * PER, :]
                    o.go(v.tensor_copy(hm[r, 0:PER, SEQ:TOK], src))
                o.tell(S["mixed"])

                split_w(C_OUT, C_OUT + 1)
                split_s(hm_lo, hm, hm_hi, KB)
                for m in range(KB):
                    split_w(C_OUT + m + 2)
                    evac(hf[:, m, HALF:TOK])

                def add_normed(src, g):
                    n = o.n
                    for k in range(KB + 1):
                        if k < KB:
                            o.go(v.scalar_tensor_tensor(src[:, k, :], src[:, k, :], C(g, k), rs, MUL, MUL))
                        if k:
                            dve.wait_ge(S["v_own"], n + k)
                            v.tensor_tensor(x[:, k - 1, :], x[:, k - 1, :], src[:, k - 1, :], ADD).then_inc(S["norm_h"], 1)

                norm_inv(2)
                add_normed(hf, "mix_post")
                norm_inv(3)
                for k in range(KB):
                    v.scalar_tensor_tensor(hm[:, k, :], x[:, k, :], C("ffn_pre", k), rs, MUL, MUL).then_inc(S["norm_h"], 1)
                split_s(hm_lo, hm, hm_hi, KB)
                o.do(v.memset(gx[:, :, 0:2], 0.0))
                dve.wait_ge(S["loads_s"], 32)

                def conv(i):
                    s = i % 2
                    n = NT + RP + KB + 2 * i + 1
                    dve.wait_ge(S["evac_a"], n)
                    if i >= 2:
                        dve.wait_ge(S["ffn_h"], i - 1)
                    p_, s_ = cv[:, s, 0:SEQ], cv[:, s, SEQ:TOK]
                    o.go(v.tensor_scalar(p_, gx[:, s, 0:SEQ], C("cw0", i), C("cb", i), MUL, ADD))
                    o.do(v.tensor_scalar(s_, cprev[:, i, 0, :], C("cw0", i), C("cb", i), MUL, ADD))
                    o.go(v.scalar_tensor_tensor(p_, gx[:, s, 1:1 + SEQ], C("cw1", i), p_, MUL, ADD))
                    o.do(v.scalar_tensor_tensor(s_, cprev[:, i, 1, :], C("cw1", i), s_, MUL, ADD))
                    o.go(v.scalar_tensor_tensor(cv[:, s, :], gx[:, s, 2:2 + TOK], C("cw2", i), cv[:, s, :], MUL, ADD))
                    o.tell(S["ffn_c"])

                for i in range(FT):
                    split_w(C_UP + 2 * i + 2)
                    dve.sem_inc(S["evac_v"], 1)
                    conv(i)
                    n_dense[0] += 1
                    n = n_dense[0]
                    split_w(C_UP + 2 * i + 3)
                    dve.wait_ge(S["w_used"], tile_done(n))
                    dve.wait_ge(S["ffn_act"], i + 1)
                    o.do(v.tensor_tensor(halves(hf[:, i, :]), halves(cv[:, i % 2, :]), bank2(2 * (n % 3)), MUL))
                    dve.sem_inc(S["evac_v"], 1)
                    dve.sem_inc(S["ffn_h"], 1)
                    n_dense[0] += 1
                split_s(hf_lo, hf, hf_hi, FT)
                for m in range(KB):
                    split_w(*(C_DOWN + 3 * m + i for i in (2, 3, 4)))
                    evac(hm[:, m, HALF:TOK])
                norm_inv(4)
                add_normed(hm, "ffn_post")
                dve.wait_ge(S["norm_h"], 4 * KB)
                meet(dve, "v", S["arrive"])


HEAD_ORDER = [g * PER + i for i in range(PER) for g in range(GROUPS)]


def tiles(a):
    return np.swapaxes(a.reshape(a.shape[:-1] + (-1, P)), -1, -2)


def weight_chunks(w_in, w_out, w_up, w_down):
    q_cols = np.concatenate([np.arange(h * HD, (h + 1) * HD) for h in HEAD_ORDER])
    nsa_w = HEADS * HD
    kv_w = 6 * P
    out = np.zeros((DEPTH, N_CHUNK, P, KB, P), w_in.dtype)

    def put(at, w):
        k, m = w.shape[1] // P, w.shape[2] // P
        t = w.reshape(DEPTH, k, P, m, P).transpose(0, 3, 2, 1, 4)
        for i in range(m):
            for c in range(-(-k // KB)):
                part = t[:, i, :, c * KB:(c + 1) * KB]
                out[:, at, :, 0:part.shape[2]] = part
                at += 1
        return at

    wq = w_in[:, :, q_cols]
    rest = w_in[:, :, nsa_w:nsa_w + kv_w]
    gate = w_in[:, :, nsa_w + kv_w:nsa_w + kv_w + 24]
    n = put(0, np.concatenate([wq, rest, w_in[:, :, nsa_w + kv_w + 24:]], 2))
    flat = out.reshape(DEPTH, N_CHUNK, P, KB * P)
    flat[:, n, :, 0:KB * 24] = gate.reshape(DEPTH, KB, P, 24).transpose(0, 2, 1, 3).reshape(DEPTH, P, KB * 24)
    n = put(n + 1, np.concatenate([w_out[:, q_cols], w_out[:, nsa_w:]], 1))
    up = np.stack([w_up[:, :, 0:FF].reshape(DEPTH, D_MODEL, FT, P), w_up[:, :, FF:].reshape(DEPTH, D_MODEL, FT, P)], 3)
    n = put(n, up.reshape(DEPTH, D_MODEL, 2 * FF))
    n = put(n, w_down)
    assert n == N_CHUNK
    return flat


OUTS = {
    "y": (KB, P, TOK), "kv": (DEPTH, P, 6 * TOK), "win_old": (DEPTH, DEC, (WIN - 1) * 2 * P),
    "wkv_p": (DEPTH, P, RJ * CH), "wkv_s": (DEPTH, P, RJ * DEC * CH), "shift": (DEPTH, P, RP * (1 + DEC)),
    "conv_p": (DEPTH, P, FT * 2), "conv_s": (DEPTH, P, FT * 2 * DEC),
}


def kernel(x_prompt, x_sample, cache_kv, page_table, state_win, state_wkv, state_shift, state_conv,
           norm_mix_pre, norm_mix_post, norm_ffn_pre, norm_ffn_post, w_in, w_out,
           cmp_pe, cmp_w1, cmp_w2, rwkv_mu, rwkv_w0, rwkv_w_up, rwkv_a0, rwkv_a_up, rwkv_g_up,
           rwkv_k_k, rwkv_k_a, rwkv_r_k, rwkv_lnx_w, rwkv_lnx_b,
           ffn_w_up, ffn_conv_w, ffn_conv_b, ffn_w_down):
    import concourse.bacc as bacc
    from concourse.bass_utils import run_bass_kernel_spmd

    arr = lambda a: np.asarray(a)
    xp, xs = arr(x_prompt)[0], arr(x_sample)[:, 0]
    cache = arr(cache_kv).reshape(DEPTH * N_POOL, PAGE, 4, P)
    win = arr(state_win)
    fm = cache.transpose(0, 3, 2, 1)
    conv_w = arr(ffn_conv_w)
    lora = np.concatenate([np.concatenate([arr(rwkv_w_up), arr(rwkv_a_up)], 1), arr(rwkv_g_up)], 2)
    wkv = arr(state_wkv).reshape(DEPTH, DEC, RJ, 2, HD, HD)
    cols = {"mix_pre": norm_mix_pre, "mix_post": norm_mix_post, "ffn_pre": norm_ffn_pre, "ffn_post": norm_ffn_post,
            "mu": rwkv_mu, "w0": rwkv_w0, "a0": rwkv_a0, "k_k": rwkv_k_k, "k_a": rwkv_k_a,
            "r_k": arr(rwkv_r_k).reshape(DEPTH, RW), "lnw": rwkv_lnx_w, "lnb": rwkv_lnx_b,
            "cw0": conv_w[:, 0], "cw1": conv_w[:, 1], "cw2": conv_w[:, 2], "cb": ffn_conv_b}
    inputs = {
        "consts": constants()[0],
        "trig": constants()[1],
        "pages": arr(page_table).reshape(1, -1),
        "x": np.concatenate([xp, xs], 0).T.reshape(KB, P, TOK),
        "cols": np.concatenate([tiles(arr(cols[n])) for n in COLS], 2),
        "shift": arr(state_shift).reshape(DEPTH, DEC, RP, P).transpose(0, 3, 2, 1).reshape(DEPTH, P, -1),
        "lora": lora,
        "w": weight_chunks(arr(w_in), arr(w_out), arr(ffn_w_up), arr(ffn_w_down)),
        "wkv": wkv.transpose(0, 3, 5, 2, 1, 4).reshape(DEPTH, P, -1),
        "w1": arr(cmp_w1).transpose(0, 1, 3, 2, 4).reshape(DEPTH, 2, HD, -1),
        "w1_pairs": arr(cmp_w1).reshape(DEPTH, 2, 2, STRIDE // 2, 2, HD, HD).transpose(0, 4, 5, 1, 3, 2, 6).reshape(DEPTH, P, -1),
        "w2": arr(cmp_w2),
        "pe": arr(cmp_pe).transpose(0, 1, 3, 2),
        "win": win[:, :, 1:].reshape(DEPTH, DEC, -1),
        "kwin": win[:, :, :, 0].reshape(DEPTH, DEC, WIN, P).transpose(0, 1, 3, 2),
        "vwin": win[:, :, :, 1].reshape(DEPTH, DEC, 4, P, P).transpose(0, 1, 3, 2, 4).reshape(DEPTH, DEC, P, WIN),
        "kv_cmp": cache[:, :, 0:2].reshape(DEPTH * N_POOL, PAGE // 2, 2, 2, GROUPS, HD).transpose(0, 2, 5, 3, 4, 1).reshape(DEPTH * N_POOL, P, 2 * PAGE),
        "k_sel": fm[:, :, 2],
        "v_sel": cache[:, :, 3],
        "conv": arr(state_conv).reshape(DEPTH, DEC, 2, FT, P).transpose(0, 4, 3, 2, 1).reshape(DEPTH, P, -1),
    }
    nc = bacc.Bacc("TRN2", target_bir_lowering=False, num_devices=1)
    arrays, I, O = {}, {}, {}
    for name, a in inputs.items():
        a = np.ascontiguousarray(a)
        arrays["in_" + name] = a
        I[name] = nc.dram_tensor("in_" + name, a.shape, mybir.dt.from_np(a.dtype), kind="ExternalInput").ap()
    for name, shape in OUTS.items():
        O[name] = nc.dram_tensor("out_" + name, shape, F32, kind="ExternalOutput").ap()
    build(nc, I, O)
    res = run_bass_kernel_spmd(nc, [arrays], core_ids=[0]).results[0]
    r = {n: np.asarray(res["out_" + n]) for n in OUTS}

    y = r["y"].reshape(D_MODEL, TOK).T
    kv = r["kv"].reshape(DEPTH, GROUPS, HD, 6, TOK).transpose(0, 4, 3, 1, 2)
    win_new = np.concatenate([r["win_old"].reshape(DEPTH, DEC, WIN - 1, 2, GROUPS, HD), kv[:, SEQ:, None, 4:6]], 2)
    back = lambda a: a.reshape(DEPTH, 2, HD, RJ, -1, HD).transpose(0, 4, 3, 1, 5, 2).reshape(DEPTH, -1, HEADS, HD, HD)
    shift = r["shift"].reshape(DEPTH, P, RP, 1 + DEC).transpose(0, 3, 2, 1).reshape(DEPTH, 1 + DEC, RP * P)
    conv_p = r["conv_p"].reshape(DEPTH, P, FT, 2).transpose(0, 3, 2, 1).reshape(DEPTH, 1, 2, FF)
    conv_s = r["conv_s"].reshape(DEPTH, P, FT, 2, DEC).transpose(0, 4, 3, 2, 1).reshape(DEPTH, DEC, 2, FF)
    outs = (y[None, 0:SEQ], y[SEQ:, None], kv[:, None, 0:SEQ, 0:4], kv[:, SEQ:, None, 0:4],
            kv[:, None, 0:SEQ, 4:6], win_new, back(r["wkv_p"]), back(r["wkv_s"]),
            shift[:, 0:1], shift[:, 1:], conv_p, conv_s)
    return tuple(np.ascontiguousarray(a) for a in outs)
```
